# Optimizing a Trainium2 kernel written in Bass

```python
import math
import jax
import jax.numpy as jnp
from jax import lax
import numpy as np

D_MODEL = 1024
BATCH = 1
SEQ = 256
DEPTH = 1

HEAD_DIM = 64
BRANCH_WIDTH = D_MODEL // 2
N_BRANCHES = 4
N_HEADS = BRANCH_WIDTH // HEAD_DIM
SSM_HEADS = N_HEADS
SSM_GROUPS = 2
SSM_STATE = 128
SSM_CONV = 4
SSM_CHUNK = 256
SSM_BC = SSM_GROUPS * SSM_STATE
SSM_CONV_DIM = BRANCH_WIDTH + 2 * SSM_BC
MOBA_BLOCK = 256
MOBA_TOPK = 3
MOBA_Q_CHUNK = 64
FOX_Q_BLOCK = 128
SWA_WINDOW = 128
SWA_KV_HEADS = 2
REL_BUCKETS = 32
REL_MAX_EXACT = REL_BUCKETS // 2
REL_MAX_DISTANCE = 1024
N_BIAS_HEADS = 2 * N_HEADS
D_FF = 256 * math.ceil(8 * D_MODEL / 3 / 256)
NORM_EPS = 1e-6
SPLIT_SIZES = (
    BRANCH_WIDTH,
    SSM_CONV_DIM,
    SSM_HEADS,
    3 * BRANCH_WIDTH,
    3 * BRANCH_WIDTH,
    N_HEADS,
    BRANCH_WIDTH,
    2 * SWA_KV_HEADS * HEAD_DIM,
    N_BRANCHES * D_MODEL,
)
D_IN_PROJ = sum(SPLIT_SIZES)
SPLIT_POINTS = [int(v) for v in np.cumsum(SPLIT_SIZES)[:-1]]


def rmsnorm(x, w):
    xf = x.astype(jnp.float32)
    y = xf * lax.rsqrt(jnp.mean(xf * xf, axis=-1, keepdims=True) + NORM_EPS)
    return (y * w.astype(jnp.float32)).astype(x.dtype)

def rel_bucket(dist):
    dist = jnp.maximum(dist, 0)
    d = jnp.maximum(dist, 1).astype(jnp.float32)
    large = REL_MAX_EXACT + (jnp.log(d / REL_MAX_EXACT) / math.log(REL_MAX_DISTANCE / REL_MAX_EXACT)
                             * (REL_BUCKETS - REL_MAX_EXACT)).astype(jnp.int32)
    large = jnp.minimum(large, REL_BUCKETS - 1)
    return jnp.where(dist < REL_MAX_EXACT, dist, large)

def causal_depthwise_conv(u, w, b):
    c = u.shape[-1]
    out = lax.conv_general_dilated(u, w.astype(u.dtype)[:, None, :], window_strides=(1,),
                                   padding=((w.shape[0] - 1, 0),),
                                   dimension_numbers=('NWC', 'WIO', 'NWC'),
                                   feature_group_count=c)
    return out + b.astype(u.dtype)

def ssd_chunked_scan(xs, bm, cm, dt_raw, dt_bias, a_log, d_skip):
    f32 = jnp.float32
    bsz, s_len, n_h, p_dim = xs.shape
    n_g, n_s = bm.shape[2], bm.shape[3]
    r = n_h // n_g
    lc = SSM_CHUNK
    nc = -(-s_len // lc)
    pad = nc * lc - s_len
    xs, bm, cm = xs.astype(f32), bm.astype(f32), cm.astype(f32)
    dt = jax.nn.softplus(dt_raw.astype(f32) + dt_bias.astype(f32))
    a = dt * (-jnp.exp(a_log.astype(f32)))

    def padseq(u):
        return jnp.pad(u, [(0, 0), (0, pad)] + [(0, 0)] * (u.ndim - 2))

    xc = padseq(xs * dt[..., None]).reshape(bsz, nc, lc, n_g, r, p_dim)
    bc = padseq(bm).reshape(bsz, nc, lc, n_g, n_s)
    cc = padseq(cm).reshape(bsz, nc, lc, n_g, n_s)
    acum_l = jnp.cumsum(padseq(a).reshape(bsz, nc, lc, n_g, r), axis=2)
    acum = jnp.moveaxis(acum_l, 2, -1)
    causal = jnp.tril(jnp.ones((lc, lc), dtype=bool))
    decay_in = jnp.exp(jnp.where(causal, acum[..., :, None] - acum[..., None, :], -jnp.inf))
    cb = jnp.einsum('bclgn,bcsgn->bcgls', cc, bc)
    y_diag = jnp.einsum('bcgrls,bcsgrp->bclgrp', cb[:, :, :, None] * decay_in, xc)
    decay_to_end = jnp.exp(acum_l[:, :, -1:] - acum_l)
    states = jnp.einsum('bclgn,bclgrp->bcgrpn', bc, xc * decay_to_end[..., None])
    chunk_decay = jnp.exp(acum[..., -1])

    def step(h, inp):
        st, dec = inp
        return h * dec[..., None, None] + st, h

    h0 = jnp.zeros((bsz, n_g, r, p_dim, n_s), f32)
    _, h_in = lax.scan(step, h0, (jnp.moveaxis(states, 1, 0), jnp.moveaxis(chunk_decay, 1, 0)))
    h_in = jnp.moveaxis(h_in, 0, 1)
    y_off = jnp.einsum('bclgn,bcgrpn->bclgrp', cc, h_in) * jnp.exp(acum_l)[..., None]
    y = (y_diag + y_off).reshape(bsz, nc * lc, n_h, p_dim)[:, :s_len]
    return y + d_skip.astype(f32)[:, None] * xs

def mamba2_branch(z, xbc, dt_raw, conv_w, conv_b, dt_bias, a_log, d_skip, norm_w):
    bsz, s_len, _ = z.shape
    xbc = jax.nn.silu(causal_depthwise_conv(xbc, conv_w, conv_b))
    xs, bm, cm = jnp.split(xbc, [BRANCH_WIDTH, BRANCH_WIDTH + SSM_BC], axis=-1)
    y = ssd_chunked_scan(xs.reshape(bsz, s_len, SSM_HEADS, HEAD_DIM),
                         bm.reshape(bsz, s_len, SSM_GROUPS, SSM_STATE),
                         cm.reshape(bsz, s_len, SSM_GROUPS, SSM_STATE),
                         dt_raw, dt_bias, a_log, d_skip)
    y = y.reshape(bsz, s_len, BRANCH_WIDTH).astype(z.dtype)
    return rmsnorm(y * jax.nn.silu(z), norm_w)

def moba_attention(q, k, v, bias_tab):
    f32 = jnp.float32
    bsz, s_len, n_h, hd = q.shape
    nblk = -(-s_len // MOBA_BLOCK)
    s_pad = nblk * MOBA_BLOCK
    topk = min(MOBA_TOPK, nblk)
    scale = hd ** -0.5
    qh = q.transpose(0, 2, 1, 3)

    def blocks(u):
        u = jnp.pad(u, ((0, 0), (0, s_pad - s_len), (0, 0), (0, 0)))
        return u.reshape(bsz, nblk, MOBA_BLOCK, n_h, hd).transpose(0, 3, 1, 2, 4)

    kb, vb = blocks(k), blocks(v)
    k_mean = jnp.mean(kb.astype(f32), axis=3)
    q_blk = jnp.arange(s_len) // MOBA_BLOCK
    gate = jnp.einsum('bhsd,bhnd->bhsn', qh.astype(f32), k_mean)
    fully_past = jnp.arange(nblk)[None, :] < q_blk[:, None]
    gate = jnp.where(fully_past, gate, -jnp.inf)
    _, sel = lax.top_k(gate, topk)
    sel_valid = jnp.arange(topk)[None, :] < q_blk[:, None]
    bias_ht = bias_tab.T.astype(f32)
    b_idx = jnp.arange(bsz)[:, None, None, None]
    h_idx = jnp.arange(n_h)[None, :, None, None]
    blk_off = jnp.arange(MOBA_BLOCK)

    def chunk(c):
        start = c * MOBA_Q_CHUNK
        qc = lax.dynamic_slice_in_dim(qh, start, MOBA_Q_CHUNK, axis=2)
        selc = lax.dynamic_slice_in_dim(sel, start, MOBA_Q_CHUNK, axis=2)
        validc = lax.dynamic_slice_in_dim(sel_valid, start, MOBA_Q_CHUNK, axis=0)
        qpos = start + jnp.arange(MOBA_Q_CHUNK)
        kg = kb[b_idx, h_idx, selc]
        vg = vb[b_idx, h_idx, selc]
        s_sel = jnp.einsum('bhqd,bhqkjd->bhqkj', qc, kg).astype(f32) * scale
        kpos = selc[..., None] * MOBA_BLOCK + blk_off
        s_sel = s_sel + bias_ht[h_idx[..., None], rel_bucket(qpos[:, None, None] - kpos)]
        s_sel = jnp.where(validc[None, None, :, :, None], s_sel, -jnp.inf)
        own = start // MOBA_BLOCK
        ko = lax.dynamic_index_in_dim(kb, own, axis=2, keepdims=False)
        vo = lax.dynamic_index_in_dim(vb, own, axis=2, keepdims=False)
        dist_own = qpos[:, None] - (own * MOBA_BLOCK + blk_off)[None, :]
        s_own = jnp.einsum('bhqd,bhjd->bhqj', qc, ko).astype(f32) * scale
        s_own = s_own + bias_ht[:, rel_bucket(dist_own)][None]
        s_own = jnp.where(dist_own >= 0, s_own, -jnp.inf)
        logits = jnp.concatenate([s_sel.reshape(bsz, n_h, MOBA_Q_CHUNK, topk * MOBA_BLOCK), s_own], axis=-1)
        p = jax.nn.softmax(logits, axis=-1)
        p_sel = p[..., :topk * MOBA_BLOCK].reshape(bsz, n_h, MOBA_Q_CHUNK, topk, MOBA_BLOCK).astype(v.dtype)
        p_own = p[..., topk * MOBA_BLOCK:].astype(v.dtype)
        return (jnp.einsum('bhqkj,bhqkjd->bhqd', p_sel, vg)
                + jnp.einsum('bhqj,bhjd->bhqd', p_own, vo))

    out = lax.map(chunk, jnp.arange(s_len // MOBA_Q_CHUNK))
    return out.transpose(1, 0, 3, 2, 4).reshape(bsz, s_len, n_h * hd)

def forgetting_attention(q, k, v, f_logit):
    f32 = jnp.float32
    bsz, s_len, n_h, hd = q.shape
    scale = hd ** -0.5
    cum = jnp.cumsum(jax.nn.log_sigmoid(f_logit.astype(f32)), axis=1).transpose(0, 2, 1)
    qh, kh, vh = (u.transpose(0, 2, 1, 3) for u in (q, k, v))
    kpos = jnp.arange(s_len)

    def block(i):
        start = i * FOX_Q_BLOCK
        qb = lax.dynamic_slice_in_dim(qh, start, FOX_Q_BLOCK, axis=2)
        cq = lax.dynamic_slice_in_dim(cum, start, FOX_Q_BLOCK, axis=2)
        s = (jnp.einsum('bhqd,bhkd->bhqk', qb, kh).astype(f32) * scale
             + (cq[..., :, None] - cum[..., None, :]))
        causal = (start + jnp.arange(FOX_Q_BLOCK))[:, None] >= kpos[None, :]
        p = jax.nn.softmax(jnp.where(causal, s, -jnp.inf), axis=-1)
        return jnp.einsum('bhqk,bhkd->bhqd', p.astype(v.dtype), vh)

    out = lax.map(block, jnp.arange(s_len // FOX_Q_BLOCK))
    return out.transpose(1, 0, 3, 2, 4).reshape(bsz, s_len, n_h * hd)

def sliding_window_attention(q, k, v, sinks, bias_tab):
    f32 = jnp.float32
    bsz, s_len, n_q, hd = q.shape
    n_kv = k.shape[2]
    grp = n_q // n_kv
    w = SWA_WINDOW
    nb = s_len // w
    scale = hd ** -0.5
    qb = q.reshape(bsz, nb, w, n_kv, grp, hd)

    def band(u):
        ub = u.reshape(bsz, nb, w, n_kv, hd)
        prev = jnp.pad(ub, ((0, 0), (1, 0), (0, 0), (0, 0), (0, 0)))[:, :-1]
        return jnp.concatenate([prev, ub], axis=2)

    kk, vv = band(k), band(v)
    s = jnp.einsum('bnqkgd,bnjkd->bnkgqj', qb, kk).astype(f32) * scale
    qi = jnp.arange(w)[:, None]
    kj = jnp.arange(2 * w)[None, :]
    dist = qi + w - kj
    in_window = (dist >= 0) & (dist < w)
    key_pos = jnp.arange(nb)[:, None, None] * w + kj[None] - w
    mask = in_window[None] & (key_pos >= 0)
    bias = bias_tab.astype(f32)[rel_bucket(dist)].transpose(2, 0, 1).reshape(n_kv, grp, w, 2 * w)
    s = jnp.where(mask[None, :, None, None], s + bias, -jnp.inf)
    sink = jnp.broadcast_to(sinks.astype(f32).reshape(n_kv, grp, 1, 1), s.shape[:-1] + (1,))
    p = jax.nn.softmax(jnp.concatenate([s, sink], axis=-1), axis=-1)[..., :-1]
    out = jnp.einsum('bnkgqj,bnjkd->bnqkgd', p.astype(v.dtype), vv)
    return out.reshape(bsz, s_len, n_q * hd)

def hybrid_mixer(h, w_in, conv_w, conv_b, dt_bias, a_log, d_skip, ssm_norm_w,
                 forget_bias, sinks, rel_bias, w_branch, w_out):
    bsz, s_len, _ = h.shape
    proj = h @ w_in
    (m_z, m_xbc, m_dt, b_qkv, c_qkv, c_f, d_q, d_kv, gate_logits) = jnp.split(proj, SPLIT_POINTS, axis=-1)

    def heads(u, n):
        return u.reshape(bsz, s_len, n, HEAD_DIM)

    y_a = mamba2_branch(m_z, m_xbc, m_dt, conv_w, conv_b, dt_bias, a_log, d_skip, ssm_norm_w)
    bq, bk, bv = jnp.split(b_qkv, 3, axis=-1)
    y_b = moba_attention(heads(bq, N_HEADS), heads(bk, N_HEADS), heads(bv, N_HEADS), rel_bias[:, :N_HEADS])
    cq, ck, cv = jnp.split(c_qkv, 3, axis=-1)
    y_c = forgetting_attention(heads(cq, N_HEADS), heads(ck, N_HEADS), heads(cv, N_HEADS), c_f + forget_bias)
    dk, dv = jnp.split(d_kv, 2, axis=-1)
    y_d = sliding_window_attention(heads(d_q, N_HEADS), heads(dk, SWA_KV_HEADS), heads(dv, SWA_KV_HEADS),
                                   sinks, rel_bias[:, N_HEADS:])
    branches = jnp.stack([y_a, y_b, y_c, y_d], axis=2)
    branch_out = jnp.einsum('bsiw,iwd->bsid', branches, w_branch)
    gates = jax.nn.sigmoid(gate_logits.reshape(bsz, s_len, N_BRANCHES, D_MODEL))
    return jnp.sum(gates * branch_out, axis=2) @ w_out

def swiglu(h, w_gate, w_up, w_down):
    return (jax.nn.silu(h @ w_gate) * (h @ w_up)) @ w_down

def first_inputs(seed: int = 0) -> dict:
    key = jax.random.key(seed)
    ks = jax.random.split(key, 20)
    nrm = jax.random.normal
    x = nrm(ks[0], (BATCH, SEQ, D_MODEL), jnp.float32)
    w_in = nrm(ks[1], (DEPTH, D_MODEL, D_IN_PROJ), jnp.float32) * D_MODEL ** -0.5
    conv_w = nrm(ks[2], (DEPTH, SSM_CONV, SSM_CONV_DIM), jnp.float32) * SSM_CONV ** -0.5
    conv_b = 0.02 * nrm(ks[3], (DEPTH, SSM_CONV_DIM), jnp.float32)
    dt0 = jnp.exp(jax.random.uniform(ks[4], (DEPTH, SSM_HEADS), jnp.float32,
                                     minval=math.log(1e-3), maxval=math.log(1e-1)))
    dt_bias = dt0 + jnp.log(-jnp.expm1(-dt0))
    a_log = jnp.log(jax.random.uniform(ks[5], (DEPTH, SSM_HEADS), jnp.float32, minval=1.0, maxval=16.0))
    d_skip = 1.0 + 0.1 * nrm(ks[6], (DEPTH, SSM_HEADS), jnp.float32)
    ssm_norm_w = 1.0 + 0.05 * nrm(ks[7], (DEPTH, BRANCH_WIDTH), jnp.float32)
    forget_bias = jax.random.uniform(ks[8], (DEPTH, N_HEADS), jnp.float32, minval=1.0, maxval=6.0)
    sinks = nrm(ks[9], (DEPTH, N_HEADS), jnp.float32)
    rel_bias = 0.3 * nrm(ks[10], (REL_BUCKETS, N_BIAS_HEADS), jnp.float32)
    w_branch = nrm(ks[11], (DEPTH, N_BRANCHES, BRANCH_WIDTH, D_MODEL), jnp.float32) * BRANCH_WIDTH ** -0.5
    w_out = nrm(ks[12], (DEPTH, D_MODEL, D_MODEL), jnp.float32) * D_MODEL ** -0.5
    norm_mix = 1.0 + 0.05 * nrm(ks[13], (DEPTH, D_MODEL), jnp.float32)
    norm_ffn = 1.0 + 0.05 * nrm(ks[14], (DEPTH, D_MODEL), jnp.float32)
    w_ffn_gate = nrm(ks[15], (DEPTH, D_MODEL, D_FF), jnp.float32) * D_MODEL ** -0.5
    w_ffn_up = nrm(ks[16], (DEPTH, D_MODEL, D_FF), jnp.float32) * D_MODEL ** -0.5
    w_ffn_down = nrm(ks[17], (DEPTH, D_FF, D_MODEL), jnp.float32) * D_FF ** -0.5
    norm_final = 1.0 + 0.05 * nrm(ks[18], (D_MODEL,), jnp.float32)
    return {'x': x, 'w_in': w_in, 'conv_w': conv_w, 'conv_b': conv_b, 'dt_bias': dt_bias,
            'a_log': a_log, 'd_skip': d_skip, 'ssm_norm_w': ssm_norm_w, 'forget_bias': forget_bias,
            'sinks': sinks, 'rel_bias': rel_bias, 'w_branch': w_branch, 'w_out': w_out,
            'norm_mix': norm_mix, 'norm_ffn': norm_ffn, 'w_ffn_gate': w_ffn_gate,
            'w_ffn_up': w_ffn_up, 'w_ffn_down': w_ffn_down, 'norm_final': norm_final}

def first_block(x, w_in, conv_w, conv_b, dt_bias, a_log, d_skip, ssm_norm_w, forget_bias,
              sinks, rel_bias, w_branch, w_out, norm_mix, norm_ffn, w_ffn_gate,
              w_ffn_up, w_ffn_down, norm_final):
    for l in range(DEPTH):
        h = rmsnorm(x, norm_mix[l])
        x = x + hybrid_mixer(h, w_in[l], conv_w[l], conv_b[l], dt_bias[l], a_log[l], d_skip[l],
                             ssm_norm_w[l], forget_bias[l], sinks[l], rel_bias, w_branch[l], w_out[l])
        h = rmsnorm(x, norm_ffn[l])
        x = x + swiglu(h, w_ffn_gate[l], w_ffn_up[l], w_ffn_down[l])
    return rmsnorm(x, norm_final)


CHUNK = 64
Q_BLOCK = 128
N_MIX_HEADS = D_MODEL // HEAD_DIM
MLA_HEADS = N_MIX_HEADS // 4
RWKV_HEADS = (N_MIX_HEADS - MLA_HEADS) // 2
GDN_HEADS = N_MIX_HEADS - MLA_HEADS - RWKV_HEADS
RWKV_WIDTH = RWKV_HEADS * HEAD_DIM
MLA_WIDTH = MLA_HEADS * HEAD_DIM
GDN_WIDTH = GDN_HEADS * HEAD_DIM
MIX_WIDTH = RWKV_WIDTH + MLA_WIDTH + GDN_WIDTH

RWKV_DECAY_LORA = 64
RWKV_ICLR_LORA = 64
RWKV_GATE_LORA = 128
RWKV_GN_EPS = 64e-5

MLA_NOPE_DIM = 64
MLA_ROPE_DIM = 32
MLA_QK_DIM = MLA_NOPE_DIM + MLA_ROPE_DIM
MLA_V_DIM = HEAD_DIM
MLA_Q_LORA = 256
MLA_KV_LORA = 128
ROPE_BASE = 10000.0

GDN_CONV = 4

D_FF_2 = 4 * D_MODEL

RWKV_SPLITS = (RWKV_WIDTH, RWKV_WIDTH, RWKV_WIDTH, RWKV_DECAY_LORA, RWKV_ICLR_LORA, RWKV_GATE_LORA)
MLA_SPLITS = (MLA_Q_LORA, MLA_KV_LORA, MLA_ROPE_DIM)
GDN_SPLITS = (GDN_WIDTH, GDN_WIDTH, GDN_WIDTH, GDN_WIDTH, GDN_HEADS, GDN_HEADS)
RWKV_IN = 3 * RWKV_WIDTH + RWKV_DECAY_LORA + RWKV_ICLR_LORA + RWKV_GATE_LORA
MLA_IN = MLA_Q_LORA + MLA_KV_LORA + MLA_ROPE_DIM
GDN_IN = 4 * GDN_WIDTH + 2 * GDN_HEADS
P_IN = RWKV_IN + MLA_IN + GDN_IN


def _split(t, sizes):
    idx = np.cumsum(np.array(sizes))[:-1].tolist()
    return jnp.split(t, idx, axis=-1)

def _rms(x, g, eps=NORM_EPS):
    xf = x.astype(jnp.float32)
    y = xf * lax.rsqrt(jnp.mean(xf * xf, axis=-1, keepdims=True) + eps)
    return (y * g.astype(jnp.float32)).astype(x.dtype)

def _l2norm(x, eps=1e-6):
    xf = x.astype(jnp.float32)
    return xf * lax.rsqrt(jnp.sum(xf * xf, axis=-1, keepdims=True) + eps)

def _rope(t, cos, sin):
    t1, t2 = jnp.split(t, 2, axis=-1)
    return jnp.concatenate([t1 * cos - t2 * sin, t1 * sin + t2 * cos], axis=-1)

def rwkv7_time_mix(p, mu, w0, w2, a0, a2, g2, k_k, k_a, r_k, gn_g, gn_b):
    f32 = jnp.float32
    B, S, _ = p.shape
    p_prev = jnp.pad(p, ((0, 0), (1, 0), (0, 0)))[:, :-1]
    z = p + (p_prev - p) * mu
    r, k, v, zw, za, zg = _split(z, RWKV_SPLITS)
    w_logit = (w0 + jnp.tanh(zw) @ w2).astype(f32)
    decay = jnp.exp(-jnp.exp(-jax.nn.softplus(-w_logit) - 0.5))
    a = jax.nn.sigmoid((a0 + za @ a2).astype(f32))
    g = jax.nn.sigmoid(zg) @ g2
    hs = lambda t: t.reshape(B, S, RWKV_HEADS, HEAD_DIM).astype(f32)
    hp = lambda t: t.reshape(RWKV_HEADS, HEAD_DIM).astype(f32)
    r, k, v, a, decay = hs(r), hs(k), hs(v), hs(a), hs(decay)
    kk = _l2norm(k * hp(k_k))
    k = k * (1.0 + (a - 1.0) * hp(k_a))

    def step(state, inp):
        r_t, w_t, k_t, v_t, kk_t, b_t = inp
        sa = jnp.einsum('bhvk,bhk->bhv', state, -kk_t)
        state = (state * w_t[:, :, None, :] + sa[..., None] * b_t[:, :, None, :]
                 + v_t[..., None] * k_t[:, :, None, :])
        return state, jnp.einsum('bhvk,bhk->bhv', state, r_t)

    tm = lambda t: jnp.moveaxis(t, 1, 0)
    s0 = jnp.zeros((B, RWKV_HEADS, HEAD_DIM, HEAD_DIM), f32)
    _, y = lax.scan(step, s0, (tm(r), tm(decay), tm(k), tm(v), tm(kk), tm(kk * a)))
    y = jnp.moveaxis(y, 0, 1)
    mean = jnp.mean(y, axis=-1, keepdims=True)
    var = jnp.mean(jnp.square(y - mean), axis=-1, keepdims=True)
    y = ((y - mean) * lax.rsqrt(var + RWKV_GN_EPS)).reshape(B, S, RWKV_WIDTH)
    y = y * gn_g.astype(f32) + gn_b.astype(f32)
    bonus = jnp.sum(r * k * r_k.astype(f32), axis=-1, keepdims=True) * v
    y = y + bonus.reshape(B, S, RWKV_WIDTH)
    return (y * g.astype(f32)).astype(p.dtype)

def mla_attention(p, positions, q_norm_g, w_uq, kv_norm_g, w_ukv, q_qk_g, k_qk_g):
    f32 = jnp.float32
    B, S, _ = p.shape
    c_q, c_kv, k_rope = _split(p, MLA_SPLITS)
    q = (_rms(c_q, q_norm_g) @ w_uq).reshape(B, S, MLA_HEADS, MLA_QK_DIM)
    kv = (_rms(c_kv, kv_norm_g) @ w_ukv).reshape(B, S, MLA_HEADS, MLA_NOPE_DIM + MLA_V_DIM)
    k_nope, v = jnp.split(kv, [MLA_NOPE_DIM], axis=-1)
    k_rope = jnp.broadcast_to(k_rope[:, :, None, :], (B, S, MLA_HEADS, MLA_ROPE_DIM))
    k = jnp.concatenate([k_nope, k_rope], axis=-1)
    q = _rms(q, q_qk_g)
    k = _rms(k, k_qk_g)
    inv_freq = ROPE_BASE ** (-jnp.arange(0, MLA_ROPE_DIM, 2, dtype=f32) / MLA_ROPE_DIM)
    ang = positions.astype(f32)[..., None] * inv_freq
    cos = jnp.cos(ang)[:, :, None, :].astype(q.dtype)
    sin = jnp.sin(ang)[:, :, None, :].astype(q.dtype)
    q = jnp.concatenate([q[..., :MLA_NOPE_DIM], _rope(q[..., MLA_NOPE_DIM:], cos, sin)], axis=-1)
    k = jnp.concatenate([k[..., :MLA_NOPE_DIM], _rope(k[..., MLA_NOPE_DIM:], cos, sin)], axis=-1)
    scale = MLA_QK_DIM ** -0.5
    nb = S // Q_BLOCK
    qb = jnp.moveaxis(q.reshape(B, nb, Q_BLOCK, MLA_HEADS, MLA_QK_DIM), 1, 0)
    k_chunk = jnp.arange(S) // CHUNK

    def block(args):
        q_blk, i = args
        s = jnp.einsum('bqhd,bkhd->bhqk', q_blk, k).astype(f32) * scale
        q_chunk = (i * Q_BLOCK + jnp.arange(Q_BLOCK)) // CHUNK
        s = jnp.where(k_chunk[None, :] <= q_chunk[:, None], s, -jnp.inf)
        prob = jax.nn.softmax(s, axis=-1).astype(v.dtype)
        return jnp.einsum('bhqk,bkhd->bqhd', prob, v)

    o = lax.map(block, (qb, jnp.arange(nb)))
    return jnp.moveaxis(o, 0, 1).reshape(B, S, MLA_WIDTH)

def _chunk_gated_delta_rule(q, k, v, beta, g):
    B, S, H, Dk = q.shape
    Dv = v.shape[-1]
    NC, L = S // CHUNK, CHUNK
    ch = lambda t: jnp.moveaxis(t.reshape(B, NC, L, H, -1), 3, 1)
    q, k, v = ch(q), ch(k), ch(v)
    beta, g = ch(beta[..., None])[..., 0], ch(g[..., None])[..., 0]
    gc = jnp.cumsum(g, axis=-1)
    idx = jnp.arange(L)
    incl = idx[:, None] >= idx[None, :]
    strict = idx[:, None] > idx[None, :]
    decay = jnp.exp(jnp.where(incl, gc[..., :, None] - gc[..., None, :], -jnp.inf))
    A = jnp.where(strict, jnp.einsum('bhnld,bhnmd->bhnlm', k, k) * decay * beta[..., :, None], 0.0)
    rhs = jnp.concatenate([v * beta[..., None], k * (beta * jnp.exp(gc))[..., None]], axis=-1)
    sol = lax.linalg.triangular_solve(A + jnp.eye(L, dtype=A.dtype), rhs,
                                      left_side=True, lower=True, unit_diagonal=True)
    u, w = sol[..., :Dv], sol[..., Dv:]
    attn = jnp.einsum('bhnld,bhnmd->bhnlm', q, k) * decay
    q_dec = q * jnp.exp(gc)[..., None]
    k_dec = k * jnp.exp(gc[..., -1:] - gc)[..., None]
    chunk_decay = jnp.exp(gc[..., -1])

    def step(state, inp):
        u_c, w_c, attn_c, q_c, k_c, d_c = inp
        delta = u_c - jnp.einsum('bhlk,bhkv->bhlv', w_c, state)
        o_c = jnp.einsum('bhlk,bhkv->bhlv', q_c, state) + jnp.einsum('bhlm,bhmv->bhlv', attn_c, delta)
        state = d_c[..., None, None] * state + jnp.einsum('bhlk,bhlv->bhkv', k_c, delta)
        return state, o_c

    cm = lambda t: jnp.moveaxis(t, 2, 0)
    s0 = jnp.zeros((B, H, Dk, Dv), jnp.float32)
    _, o = lax.scan(step, s0, (cm(u), cm(w), cm(attn), cm(q_dec), cm(k_dec), cm(chunk_decay)))
    return jnp.transpose(o, (1, 0, 3, 2, 4)).reshape(B, S, H, Dv)

def gated_deltanet(p, conv_w, a_log, dt_bias, o_norm_g):
    f32 = jnp.float32
    B, S, _ = p.shape
    q, k, v, gate, b, a = _split(p, GDN_SPLITS)
    qkv = jnp.concatenate([q, k, v], axis=-1)
    qkv = lax.conv_general_dilated(qkv, conv_w[:, None, :].astype(qkv.dtype), window_strides=(1,),
                                   padding=[(GDN_CONV - 1, 0)], dimension_numbers=('NWC', 'WIO', 'NWC'),
                                   feature_group_count=3 * GDN_WIDTH)
    q, k, v = jnp.split(jax.nn.silu(qkv), 3, axis=-1)
    hd = lambda t: t.reshape(B, S, GDN_HEADS, HEAD_DIM)
    q = _l2norm(hd(q)) * (HEAD_DIM ** -0.5)
    k = _l2norm(hd(k))
    v = hd(v).astype(f32)
    beta = jax.nn.sigmoid(b.astype(f32))
    g = -jnp.exp(a_log.astype(f32)) * jax.nn.softplus(a.astype(f32) + dt_bias.astype(f32))
    o = _chunk_gated_delta_rule(q, k, v, beta, g)
    o = _rms(o, o_norm_g) * jax.nn.silu(hd(gate).astype(f32))
    return o.reshape(B, S, GDN_WIDTH).astype(p.dtype)

def second_inputs(seed: int = 0) -> dict:
    key = jax.random.key(seed)
    keys = list(jax.random.split(key, 40))
    f32 = jnp.float32
    L = DEPTH

    def nrm(shape, scale):
        return jax.random.normal(keys.pop(), shape, f32) * scale

    def gain(shape):
        return 1.0 + 0.05 * jax.random.normal(keys.pop(), shape, f32)

    inp = {}
    inp['x'] = nrm((BATCH, SEQ, D_MODEL), 1.0)
    inp['positions'] = jnp.tile(jnp.arange(SEQ, dtype=jnp.int32)[None, :], (BATCH, 1))
    inp['ln_mix_g'] = gain((L, D_MODEL))
    inp['w_in'] = nrm((L, D_MODEL, P_IN), D_MODEL ** -0.5)
    inp['w_out'] = nrm((L, MIX_WIDTH, D_MODEL), MIX_WIDTH ** -0.5)
    inp['ln_ffn_g'] = gain((L, D_MODEL))
    inp['w_ff1'] = nrm((L, D_MODEL, D_FF_2), D_MODEL ** -0.5)
    inp['w_ff2'] = nrm((L, D_FF_2, D_MODEL), D_FF_2 ** -0.5)
    inp['rwkv_mu'] = jax.random.uniform(keys.pop(), (L, RWKV_IN), f32, 0.0, 1.0)
    inp['rwkv_w0'] = jax.random.uniform(keys.pop(), (L, RWKV_WIDTH), f32, -6.0, 1.0)
    inp['rwkv_w2'] = nrm((L, RWKV_DECAY_LORA, RWKV_WIDTH), 0.5 * RWKV_DECAY_LORA ** -0.5)
    inp['rwkv_a0'] = nrm((L, RWKV_WIDTH), 0.1)
    inp['rwkv_a2'] = nrm((L, RWKV_ICLR_LORA, RWKV_WIDTH), 0.5 * RWKV_ICLR_LORA ** -0.5)
    inp['rwkv_g2'] = nrm((L, RWKV_GATE_LORA, RWKV_WIDTH), RWKV_GATE_LORA ** -0.5)
    inp['rwkv_k_k'] = 0.85 + nrm((L, RWKV_WIDTH), 0.05)
    inp['rwkv_k_a'] = 1.0 + nrm((L, RWKV_WIDTH), 0.05)
    inp['rwkv_r_k'] = nrm((L, RWKV_HEADS, HEAD_DIM), 0.1)
    inp['rwkv_gn_g'] = gain((L, RWKV_WIDTH))
    inp['rwkv_gn_b'] = nrm((L, RWKV_WIDTH), 0.02)
    inp['mla_q_norm_g'] = gain((L, MLA_Q_LORA))
    inp['mla_w_uq'] = nrm((L, MLA_Q_LORA, MLA_HEADS * MLA_QK_DIM), MLA_Q_LORA ** -0.5)
    inp['mla_kv_norm_g'] = gain((L, MLA_KV_LORA))
    inp['mla_w_ukv'] = nrm((L, MLA_KV_LORA, MLA_HEADS * (MLA_NOPE_DIM + MLA_V_DIM)), MLA_KV_LORA ** -0.5)
    inp['mla_q_qk_g'] = gain((L, MLA_QK_DIM))
    inp['mla_k_qk_g'] = gain((L, MLA_QK_DIM))
    inp['gdn_conv_w'] = nrm((L, GDN_CONV, 3 * GDN_WIDTH), GDN_CONV ** -0.5)
    inp['gdn_a_log'] = jnp.log(jax.random.uniform(keys.pop(), (L, GDN_HEADS), f32, 1.0, 16.0))
    dt = jnp.exp(jax.random.uniform(keys.pop(), (L, GDN_HEADS), f32, math.log(1e-3), math.log(1e-1)))
    inp['gdn_dt_bias'] = dt + jnp.log(-jnp.expm1(-dt))
    inp['gdn_o_norm_g'] = gain((L, HEAD_DIM))
    return inp

def second_block(x, positions, ln_mix_g, w_in, w_out, ln_ffn_g, w_ff1, w_ff2,
              rwkv_mu, rwkv_w0, rwkv_w2, rwkv_a0, rwkv_a2, rwkv_g2, rwkv_k_k, rwkv_k_a,
              rwkv_r_k, rwkv_gn_g, rwkv_gn_b,
              mla_q_norm_g, mla_w_uq, mla_kv_norm_g, mla_w_ukv, mla_q_qk_g, mla_k_qk_g,
              gdn_conv_w, gdn_a_log, gdn_dt_bias, gdn_o_norm_g):
    h = x
    for l in range(DEPTH):
        u = _rms(h, ln_mix_g[l])
        p = u @ w_in[l]
        p_rwkv, p_mla, p_gdn = _split(p, (RWKV_IN, MLA_IN, GDN_IN))
        y_rwkv = rwkv7_time_mix(p_rwkv, rwkv_mu[l], rwkv_w0[l], rwkv_w2[l], rwkv_a0[l], rwkv_a2[l],
                                rwkv_g2[l], rwkv_k_k[l], rwkv_k_a[l], rwkv_r_k[l],
                                rwkv_gn_g[l], rwkv_gn_b[l])
        y_mla = mla_attention(p_mla, positions, mla_q_norm_g[l], mla_w_uq[l], mla_kv_norm_g[l],
                              mla_w_ukv[l], mla_q_qk_g[l], mla_k_qk_g[l])
        y_gdn = gated_deltanet(p_gdn, gdn_conv_w[l], gdn_a_log[l], gdn_dt_bias[l], gdn_o_norm_g[l])
        y = jnp.concatenate([y_rwkv, y_mla, y_gdn], axis=-1)
        h = h + y @ w_out[l]
        u = _rms(h, ln_ffn_g[l])
        h = h + jnp.square(jax.nn.relu(u @ w_ff1[l])) @ w_ff2[l]
    return h


def setup_inputs(seed=0):
    out = dict(first_inputs(seed))
    for name, value in second_inputs(seed + 1).items():
        if name != "x":
            out[name + "_2"] = value
    return out


def reference(
    x, w_in, conv_w, conv_b, dt_bias, a_log, d_skip, ssm_norm_w, forget_bias, sinks, rel_bias,
    w_branch, w_out, norm_mix, norm_ffn, w_ffn_gate, w_ffn_up, w_ffn_down, norm_final,
    positions_2, ln_mix_g_2, w_in_2, w_out_2, ln_ffn_g_2, w_ff1_2, w_ff2_2, rwkv_mu_2,
    rwkv_w0_2, rwkv_w2_2, rwkv_a0_2, rwkv_a2_2, rwkv_g2_2, rwkv_k_k_2, rwkv_k_a_2, rwkv_r_k_2,
    rwkv_gn_g_2, rwkv_gn_b_2, mla_q_norm_g_2, mla_w_uq_2, mla_kv_norm_g_2, mla_w_ukv_2,
    mla_q_qk_g_2, mla_k_qk_g_2, gdn_conv_w_2, gdn_a_log_2, gdn_dt_bias_2, gdn_o_norm_g_2,
):
    x = first_block(
        x, w_in, conv_w, conv_b, dt_bias, a_log, d_skip, ssm_norm_w, forget_bias, sinks,
        rel_bias, w_branch, w_out, norm_mix, norm_ffn, w_ffn_gate, w_ffn_up, w_ffn_down,
        norm_final,
    )
    return second_block(
        x, positions_2, ln_mix_g_2, w_in_2, w_out_2, ln_ffn_g_2, w_ff1_2, w_ff2_2, rwkv_mu_2,
        rwkv_w0_2, rwkv_w2_2, rwkv_a0_2, rwkv_a2_2, rwkv_g2_2, rwkv_k_k_2, rwkv_k_a_2,
        rwkv_r_k_2, rwkv_gn_g_2, rwkv_gn_b_2, mla_q_norm_g_2, mla_w_uq_2, mla_kv_norm_g_2,
        mla_w_ukv_2, mla_q_qk_g_2, mla_k_qk_g_2, gdn_conv_w_2, gdn_a_log_2, gdn_dt_bias_2,
        gdn_o_norm_g_2,
    )


_drawn_inputs = setup_inputs


def setup_inputs(seed=0):
    import zlib

    import numpy as np

    out = dict(_drawn_inputs(seed))
    spreads = {}
    factors = {'conv_b': 3.3,
     'sinks': 2.795,
     'rwkv_w2_2': 6.622,
     'rwkv_a0_2': 4.159,
     'rwkv_k_k_2': 118.866,
     'rwkv_k_a_2': 3.15,
     'rwkv_gn_g_2': 15.496,
     'rwkv_gn_b_2': 39.949,
     'mla_q_norm_g_2': 8.0,
     'mla_kv_norm_g_2': 8.0,
     'mla_q_qk_g_2': 8.0,
     'mla_k_qk_g_2': 8.0,
     'gdn_o_norm_g_2': 13.124,
     'ln_ffn_g_2': 3.564,
     'rwkv_r_k_2': 4.069}
    for name, (base, spread) in spreads.items():
        noise = np.random.default_rng([zlib.crc32(name.encode()), seed]).standard_normal(out[name].shape)
        drawn = base * np.exp(spread * noise) if base else spread * noise
        out[name] = jnp.asarray(drawn.astype(out[name].dtype))
    for name, factor in factors.items():
        out[name] = (out[name] * factor).astype(out[name].dtype)
    return out
```

```python
from contextlib import ExitStack

import concourse.bass as bass
from concourse import mybir

F32 = mybir.dt.float32
F32R = mybir.dt.float32r
I32 = mybir.dt.int32
ALU = mybir.AluOpType
ACT = mybir.ActivationFunctionType
AX_X = mybir.AxisListType.X

P = 128
S = 256
TT = S // P
D = 1024
KD = D // P
HD = 64
NH = 8
BW = 512
EPS = 1e-6
NEG = -1e30
NRING = 3
SLOT = 4096
FF1_CHUNKS, FF1_KT = 11, 22
FF2_CHUNKS, FF2_KT = 8, 32
RH = 6
MH, QK, NOPE, ROPE = 4, 96, 64, 32
NM = 2 * RH
LEVELS = 7

CHUNKS = [("in1", i, w) for i, w in enumerate([KD * 272] + [KD * 512] * 10)]
CHUNKS += [("gate", i, KD * 512) for i in range(8)]
CHUNKS += [("branch", i, 4 * D) for i in range(4)]
CHUNKS += [("out1", i, KD * 512) for i in range(2)]
CHUNKS += [("ffn1", i, KD * 512) for i in range(FF1_CHUNKS)]
CHUNKS += [("down1", i, min(4, FF1_KT - 4 * i) * D) for i in range((FF1_KT + 3) // 4)]
CHUNKS += [("in2", i, w) for i, w in enumerate([KD * 416, KD * 512, KD * 512, KD * 396] + [KD * 512] * 3)]
CHUNKS += [("out2", i, KD * 512) for i in range(2)]
CHUNKS += [("ffn2", i, KD * 512) for i in range(FF2_CHUNKS)]
CHUNKS += [("down2", i, 4 * D) for i in range(FF2_KT // 4)]
CHUNK_AT = {(n, i): k for k, (n, i, _) in enumerate(CHUNKS)}
OFFSET = [0]
for _n, _i, _w in CHUNKS:
    OFFSET.append(OFFSET[-1] + P * _w)

JOBS = [("in1", i, j) for i in range(11) for j in range(2)]
JOBS += [("gate", i, j) for i in range(8) for j in range(2)]
JOBS += [("branch", i, j) for i in range(4) for j in range(4)]
JOBS += [("out1", i, j) for i in range(2) for j in range(2)]
JOBS += [("ffn1", i, j) for i in range(FF1_CHUNKS) for j in range(2)]
JOBS += [("in2", i, j) for i in range(7) for j in range(3 if i == 3 else 2)]
JOBS += [("out2", i, j) for i in range(2) for j in range(2)]
JOBS += [("ffn2", i, j) for i in range(FF2_CHUNKS) for j in range(2)]
JOB_AT = {j: k for k, j in enumerate(JOBS)}

SPLIT = ("branch", "out1", "ffn1", "down1", "out2", "ffn2", "down2")
PIECE = 2048
PIECES = [(n, i, j) for n, i, w in CHUNKS if n in SPLIT for j in range(w // PIECE)]
PIECE_AT = {p: k for k, p in enumerate(PIECES)}

PARAMS = [("norm_mix", 8), ("norm_ffn", 8), ("ln_mix", 8), ("ln_ffn", 8), ("conv_w", 32), ("conv_b", 8),
          ("ssm_norm", 4), ("dt_bias", 1), ("a_log", 1), ("forget_bias", 1), ("sinks", 8), ("d_skip", 8)]
PARAMS2 = [("mu", 11), ("w0", 3), ("a0", 3), ("k_k", 3), ("k_a", 3), ("r_k", 3), ("gn_g", 3), ("gn_b", 3),
           ("q_norm", 2), ("kv_norm", 1), ("g_conv", 36), ("g_alog", 1), ("g_dtb", 1), ("o_norm", 1),
           ("q_qk", 96), ("k_qk", 96), ("w2a2", 384), ("g2", 384), ("uq", 768), ("ukv", 512),
           ("inv_freq", 16), ("strict", 128), ("incl", 128), ("levels", LEVELS * 128), ("blockones", 128), ("pair_rows", 384)]
CONSTS = [("ident", 128), ("causal", 256), ("ssd_mask", 384), ("mla_mask", 256), ("ones", 256)]
TABLES = [("onehot", 384), ("table_mask", 384)]


def columns(table):
    at, out = 0, {}
    for name, n in table:
        out[name] = (at, at + n)
        at += n
    return out, at


PCOL, NP1 = columns(PARAMS)
P2COL, NP2 = columns(PARAMS2)
CCOL, NC = columns(CONSTS)
TCOL, NT = columns(TABLES)

UNITS = [(b, h) for b in (2, 0, 1, 3) for h in range(NH)]

TWO_PI_A, TWO_PI_B, TWO_PI_C = 6.28125, 0.0019340515136718750, 1.2556659146e-06
ROUND = 12582912.0
E_HALF = 0.6065306597126334


def weight_slots(kind, index):
    k = CHUNK_AT[kind, index]
    return k % NRING, k // NRING + 1


def pieces_before(kind, index, j, counted):
    return sum(1 for p in PIECES[:PIECE_AT[kind, index, j] + 1] if p[0] in counted)


def norm_fills(n):
    return [(("norm", n, b), b) for b in range(4)]


def ring(names, banks, start=0):
    return [(name, banks[(start + k) % len(banks)]) for k, name in enumerate(names)]


HIGH = [4, 5, 6, 7]
ALL8 = [4, 5, 6, 7, 0, 1, 2, 3]
FILLS = [(("table",), 4)] + norm_fills(0)
FILLS += [(("dt_T",), 5), (("xs_T", 0), 6), (("xs_T", 1), 7), (("cb", 0), 4), (("cb", 1), 5)]
FILLS += [(("y_T", i, b), 4 + 2 * (i % 2) + b) for i in range(4) for b in range(2)]
FILLS += [(("mix_T", b), 4 + b) for b in range(4)]
FILLS += norm_fills(1) + [(("down1", b), 4 + b) for b in range(4)]
FILLS += norm_fills(2)
FILLS += ring([("mla_ss",), ("mla_q", 0), ("mla_q", 1), ("mla_kv", 0), ("mla_kv", 1)]
              + [("mla_T", b) for b in range(4)], HIGH)
FILLS += [(("yM_T",), 4)]
EARLY_RW = [("lora", 0), ("lora", 1), ("lora", 2), ("lora", 3), ("rw_g", 0), ("rw_g", 1), ("kk_ss", 0), ("kk_ss", 1),
            ("bonus", 0), ("bonus", 1), ("b_T",), ("k_T",), ("v_T", 0), ("v_T", 1)]
MATS = [(kind, g) for kind in ("aab", "aak", "mrb", "mrk") for g in range(4)]


def matrix(c, h):
    return c * RH + (h % 2) * 3 + h // 2


PLACES = sorted((matrix(c, h), c, h) for c in range(2) for h in range(RH))


def inverse_names(fam):
    out = [(fam, "t0", g) for g in range(3)]
    for lv in range(1, LEVELS):
        out += [(fam, "p", lv, g) for g in range(3)]
        if lv < LEVELS - 1:
            out += [(fam, "t", lv, g) for g in range(3)]
        out += [(fam, "tt", lv, g) for g in range(3)]
    return out


SOLVE_RW = [("sa", 0), ("st",), ("r1", 0), ("r1", 1), ("sa", 1), ("y", 0), ("y", 1)]
POST_RW = [("gn_mean", 0), ("gn_mean", 1), ("gn_var", 0), ("gn_var", 1)]
GDN_PRE = [("gq_ss", 0), ("gq_ss", 1), ("gk_ss", 0), ("gk_ss", 1), ("beta", 0), ("beta", 1), ("g_e",),
           ("g_k",), ("gv_T", 0), ("gv_T", 1), ("gk_T",)] \
    + [("decay", g) for g in range(3)] + [("gkk", g) for g in range(4)] + [("gqk", g) for g in range(4)]
SOLVE_G = [("du", 0), ("gst",), ("gr1", 0), ("gr1", 1), ("du", 1), ("o", 0), ("o", 1), ("o_ss", 0), ("o_ss", 1)]
FILLS += ring(EARLY_RW + MATS + [("av", 0), ("av", 1)] + inverse_names("rw") + SOLVE_RW + POST_RW
              + GDN_PRE + inverse_names("gd") + SOLVE_G, ALL8)
FILLS += norm_fills(3) + [(("down2", b), 4 + b) for b in range(4)]
FILL_AT = {name: k for k, (name, _) in enumerate(FILLS)}
FILL_USES = []
_seen = [0] * 8
for _name, _b in FILLS:
    FILL_USES.append(_seen[_b])
    _seen[_b] += 1


def build(nc, x, weights, params, params2, consts, tables, rel_bias, norm_final, positions, table_dram, out):
    with ExitStack() as ctx:
        def sb(name, shape, dt=F32):
            return ctx.enter_context(nc.sbuf_tensor(name, shape, dt))

        sems = {}

        def sem(name):
            if name not in sems:
                sems[name] = ctx.enter_context(nc.semaphore(name))
            return sems[name]

        places = {}

        def placed(name, shape):
            places[name] = (nc.sbuf_base + 31) // 32 * 32
            return sb(name, shape)

        def over(name, place, at, shape):
            return nc.alloc_sbuf_tensor_at(name, [P] + shape, F32R, offset=places[place] + 4 * at)

        rings = [sb(f"weights{i}", [P, SLOT]) for i in range(NRING)]
        X = sb("X", [P, TT, D])
        HN = placed("HN", [P, TT, D])
        HT = placed("HT", [P, KD, S])
        PRM = sb("PRM", [P, NP1])
        CST = sb("CST", [P, NC])
        NF = sb("NF", [P, D])
        RELB = sb("RELB", [32, 2 * NH])
        POS = sb("POS", [P, TT], I32)
        BIAS = sb("BIAS", [P, 2 * NH, S])
        STAT = sb("STAT", [P, 64])
        SM8 = sb("SM8", [NH, 1792])
        negident = sb("negident", [P, P])
        one_minus_mu = sb("one_minus_mu", [P, 11])
        ARENA = placed("ARENA", [P, 26112])
        OVER_HT, OVER_HN = over("OVER_HT", "HT", 0, [KD, S]), over("OVER_HN", "HN", 0, [KD, S])
        W_HIGH = [[over(f"W_HIGH{b}{i}", "ARENA", at, [PIECE]) for i, at in enumerate(ats)]
                  for b, ats in enumerate(((10240, 12288), (0, 2048)))]
        W_LOW = [[over(f"W_LOW{b}{i}", "ARENA", at, [PIECE]) for i, at in enumerate(ats)]
                 for b, ats in enumerate(((14336, 24064), (4096, 6144)))]
        HID1_HIGH, HID1_LOW = over("HID1_HIGH", "ARENA", 0, [FF1_KT, S]), over("HID1_LOW", "ARENA", 16384, [FF1_KT, S])
        HID2_HIGH, HID2_LOW = over("HID2_HIGH", "ARENA", 8192, [FF2_KT, S]), over("HID2_LOW", "ARENA", 16384, [FF2_KT, S])

        def area(at, *shape):
            n = 1
            for v in shape:
                n *= v
            a = ARENA[:, at:at + n]
            if len(shape) == 2:
                a = a.rearrange("p (a b) -> p a b", a=shape[0])
            return a

        def prm(name, j=0, n=1):
            a = PCOL[name][0] + j
            return PRM[:, a:a + n]

        P2 = BIAS[:, :, :].rearrange("p a b -> p (a b)")

        def prm2(name, j=0, n=1):
            a = P2COL[name][0] + j
            return P2[:, a:a + n]

        def cst(name):
            a, b = CCOL[name]
            return CST[:, a:b]

        TBL = ARENA[:, 0:NT]

        def tbl(name):
            a, b = TCOL[name]
            return TBL[:, a:b]

        ident = cst("ident")
        ones = cst("ones")

        GT = area(0, TT, 4 * D)
        SG = area(5632, 2, 512)
        HF1 = area(6656, 2, 512)
        XBC = area(8192, 8, S)
        CQ1, CK1 = area(10240, 4, S), area(11264, 4, S)
        BQ1, BK1 = area(12288, 4, S), area(13312, 4, S)
        DQ1, DK1 = area(14336, 4, S), area(15360, S)
        CV1, BV1, DV1 = area(15616, TT, BW), area(16640, TT, BW), area(17664, TT, P)
        YB = [HN[:, 0, :].rearrange("p (t w) -> p t w", t=TT)] + [area(17920 + 1024 * i, TT, BW) for i in range(3)]
        SILZ = HN[:, 1, :].rearrange("p (t w) -> p t w", t=TT)
        CB = area(20992, 2, 384)
        XDT = area(21760, TT, BW)
        SB_, PB_, PT_ = area(22784, 2, 384), area(23552, 2, 384), area(24320, 2, 384)
        YT_HIGH = [over(f"YT_HIGH{i}", "ARENA", at, [4, S]) for i, at in enumerate((8192, 9216))]
        YT_LOW = [over(f"YT_LOW{i}", "ARENA", at, [4, S]) for i, at in enumerate((16384, 21504))]
        TMP = area(20992, 512)
        STG = area(22784, 2, 512)
        ACC, TH = area(25088, 2, S), area(25600, 2, S)

        RZ = area(0, 11, S)
        LO, K3, V3, R3 = RZ[:, 0:2, :], RZ[:, 2:5, :], RZ[:, 5:8, :], RZ[:, 8:11, :]
        A3, KK, GM, BON, GG, LW, G3, E3, T3 = [area(2816 + 768 * i, 3, S) for i in range(9)]
        GZ = area(9728, 12, S)
        GQ, GK, GV, GGT = [GZ[:, 3 * i:3 * i + 3, :] for i in range(4)]
        GKB = area(12800, 3, S)
        GKE, GQD, GKD = [area(13568 + 384 * i, 3, P) for i in range(3)]
        BTk, KTk, GKT = [HN[:, 0, 384 * i:384 * (i + 1)] if i < 2 else area(14720, 384) for i in range(3)]
        VT = HN[:, 1, 0:768].rearrange("p (c w) -> p c w", c=2)
        GVT = area(15104, 2, 384)
        AT, TM, TTM, PM = [area(15872 + 1536 * i, NM, P) for i in range(4)]
        MB = area(22016, NM, P)
        MK = area(2816 + 768 * 5, NM, P)
        GAT = MB
        RR = area(23552, 2, 384)
        SA = area(24320, 2, 384)
        ST = area(25088 + 0, 3, HD)
        CQF, SQM = area(15872, 3, S), area(16640, 3, S)
        KR = area(17408, TT, ROPE)
        QM, KM = area(17472, 8, QK), area(18240, 8, QK)
        VM = area(19008, TT, MH * HD)
        SQQ = area(19520, 8, QK)
        QTm, KTm = area(20288, MH, S), area(21312, MH, S)
        COS, SIN, ROT = area(22336, TT, 16), area(22368, TT, 16), area(19520, 4, 128)
        GTMP = area(13568, 3, S)
        YM = NF[:, 0:512].rearrange("p (t w) -> p t w", t=TT)
        YT2 = HT
        HF2 = area(24576, 2, 512)

        BK = [ctx.enter_context(nc.psum_tensor(f"bank{i}", [P, 512], F32)) for i in range(8)]

        def bank_of(name):
            return BK[FILLS[FILL_AT[name]][1]]

        def job_bank(job):
            return BK[JOB_AT[job] % 4]

        def fill_arrived(eng, name):
            eng.wait_ge(sem("fills_written"), FILL_AT[name] + 1)
            return bank_of(name)

        def fill_out(ins, name):
            ins.then_inc(sem(f"fill_out{FILLS[FILL_AT[name]][1]}"), 1)

        def wait_fill_out(eng, name):
            f = FILL_AT[name]
            eng.wait_ge(sem(f"fill_out{FILLS[f][1]}"), FILL_USES[f] + 1)

        def job_arrived(eng, job):
            eng.wait_ge(sem("jobs_written"), JOB_AT[job] + 1)
            return job_bank(job)

        def job_out(ins, job):
            ins.then_inc(sem(f"job_out{JOB_AT[job] % 4}"), 1)

        def wait_job_out(eng, job):
            j = JOB_AT[job]
            eng.wait_ge(sem(f"job_out{j % 4}"), j // 4 + 1)

        def piece_parts(k):
            kind = PIECES[k][0]
            rows = {"branch": 4, "down1": 2, "down2": 2}.get(kind, KD)
            b = 1 if kind in ("out2", "ffn2", "down2") else 0
            return [t[b][k % 2][:, :].rearrange("p (k n) -> p k n", k=rows) for t in (W_HIGH, W_LOW)]

        def piece_source(k):
            kind, i, j = PIECES[k]
            width = CHUNKS[CHUNK_AT[kind, i]][2]
            rows = {"branch": 4, "down1": width // D, "down2": width // D}.get(kind, KD)
            w = rings[weight_slots(kind, i)[0]][:, 0:width].rearrange("p (k n) -> p k n", k=rows)
            if kind in ("down1", "down2"):
                return w[:, 2 * j:2 * j + 2, :]
            n = 512 if kind == "branch" else 256
            return w[:, :, j * n:(j + 1) * n]

        def wait_piece_used(eng, k):
            kind, i, j = PIECES[k]
            if kind in ("ffn1", "ffn2"):
                eng.wait_ge(sem("jobs_written"), JOB_AT[kind, i, j] + 1)
            elif kind == "branch":
                eng.wait_ge(sem("jobs_written"), JOB_AT[kind, i, 2 * j + 1] + 1)
            elif kind in ("out1", "out2"):
                if j == 0:
                    eng.wait_ge(sem("first_halves"), pieces_before(kind, i, j, ("out1", "out2")) // 2 + 1)
                else:
                    eng.wait_ge(sem("jobs_written"), JOB_AT[kind, i, 1] + 1)
            elif PIECES[k + 1:k + 2] and PIECES[k + 1][0] == kind:
                eng.wait_ge(sem(kind + "_pieces_read"), pieces_before(kind, i, j, (kind,)))
            else:
                eng.wait_ge(sem("fills_written"), FILL_AT[kind, 3] + 1)

        def attention_units(n):
            return sum(1 for b, _ in ALL_UNITS[:n] if b != 0)

        ALL_UNITS = UNITS + [(4, h) for h in range(MH)]
        NU = len(UNITS)

        block = ctx.enter_context(nc.Block())

        @block.sync
        def _(sp):
            for k, (kind, i, width) in enumerate(CHUNKS):
                if k >= NRING:
                    was, n = CHUNKS[k - NRING][0:2]
                    if was in SPLIT:
                        sp.wait_ge(sem("pieces_split"), max(PIECE_AT[p] for p in PIECES if p[:2] == (was, n)) + 1)
                    else:
                        sp.wait_ge(sem("jobs_written"), max(JOB_AT[j] for j in JOBS if j[:2] == (was, n)) + 1)
                src = weights[OFFSET[k]:OFFSET[k + 1]].rearrange("(p n) -> p n", p=P)
                sp.dma_start(rings[k % NRING][:, 0:width], src).then_inc(sem(f"weights_in{k % NRING}"), 16)
            for b in range(4):
                wait_fill_out(sp, ("down2", b))
            sp.dma_start(out.rearrange("b (t p) d -> p (b t) d", p=P), X[:, :, :]).then_inc(sem("out_stored"), 16)
            sp.wait_ge(sem("out_stored"), 16)

        SUMSQ, MEANSQ, RMS, RSTD = [STAT[:, 2 * i:2 * i + 2] for i in range(4)]
        NEGM, RSUM, RREC, ESINK = [STAT[:, 8 + 4 * i:12 + 4 * i].rearrange("p (u t) -> p u t", u=2) for i in range(4)]
        DTT = STAT[:, 24:40]
        NSINK = STAT[:, 40:48]
        EGC = STAT[:, 48:51]
        EALOG = STAT[:, 51:52]
        QKSS = area(22500, 16)
        POSF = area(22516, 2)
        SPX, DECAY, ACUM, FCUM, SPT = [SM8[:, a:b] for a, b in ((0, 512), (512, 768), (768, 1024), (1024, 1280), (1280, 1792))]
        BETA, GCUM, EGCUM, EKEND, GAX, GSPT, GLOG = [SM8[0:RH, a:b] for a, b in (
            (0, 256), (256, 512), (512, 768), (768, 896), (1024, 1280), (1280, 1536), (1536, 1792))]

        @block.tensor
        def _(pe):
            state = {"fill": 0, "job": 0}

            def open_fill(name):
                f = state["fill"]
                assert FILLS[f][0] == name, (FILLS[f], name)
                b = FILLS[f][1]
                if FILL_USES[f]:
                    pe.wait_ge(sem(f"fill_out{b}"), FILL_USES[f])
                return BK[b]

            def close_fill(ins):
                state["fill"] += 1
                ins.then_inc(sem("fills_written"), 1)

            def open_job(job):
                j = state["job"]
                assert JOBS[j] == job, (JOBS[j], job)
                if j >= 4:
                    pe.wait_ge(sem(f"job_out{j % 4}"), j // 4)
                return BK[j % 4]

            def close_job(ins):
                state["job"] += 1
                ins.then_inc(sem("jobs_written"), 1)

            def chunk(kind, i, k, n):
                slot, turn = weight_slots(kind, i)
                pe.wait_ge(sem(f"weights_in{slot}"), 16 * turn)
                return rings[slot][:, 0:k * n].rearrange("p (k n) -> p k n", k=k)

            def product_f(o, w, a, n=P):
                for k in range(KD):
                    ins = pe.matmul(o, w[:, k, a:a + n], HT[:, k, :], start=(k == 0), stop=(k == KD - 1))
                return ins

            def product_t(o, w, tt, a, n, ks=range(KD)):
                for k in ks:
                    ins = pe.matmul(o, HT[:, k, tt * P:(tt + 1) * P], w[:, k, a:a + n],
                                    start=(k == 0), stop=(k == KD - 1))
                return ins

            def norm_transposes(n):
                pe.wait_ge(sem("hn_ready"), 2 * (n + 1))
                for b in range(4):
                    o = open_fill(("norm", n, b))
                    for j in range(2):
                        for tt in range(TT):
                            k = 2 * b + j
                            ins = pe.transpose(o[:, j * S + tt * P:j * S + (tt + 1) * P],
                                               HN[:, tt, k * P:(k + 1) * P], ident)
                    close_fill(ins)
                for b in range(4):
                    wait_fill_out(pe, ("norm", n, b))

            def split_piece(kind, i, j):
                k = PIECE_AT[kind, i, j]
                pe.wait_ge(sem("pieces_split"), k + 1)
                return piece_parts(k)

            def product3(o, left, right, first=True, last=True):
                n = len(left[0])
                for k in range(n):
                    for a, b in ((0, 0), (0, 1), (1, 0)):
                        ins = pe.matmul(o, left[a][k], right[b][k], start=(first and k == 0 and a + b == 0),
                                        stop=(last and k == n - 1 and a == 1))
                return ins

            def f_jobs_split(kind, i):
                for j in range(2):
                    w = split_piece(kind, i, j)
                    o = open_job((kind, i, j))
                    for t in range(2):
                        ins = product3(o[:, t * S:(t + 1) * S],
                                       [[part[:, k, t * P:(t + 1) * P] for k in range(KD)] for part in w],
                                       [[part[:, k, :] for k in range(KD)] for part in (OVER_HT, OVER_HN)])
                    close_job(ins)

            def two_f_jobs(kind, i, tiles=4):
                w = chunk(kind, i, KD, tiles * P)
                for j in range(2):
                    o = open_job((kind, i, j))
                    for t in range(2):
                        if 2 * j + t < tiles:
                            ins = product_f(o[:, t * S:(t + 1) * S], w, (2 * j + t) * P)
                    close_job(ins)

            def two_t_jobs(kind, i):
                w = chunk(kind, i, KD, 512)
                for tt in range(TT):
                    o = open_job((kind, i, tt))
                    close_job(product_t(o[:, :], w, tt, 0, 512))

            pe.wait_ge(sem("consts_in"), 16 * 6)
            o = open_fill(("table",))
            close_fill(pe.matmul(o[0:2 * NH, 0:384], RELB[:, :], tbl("onehot")[0:32, :], start=True, stop=True))

            norm_transposes(0)

            w = chunk("in1", 0, KD, 272)
            o = open_job(("in1", 0, 0))
            product_f(o[:, 0:S], w, 0)
            close_job(product_f(o[0:NH, S:2 * S], w, 256, NH))
            o = open_job(("in1", 0, 1))
            product_f(o[0:NH, 0:S], w, 264, NH)
            for tt in range(TT):
                ins = product_t(o[:, S + tt * P:S + (tt + 1) * P], w, tt, P, P)
            close_job(ins)
            for i in (1, 2, 3):
                two_f_jobs("in1", i)
                if i == 2:
                    pe.wait_ge(sem("dt_ready"), 1)
                    o = open_fill(("dt_T",))
                    for tt in range(TT):
                        ins = pe.matmul(o[:, tt * NH:(tt + 1) * NH], SM8[:, tt * P:(tt + 1) * P],
                                        ident[0:NH, 0:NH], start=True, stop=True)
                    close_fill(ins)
            pe.wait_ge(sem("conv_done"), 8)
            for tt in range(TT):
                o = open_fill(("xs_T", tt))
                for k in range(4):
                    ins = pe.transpose(o[:, k * P:(k + 1) * P], XBC[:, k, tt * P:(tt + 1) * P], ident)
                close_fill(ins)
            for g in range(2):
                o = open_fill(("cb", g))
                pe.matmul(o[:, 0:S], XBC[:, 4 + g, 0:P], XBC[:, 6 + g, :], start=True, stop=True)
                close_fill(pe.matmul(o[:, S:384], XBC[:, 4 + g, P:S], XBC[:, 6 + g, P:S], start=True, stop=True))
            two_f_jobs("in1", 4)
            two_t_jobs("in1", 5)
            two_f_jobs("in1", 6)
            two_f_jobs("in1", 7)
            two_f_jobs("in1", 8)
            two_t_jobs("in1", 9)
            two_t_jobs("in1", 10)

            def row_of(h, n, sign):
                a = ident if sign > 0 else negident[:, :]
                return a[0:NH, h:h + 1].to_broadcast([NH, n])

            def scores(u):
                br, h = ALL_UNITS[u]
                if u >= 2:
                    pe.wait_ge(sem("scores_read"), u - 1)
                o = BK[4 + u % 2]
                if br == 0:
                    a = SM8[:, 768:768 + S]
                    for (c0, c1, s0) in ((0, S, 0), (S, 384, P)):
                        pe.matmul(o[:, c0:c1], row_of(h, P, 1), a[:, s0:S], start=True, stop=False)
                        ins = pe.matmul(o[:, c0:c1], a[:, s0:s0 + P], row_of(h, c1 - c0, -1),
                                        start=False, stop=True)
                    ins.then_inc(sem("scores_written"), 1)
                    return
                pb, t = HD * (h % 2), h // 2
                if br == 4:
                    q, k = QTm[0:QK, h, :], KTm[0:QK, h, :]
                elif br == 3:
                    pb, t = HD * (h // 4), h % 4
                    q, k = DQ1[pb:pb + HD, t, :], DK1[pb:pb + HD, :]
                else:
                    Q, K = (CQ1, CK1) if br == 2 else (BQ1, BK1)
                    q, k = Q[pb:pb + HD, t, :], K[pb:pb + HD, t, :]
                for (c0, c1, q0) in ((0, P, 0), (P, 384, P)):
                    n = c1 - c0
                    ins = pe.matmul(o[:, c0:c1], q[:, q0:q0 + P], k[:, 0:n], start=True, stop=(br != 2))
                    if br == 2:
                        cum = SM8[:, 1024:1280]
                        pe.matmul(o[:, c0:c1], cum[:, q0:q0 + P], row_of(h, n, 1), start=False, stop=False)
                        ins = pe.matmul(o[:, c0:c1], row_of(h, P, -1), cum[:, 0:n], start=False, stop=True)
                ins.then_inc(sem("scores_written"), 1)

            def probs_T(u):
                if ALL_UNITS[u][0] == 0:
                    return
                pe.wait_ge(sem("probs_ready"), u + 1)
                n = attention_units(u)
                if n:
                    pe.wait_ge(sem("probsT_by_act"), n)
                for j in range(3):
                    ins = pe.transpose(BK[6][:, j * P:(j + 1) * P], PB_[:, u % 2, j * P:(j + 1) * P], ident)
                ins.then_inc(sem("probsT_written"), 1)

            def values(u):
                br, h = ALL_UNITS[u]
                if br == 0:
                    pe.wait_ge(sem("mix_by_pool"), u + 1 - attention_units(u + 1))
                else:
                    pe.wait_ge(sem("probsT_by_act"), attention_units(u + 1))
                if u >= 1:
                    pe.wait_ge(sem("heads_done"), u)
                V, a = {0: (XDT, h * HD), 1: (BV1, h * HD), 2: (CV1, h * HD), 3: (DV1, (h // 4) * HD),
                        4: (VM, h * HD)}[br]
                o = BK[7][:, (u % 2) * P:(u % 2 + 1) * P]
                pt = PT_[:, u % 2, :]
                pe.matmul(o[:, 0:HD], pt[:, 0:P], V[:, 0, a:a + HD], start=True, stop=True)
                pe.matmul(o[:, HD:2 * HD], pt[:, P:2 * P], V[:, 0, a:a + HD], start=True, stop=False)
                pe.matmul(o[:, HD:2 * HD], pt[:, 2 * P:3 * P], V[:, 1, a:a + HD], start=False, stop=True)\
                    .then_inc(sem("heads_written"), 1)

            for i in range(5, 11):
                wait_job_out(pe, ("in1", i, 0))
                wait_job_out(pe, ("in1", i, 1))
            for name in (("xs_T", 0), ("xs_T", 1), ("cb", 0), ("cb", 1)):
                wait_fill_out(pe, name)
            pe.wait_ge(sem("rows_ready"), 1)
            for u in range(NU + 1):
                if u < NU:
                    scores(u)
                if u >= 1:
                    probs_T(u - 1)
                if u < NU:
                    g, half = divmod(u, 2)
                    i, tt = divmod(g, 2)
                    w = chunk("gate", i, KD, 512)
                    o = open_job(("gate", i, tt)) if half == 0 else job_bank(("gate", i, tt))
                    ins = product_t(o[:, :], w, tt, 0, 512, range(4 * half, 4 * half + 4))
                    if half:
                        close_job(ins)
                if u >= 1:
                    values(u - 1)

            def branch_T(i):
                if i == 0:
                    pe.wait_ge(sem("ya_ready"), 2)
                    pe.wait_ge(sem("heads_done"), NU)
                for b in range(2):
                    o = open_fill(("y_T", i, b))
                    for j in range(2):
                        for tt in range(TT):
                            k = 2 * b + j
                            ins = pe.transpose(o[:, j * S + tt * P:j * S + (tt + 1) * P],
                                               YB[i][:, tt, k * P:(k + 1) * P], ident)
                    close_fill(ins)

            def branch_product(i):
                wait_fill_out(pe, ("y_T", i, 0))
                wait_fill_out(pe, ("y_T", i, 1))
                for dc in range(2):
                    w = split_piece("branch", i, dc)
                    for tt in range(TT):
                        o = open_job(("branch", i, 2 * dc + tt))
                        close_job(product3(o[:, :], [[part[:, k, tt * P:(tt + 1) * P] for k in range(4)]
                                                     for part in (YT_HIGH[i % 2], YT_LOW[i % 2])],
                                           [[part[:, k, :] for k in range(4)] for part in w]))

            branch_T(0)
            for i in range(4):
                if i < 3:
                    branch_T(i + 1)
                branch_product(i)

            def out_jobs(kind, high, low):
                for dc in range(2):
                    for j in range(2):
                        w = split_piece(kind, dc, j)
                        for tt in range(TT):
                            o = open_job((kind, dc, tt)) if j == 0 else job_bank((kind, dc, tt))
                            state["job"] += (1 if j == 0 and tt == 0 else 0)
                            ins = product3(o[:, j * S:(j + 1) * S],
                                           [[part[:, k, tt * P:(tt + 1) * P] for k in range(KD)] for part in (high, low)],
                                           [[part[:, k, :] for k in range(KD)] for part in w])
                            if j:
                                ins.then_inc(sem("jobs_written"), 1)
                            elif tt:
                                ins.then_inc(sem("first_halves"), 1)
                    state["job"] += 1

            def down(kind, high, low, nk, ready, fills):
                o = [bank_of((fills, b)) for b in range(4)]
                for b in range(4):
                    f = FILL_AT[fills, b]
                    pe.wait_ge(sem(f"fill_out{FILLS[f][1]}"), FILL_USES[f])
                for c in range(nk // 2):
                    w = split_piece(kind, c // 2, c % 2)
                    for k in range(2):
                        t = 2 * c + k
                        ready(t)
                        for tt in range(TT):
                            for dc in range(2):
                                ins = product3(o[2 * tt + dc][:, :],
                                               [[part[:, t, tt * P:(tt + 1) * P]] for part in (high, low)],
                                               [[part[:, k, dc * 512:(dc + 1) * 512]] for part in w],
                                               first=(t == 0), last=(t == nk - 1))
                                if t == nk - 1:
                                    close_fill(ins)
                    if t < nk - 1:
                        ins.then_inc(sem(kind + "_pieces_read"), 1)

            pe.wait_ge(sem("mixed_ready"), 1)
            for b in range(4):
                o = open_fill(("mix_T", b))
                for j in range(2):
                    for tt in range(TT):
                        k = 2 * b + j
                        ins = pe.transpose(o[:, j * S + tt * P:j * S + (tt + 1) * P],
                                           HN[:, tt, k * P:(k + 1) * P], ident)
                close_fill(ins)
            for b in range(4):
                wait_fill_out(pe, ("mix_T", b))
            out_jobs("out1", OVER_HT, OVER_HN)

            norm_transposes(1)
            for i in range(FF1_CHUNKS):
                f_jobs_split("ffn1", i)
            down("down1", HID1_HIGH, HID1_LOW, FF1_KT, lambda t: pe.wait_ge(sem("hidden_split"), t // 2 + 1), "down1")

            norm_transposes(2)
            w = chunk("in2", 0, KD, 416)
            o = open_job(("in2", 0, 0))
            for t in range(2):
                ins = product_f(o[:, t * S:(t + 1) * S], w, t * P)
            close_job(ins)
            o = open_job(("in2", 0, 1))
            product_f(o[:, 0:S], w, 2 * P)
            for tt in range(TT):
                ins = product_t(o[:, S + tt * ROPE:S + (tt + 1) * ROPE], w, tt, 3 * P, ROPE)
            close_job(ins)
            two_f_jobs("in2", 1)

            wait_job_out(pe, ("in2", 0, 0))
            wait_job_out(pe, ("in2", 0, 1))
            o = open_fill(("mla_ss",))
            for t in range(2):
                pe.matmul(o[:, 0:S], ones[:, 0:P], SQM[:, t, :], start=(t == 0), stop=(t == 1))
            close_fill(pe.matmul(o[:, S:2 * S], ones[:, 0:P], SQM[:, 2, :], start=True, stop=True))
            two_f_jobs("in2", 2)
            pe.wait_ge(sem("latents_ready"), 1)
            for tt in range(TT):
                o = open_fill(("mla_q", tt))
                for t in range(2):
                    ins = pe.matmul(o[:, 0:MH * QK], CQF[:, t, tt * P:(tt + 1) * P],
                                    prm2("uq", t * 384, 384), start=(t == 0), stop=(t == 1))
                close_fill(ins)
            for tt in range(TT):
                o = open_fill(("mla_kv", tt))
                close_fill(pe.matmul(o[:, :], CQF[:, 2, tt * P:(tt + 1) * P], prm2("ukv", 0, 512),
                                     start=True, stop=True))
            w = chunk("in2", 3, KD, 396)
            o = open_job(("in2", 3, 0))
            for t in range(2):
                ins = product_f(o[:, t * S:(t + 1) * S], w, t * P)
            close_job(ins)
            close_job(product_f(open_job(("in2", 3, 1))[:, 0:S], w, 2 * P))
            o = open_job(("in2", 3, 2))
            for t in range(2):
                ins = product_f(o[0:RH, t * S:(t + 1) * S], w, 384 + RH * t, RH)
            close_job(ins)
            two_f_jobs("in2", 4)
            pe.wait_ge(sem("mla_qk_ready"), 1)
            for n, src in enumerate((QM, KM)):
                for b in range(2):
                    o = open_fill(("mla_T", 2 * n + b))
                    for j in range(2):
                        for tt in range(TT):
                            ins = pe.transpose(o[0:QK, j * S + tt * P:j * S + (tt + 1) * P],
                                               src[:, tt * MH + 2 * b + j, :], ident)
                    close_fill(ins)
            two_f_jobs("in2", 5)
            for b in range(4):
                wait_fill_out(pe, ("mla_T", b))
            for u in range(NU, NU + MH + 1):
                if u < NU + MH:
                    scores(u)
                if u > NU:
                    probs_T(u - 1)
                    values(u - 1)
            two_f_jobs("in2", 6)
            pe.wait_ge(sem("heads_done"), NU + MH)
            o = open_fill(("yM_T",))
            for j in range(2):
                for tt in range(TT):
                    ins = pe.transpose(o[:, j * S + tt * P:j * S + (tt + 1) * P],
                                       YM[:, tt, j * P:(j + 1) * P], ident)
            close_fill(ins)
            for j in range(JOB_AT["out2", 0, 0] - 4, JOB_AT["out2", 0, 0]):
                wait_job_out(pe, JOBS[j])

            def tile_slots(names):
                for name, tiles in zip(names, ((0, 1), (2,))):
                    o = open_fill(name)
                    for n, t in enumerate(tiles):
                        yield o[:, n * S:(n + 1) * S], t, t == tiles[-1]

            pe.wait_ge(sem("lora_by_act"), 1)
            for n, (pb, tiles) in enumerate(((0, (0, 1)), (0, (2,)), (HD, (0, 1)), (HD, (2,)))):
                o = open_fill(("lora", n))
                for j, t in enumerate(tiles):
                    ins = pe.matmul(o[:, j * S:(j + 1) * S], prm2("w2a2", t * P, P)[pb:pb + HD, :],
                                    LO[pb:pb + HD, 0, :], start=True, stop=True)
                close_fill(ins)
            pe.wait_ge(sem("lora_by_dve"), 1)
            for o, t, last in tile_slots([("rw_g", 0), ("rw_g", 1)]):
                ins = pe.matmul(o, prm2("g2", t * P, P), LO[:, 1, :], start=True, stop=True)
                if last:
                    close_fill(ins)

            def head_sums(names, src, ready, count):
                pe.wait_ge(sem(ready), count)
                for o, t, last in tile_slots(names):
                    ins = pe.matmul(o, prm2("blockones", 0, P), src[:, t, :], start=True, stop=True)
                    if last:
                        close_fill(ins)

            head_sums([("kk_ss", 0), ("kk_ss", 1)], T3, "rw_squares", 1)
            head_sums([("bonus", 0), ("bonus", 1)], T3, "rw_squares", 2)
            pe.wait_ge(sem("rw_factors"), 1)
            for name, src in ((("b_T",), A3), (("k_T",), K3)):
                o = open_fill(name)
                for t in range(3):
                    ins = pe.transpose(o[:, t * P:(t + 1) * P], src[:, t, 0:P], ident)
                close_fill(ins)
            for c in range(2):
                o = open_fill(("v_T", c))
                for t in range(3):
                    ins = pe.transpose(o[:, t * P:(t + 1) * P], V3[:, t, c * P:(c + 1) * P], ident)
                close_fill(ins)

            def pairs(name_of, size=4):
                for g in range(NM // size):
                    o = open_fill(name_of(g))
                    for n in range(size):
                        m, c, h = PLACES[size * g + n]
                        yield o[:, n * P:(n + 1) * P], m, c, h, n == size - 1

            for kind, s_src, t_src in (("aab", A3, KK), ("aak", K3, KK), ("mrb", A3, R3), ("mrk", K3, R3)):
                for o, m, c, h, last in pairs(lambda g: (kind, g), 3):
                    pb, t, c0 = HD * (h % 2), h // 2, c * P
                    a, b = s_src[pb:pb + HD, t, :], t_src[pb:pb + HD, t, :]
                    pe.matmul(o[:, HD:P], a[:, c0:c0 + P], b[:, c0 + HD:c0 + P], start=True, stop=True)
                    ins = pe.matmul(o[0:HD, 0:HD], a[:, c0:c0 + HD], b[:, c0:c0 + HD], start=True, stop=True)
                    if last:
                        close_fill(ins)
            for g in range(4):
                wait_fill_out(pe, ("aak", g))
            for c in range(2):
                wait_fill_out(pe, ("v_T", c))
            for c in range(2):
                o = open_fill(("av", c))
                for h in range(RH):
                    ins = pe.matmul(o[:, h * HD:(h + 1) * HD], PM[:, matrix(c, h), :], VT[:, c, h * HD:(h + 1) * HD],
                                    start=True, stop=True)
                close_fill(ins)

            def product(name, left, right, needs):
                for g in range(3):
                    for need in needs(g):
                        wait_fill_out(pe, need)
                    o = open_fill(name(g))
                    for n in range(4):
                        m = 4 * g + n
                        ins = pe.matmul(o[:, n * P:(n + 1) * P], left[:, m, :], right[:, m, :],
                                        start=True, stop=True)
                    close_fill(ins)

            def inverse(fam):
                pe.wait_ge(sem("inverse_started"), 1 if fam == "rw" else 2)
                for o, m, c, h, last in pairs(lambda g: (fam, "t0", g)):
                    ins = pe.transpose(o, TTM[:, m, :], ident)
                    if last:
                        close_fill(ins)
                for lv in range(1, LEVELS):
                    product(lambda g: (fam, "p", lv, g), AT, TM,
                            lambda g: [(fam, "t0", g) if lv == 1 else (fam, "t", lv - 1, g)])
                    before = lambda g: [(fam, "p", lv, g)] + ([(fam, "tt", lv - 1, g)] if lv > 1 else [])
                    if lv < LEVELS - 1:
                        product(lambda g: (fam, "t", lv, g), TTM, PM, before)
                    product(lambda g: (fam, "tt", lv, g), PM, TTM, before)
                for g in range(3):
                    wait_fill_out(pe, (fam, "tt", LEVELS - 1, g))

            def solve(name, rhs, c):
                o = open_fill(name)
                for h in range(RH):
                    ins = pe.matmul(o[:, h * HD:(h + 1) * HD], TTM[:, matrix(c, h), :],
                                    rhs[:, c, h * HD:(h + 1) * HD], start=True, stop=True)
                close_fill(ins)

            def place(h):
                return HD * (h % 2), h // 2

            inverse("rw")
            wait_fill_out(pe, ("av", 0))
            solve(("sa", 0), RR, 0)
            wait_fill_out(pe, ("sa", 0))
            wait_fill_out(pe, ("b_T",))
            wait_fill_out(pe, ("k_T",))
            o = open_fill(("st",))
            for h in range(RH):
                pb, t = place(h)
                cols = slice(h * HD, (h + 1) * HD)
                so = o[pb:pb + HD, t * HD:(t + 1) * HD]
                pe.matmul(so, BTk[:, cols], SA[:, 0, cols], start=True, stop=False)
                ins = pe.matmul(so, KTk[:, cols], VT[:, 0, cols], start=False, stop=True)
            close_fill(ins)
            wait_fill_out(pe, ("st",))
            for par in range(2):
                o = open_fill(("r1", par))
                for h in range(par, RH, 2):
                    pb, t = place(h)
                    ins = pe.matmul(o[:, t * HD:(t + 1) * HD], KK[pb:pb + HD, t, P:S], ST[pb:pb + HD, t, :],
                                    start=True, stop=True)
                close_fill(ins)
            wait_fill_out(pe, ("r1", 0))
            wait_fill_out(pe, ("r1", 1))
            solve(("sa", 1), RR, 1)
            wait_fill_out(pe, ("sa", 1))
            for g in range(4):
                wait_fill_out(pe, ("mrk", g))

            def outputs(names, parts, state_q, state):
                for o, t, last in tile_slots(names):
                    for h in (2 * t, 2 * t + 1):
                        pb = HD * (h % 2)
                        for c in range(2):
                            mms = [(a[:, c, h * HD:(h + 1) * HD], b[:, matrix(c, h), :]) for a, b in parts]
                            if c:
                                mms.append((state[pb:pb + HD, t, :], state_q(t)[pb:pb + HD, :]))
                            for n, (a, b) in enumerate(mms):
                                ins = pe.matmul(o[pb:pb + HD, c * P:(c + 1) * P], a, b,
                                                start=(n == 0), stop=(n == len(mms) - 1))
                    if last:
                        close_fill(ins)

            outputs([("y", 0), ("y", 1)], [(SA, MB), (VT, MK)], lambda t: R3[:, t, P:S], ST)
            wait_fill_out(pe, ("y", 0))
            wait_fill_out(pe, ("y", 1))
            head_sums([("gn_mean", 0), ("gn_mean", 1)], E3, "rw_squares", 2)
            head_sums([("gn_var", 0), ("gn_var", 1)], T3, "rw_squares", 3)

            head_sums([("gq_ss", 0), ("gq_ss", 1)], GKB, "gdn_squares", 1)
            head_sums([("gk_ss", 0), ("gk_ss", 1)], GKB, "gdn_squares", 2)
            pe.wait_ge(sem("gdn_rows"), 1)

            def pair_rows(t):
                return prm2("pair_rows", t * P, P)[0:RH, :]

            for o, t, last in tile_slots([("beta", 0), ("beta", 1)]):
                ins = pe.matmul(o, pair_rows(t), SM8[0:RH, 0:S], start=True, stop=True)
                if last:
                    close_fill(ins)
            for name, a in ((("g_e",), 512 + P), (("g_k",), 768)):
                o = open_fill(name)
                for t in range(3):
                    ins = pe.matmul(o[:, t * P:(t + 1) * P], pair_rows(t), SM8[0:RH, a:a + P],
                                    start=True, stop=True)
                close_fill(ins)
            wait_fill_out(pe, ("g_k",))
            for c in range(2):
                o = open_fill(("gv_T", c))
                for t in range(3):
                    ins = pe.transpose(o[:, t * P:(t + 1) * P], GV[:, t, c * P:(c + 1) * P], ident)
                close_fill(ins)
            o = open_fill(("gk_T",))
            for t in range(3):
                ins = pe.transpose(o[:, t * P:(t + 1) * P], GKD[:, t, :], ident)
            close_fill(ins)
            for o, m, c, h, last in pairs(lambda g: ("decay", g)):
                rows = SM8[0:RH, S + c * P:S + (c + 1) * P]
                pe.matmul(o, row_of(h, P, 1)[0:RH], rows, start=True, stop=False)
                ins = pe.matmul(o, rows, row_of(h, P, -1)[0:RH], start=False, stop=True)
                if last:
                    close_fill(ins)
            for kind, t_src in (("gkk", GKB), ("gqk", GQ)):
                for o, m, c, h, last in pairs(lambda g: (kind, g), 3):
                    pb, t = place(h)
                    ins = pe.matmul(o, GK[pb:pb + HD, t, c * P:(c + 1) * P], t_src[pb:pb + HD, t, c * P:(c + 1) * P],
                                    start=True, stop=True)
                    if last:
                        close_fill(ins)
            inverse("gd")
            for name in (("gv_T", 0), ("gv_T", 1), ("gk_T",)):
                wait_fill_out(pe, name)
            solve(("du", 0), GVT, 0)
            wait_fill_out(pe, ("du", 0))
            o = open_fill(("gst",))
            for h in range(RH):
                pb, t = place(h)
                cols = slice(h * HD, (h + 1) * HD)
                ins = pe.matmul(o[pb:pb + HD, t * HD:(t + 1) * HD], GKT[:, cols], SA[:, 0, cols],
                                start=True, stop=True)
            close_fill(ins)
            wait_fill_out(pe, ("gst",))
            for par in range(2):
                o = open_fill(("gr1", par))
                for h in range(par, RH, 2):
                    pb, t = place(h)
                    ins = pe.matmul(o[:, t * HD:(t + 1) * HD], GKE[pb:pb + HD, t, :], ST[pb:pb + HD, t, :],
                                    start=True, stop=True)
                close_fill(ins)
            wait_fill_out(pe, ("gr1", 0))
            wait_fill_out(pe, ("gr1", 1))
            solve(("du", 1), GVT, 1)
            wait_fill_out(pe, ("du", 1))
            for g in range(4):
                wait_fill_out(pe, ("gqk", g))
            outputs([("o", 0), ("o", 1)], [(SA, GAT)], lambda t: GQD[:, t, :], ST)
            head_sums([("o_ss", 0), ("o_ss", 1)], GQ, "gdn_squares", 3)

            wait_fill_out(pe, ("yM_T",))
            pe.wait_ge(sem("y2_split"), 1)
            for b in range(4):
                pe.wait_ge(sem(f"fill_out{b}"), FILL_USES[FILL_AT["norm", 3, b]])
            out_jobs("out2", OVER_HN, OVER_HT)
            norm_transposes(3)
            for i in range(FF2_CHUNKS):
                f_jobs_split("ffn2", i)
            down("down2", HID2_HIGH, HID2_LOW, FF2_KT,
                 lambda t: pe.wait_ge(sem("hidden_split"), FF1_CHUNKS + t // 2 + 1), "down2")

        def conv_weights(n):
            if n < 8:
                return [prm("conv_w", 8 * tap + n) for tap in range(4)], prm("conv_b", n)
            return [prm2("g_conv", 9 * tap + n - 8) for tap in range(4)], 0.0

        def conv_tile(n):
            if n < 8:
                return ("in1", 1 + n // 4, (n % 4) // 2), n % 2, XBC[:, n, :]
            m = n - 8
            return ("in2", 4 + m // 4, (m % 4) // 2), m % 2, GZ[:, m, :]

        STAGED = {job: n for n, job in enumerate(
            [("in1", i, j) for i in (1, 2) for j in range(2)]
            + [("in2", 1, 0), ("in2", 1, 1), ("in2", 2, 0), ("in2", 2, 1), ("in2", 3, 0), ("in2", 3, 1)]
            + [("in2", 4, 0), ("in2", 4, 1), ("in2", 5, 0), ("in2", 5, 1), ("in2", 6, 0)])}

        @block.scalar
        def _(act):
            act.dma_start(X[:, :, :], x.rearrange("b (t p) d -> p (b t) d", p=P)).then_inc(sem("x_in"), 16)
            act.dma_start(CST[:, :], consts).then_inc(sem("consts_in"), 16)
            act.dma_start(TBL, tables).then_inc(sem("consts_in"), 16)
            act.dma_start(PRM[:, :], params).then_inc(sem("consts_in"), 16)
            act.dma_start(RELB[:, :], rel_bias).then_inc(sem("consts_in"), 16)
            act.dma_start(NF[:, :], norm_final).then_inc(sem("consts_in"), 16)
            act.dma_start(POS[:, :], positions).then_inc(sem("consts_in"), 16)

            def root(n, src, dst, ready, done):
                act.wait_ge(sem(ready), n)
                act.activation(dst, src, ACT.Sqrt).then_inc(sem(done), 1)

            def norm_stats(m):
                if m == 0:
                    act.wait_ge(sem("x_in"), 16)
                elif m in (1, 4):
                    for j in range(4):
                        wait_job_out(act, ("out1" if m == 1 else "out2", j // 2, j % 2))
                elif m == 2:
                    for b in range(4):
                        wait_fill_out(act, ("down1", b))
                else:
                    act.wait_ge(sem("x2_ready"), 2)
                for tt in range(TT):
                    act.activation(HN[:, tt, :], X[:, tt, :], ACT.Square, accum_out=SUMSQ[:, tt:tt + 1])\
                        .then_inc(sem("sums_ready"), 1)
                root(m + 1, MEANSQ, RMS, "means_ready", "roots_ready")

            def split_high(k):
                if k >= len(PIECES):
                    return
                kind, i, _ = PIECES[k]
                slot, turn = weight_slots(kind, i)
                act.wait_ge(sem(f"weights_in{slot}"), 16 * turn)
                if k >= 2:
                    wait_piece_used(act, k - 2)
                act.activation(piece_parts(k)[0], piece_source(k), ACT.Copy).then_inc(sem("pieces_high"), 1)

            def norm_gains(n):
                gain = [prm("norm_mix", 0, 8), prm("norm_ffn", 0, 8), prm("ln_mix", 0, 8), prm("ln_ffn", 0, 8)][n]
                for b in range(4) if n in (1, 3) else (0, 2):
                    o = fill_arrived(act, ("norm", n, b))
                    if n in (1, 3):
                        for j in range(2):
                            k = 2 * b + j
                            ins = act.activation(OVER_HT[:, k, :], o[:, j * S:(j + 1) * S], ACT.Copy,
                                                 scale=gain[:, k:k + 1])
                        ins.then_inc(sem("operand_high"), 1)
                        continue
                    for j in range(2):
                        k = 2 * b + j
                        ins = act.activation(HT[:, k, :], o[:, j * S:(j + 1) * S], ACT.Copy, scale=gain[:, k:k + 1])
                    fill_out(ins, ("norm", n, b))

            def stage(job, reader):
                o = job_arrived(act, job)
                n = len(stage_readers)
                if n >= 2:
                    act.wait_ge(sem(stage_readers[n - 2][0]), stage_readers[n - 2][1])
                stage_readers.append(reader)
                act.activation(STG[:, n % 2, :], o[:, :], ACT.Copy)
                return o

            stage_readers = []

            def conv_tap(n, release=True):
                job, half, _ = conv_tile(n)
                w, bias = conv_weights(n)
                o = stage(job, ("conv_sum", min(n + 2, 17))) if half == 0 else job_bank(job)
                if n >= 2:
                    act.wait_ge(sem("conv_done"), n - 1)
                src = o[:, half * S:(half + 1) * S]
                if n < 8:
                    ins = act.activation(ACC[:, n % 2, :], src, ACT.Identity, bias=bias, scale=w[3])
                else:
                    ins = act.activation(ACC[:, n % 2, :], src, ACT.Copy, scale=w[3])
                ins.then_inc(sem("conv_tap"), 1)
                if half and release:
                    act.wait_ge(sem("conv_tap"), n + 1)
                    act.sem_inc(sem(f"job_out{JOB_AT[job] % 4}"), 1)

            def conv_tanh(n):
                act.wait_ge(sem("conv_sum"), n + 1)
                act.activation(TH[:, n % 2, :], ACC[:, n % 2, :], ACT.Tanh).then_inc(sem("conv_tanh"), 1)

            def convs(first, last):
                for n in range(first, last):
                    conv_tap(n)
                    if n > first:
                        conv_tanh(n - 1)
                conv_tanh(last - 1)

            def take(job, dst, scale=1.0):
                o = job_arrived(act, job)
                job_out(act.activation(dst, o[:, :], ACT.Copy, scale=scale), job)

            def take_fill(name, dst, n, scale=1.0, rows=P):
                o = fill_arrived(act, name)
                fill_out(act.activation(dst, o[0:rows, 0:n], ACT.Copy, scale=scale), name)

            def flat(t):
                return t.rearrange("p a b -> p (a b)")

            def softplus_parts(k, t):
                act.wait_ge(sem("sp_minus_abs"), k + 1)
                act.activation(t, t, ACT.Exp).then_inc(sem("sp_exp"), 1)
                act.wait_ge(sem("sp_exp1"), k + 1)
                act.activation(t, t, ACT.Ln).then_inc(sem("sp_ln"), 1)

            norm_stats(0)
            norm_gains(0)
            act.wait_ge(sem("params_halved"), 1)
            softplus_parts(0, SPT)
            act.activation(EALOG[0:NH, :], prm("a_log")[0:NH, :], ACT.Exp).then_inc(sem("a_ready"), 1)
            convs(0, 8)
            take(("in1", 3, 0), flat(CQ1[:, 0:2, :]), 0.125)
            for g in range(2):
                take_fill(("cb", g), CB[:, g, :], 384)
            take(("in1", 4, 0), flat(CK1[:, 0:2, :]))
            take(("in1", 5, 0), CV1[:, 0, :])
            take(("in1", 6, 0), flat(DQ1[:, 0:2, :]), 0.125)
            take(("in1", 7, 0), flat(BQ1[:, 0:2, :]), 0.125)
            take(("in1", 8, 0), flat(BK1[:, 0:2, :]))
            take(("in1", 9, 0), BV1[:, 0, :])
            for tt in range(TT):
                o = job_arrived(act, ("in1", 10, tt))
                act.activation(SILZ[:, tt, :], o[:, :], ACT.Tanh, scale=0.5).then_inc(sem("z_tanh"), 1)

            def exps(u):
                br, h = ALL_UNITS[u]
                act.wait_ge(sem("scores_read"), u + 1)
                if u >= 2:
                    if ALL_UNITS[u - 2][0] == 0:
                        act.wait_ge(sem("mix_by_pool"), u - 1 - attention_units(u - 1))
                    else:
                        act.wait_ge(sem("probsT_written"), attention_units(u - 1))
                    act.wait_ge(sem("heads_done"), u - 1)
                s, p = SB_[:, u % 2, :], PB_[:, u % 2, :]
                if br == 0:
                    act.activation(p, s, ACT.Exp).then_inc(sem("probs_ready"), 1)
                    return
                if br == 3:
                    act.activation(ESINK[:, u % 2, :], NEGM[:, u % 2, :], ACT.Exp, bias=prm("sinks", h))
                for tt, (c0, c1) in enumerate(((0, P), (P, 384))):
                    ins = act.activation(p[:, c0:c1], s[:, c0:c1], ACT.Exp, bias=NEGM[:, u % 2, tt:tt + 1],
                                         scale=-1.0, accum_out=RSUM[:, u % 2, tt:tt + 1])
                ins.then_inc(sem("probs_ready"), 1)

            def take_probs_T(u):
                if ALL_UNITS[u][0] == 0:
                    return
                act.wait_ge(sem("probsT_written"), attention_units(u + 1))
                if u >= 2:
                    act.wait_ge(sem("heads_written"), u - 1)
                act.activation(PT_[:, u % 2, :], BK[6][:, 0:384], ACT.Copy).then_inc(sem("probsT_by_act"), 1)

            act.wait_ge(sem("table_stored"), 16)
            for u in range(NU + 1):
                if u < NU:
                    exps(u)
                if u >= 1:
                    take_probs_T(u - 1)
                if u < NU and u % 2:
                    i, tt = divmod(u // 2, 2)
                    o = job_arrived(act, ("gate", i, tt))
                    job_out(act.activation(GT[:, tt, i * 512:(i + 1) * 512], o[:, :], ACT.Tanh, scale=0.5),
                            ("gate", i, tt))
            act.dma_start(P2[:, 0:NP2], params2).then_inc(sem("params2_in"), 16)

            for tt in range(TT):
                act.wait_ge(sem("ya_gated"), 1)
                if tt == 0:
                    split_high(0)
                    split_high(1)
                act.activation(STG[:, tt, :], YB[0][:, tt, :], ACT.Square,
                               accum_out=SUMSQ[:, tt:tt + 1]).then_inc(sem("ya_sums"), 1)
            root(1, MEANSQ, RMS, "ya_means", "ya_roots")

            def take_y_T(i):
                for b in range(2):
                    o = fill_arrived(act, ("y_T", i, b))
                    if i >= 2:
                        job_arrived(act, ("branch", i - 2, 3))
                    for j in range(2):
                        ins = act.activation(YT_HIGH[i % 2][:, 2 * b + j, :], o[:, j * S:(j + 1) * S], ACT.Copy,
                                             scale=prm("ssm_norm", 2 * b + j) if i == 0 else 1.0)
                    ins.then_inc(sem("y_high"), 1)

            take_y_T(0)
            take_y_T(1)
            for i in range(4):
                split_high(2 * i + 2)
                split_high(2 * i + 3)
                if i < 2:
                    take_y_T(i + 2)
            for b in range(4):
                o = fill_arrived(act, ("mix_T", b))
                act.activation(flat(OVER_HT[:, 2 * b:2 * b + 2, :]), o[:, :], ACT.Copy)\
                    .then_inc(sem("operand_high"), 1)
            out1 = PIECE_AT["out1", 0, 0]
            for k in range(out1 + 2, out1 + 5):
                split_high(k)
            norm_stats(1)
            split_high(out1 + 5)
            norm_gains(1)
            for c in range(FF1_CHUNKS):
                k = PIECE_AT["ffn1", c, 0]
                split_high(k + 2)
                o = job_arrived(act, ("ffn1", c, 0))
                if c >= 2:
                    wait_job_out(act, ("ffn1", c - 2, 1))
                act.activation(SG[:, c % 2, :], o[:, :], ACT.Tanh, scale=0.5).then_inc(sem("ffn_tanh"), 1)
                split_high(k + 3)
                act.wait_ge(sem("hidden_ready"), c + 1)
                act.activation(flat(HID1_HIGH[:, 2 * c:2 * c + 2, :]), HF1[:, c % 2, :], ACT.Copy)\
                    .then_inc(sem("hidden_high"), 1)
            for k in range(PIECE_AT["down1", 0, 0] + 2, PIECE_AT["out2", 0, 0]):
                split_high(k)
            norm_stats(2)
            norm_stats(3)
            norm_gains(2)

            o = job_arrived(act, ("in2", 0, 0))
            act.activation(flat(CQF[:, 0:2, :]), o[:, :], ACT.Copy)
            job_out(act.activation(flat(SQM[:, 0:2, :]), o[:, :], ACT.Square), ("in2", 0, 0))
            o = job_arrived(act, ("in2", 0, 1))
            act.activation(CQF[:, 2, :], o[:, 0:S], ACT.Copy)
            act.activation(SQM[:, 2, :], o[:, 0:S], ACT.Square)
            job_out(act.activation(flat(KR), o[:, S:S + TT * ROPE], ACT.Copy), ("in2", 0, 1))

            def shift_tiles(i, j, tiles):
                shifts[0] += 1
                o = job_arrived(act, ("in2", i, j))
                k = len(stage_readers)
                act.wait_ge(sem(stage_readers[k - 2][0]), stage_readers[k - 2][1])
                stage_readers.append(("shift_by_dve", shifts[0]))
                n = len(tiles) * S
                act.activation(STG[:, k % 2, 0:n], o[:, 0:n], ACT.Copy)
                for n, rt in enumerate(tiles):
                    ins = act.activation(RZ[:, rt, :], o[:, n * S:(n + 1) * S], ACT.Copy, scale=one_minus_mu[:, rt:rt + 1])
                job_out(ins, ("in2", i, j))

            shifts = [0]

            act.wait_ge(sem("params2_ready"), 1)
            act.wait_ge(sem("angles_ready"), 1)
            act.activation(SIN[:, :, :], SIN[:, :, :], ACT.Sin)
            act.activation(COS[:, :, :], COS[:, :, :], ACT.Sin).then_inc(sem("sincos_ready"), 1)
            act.activation(EALOG[0:RH, :], prm2("g_alog")[0:RH, :], ACT.Exp).then_inc(sem("a_ready"), 1)
            shift_tiles(1, 0, (0, 1))
            shift_tiles(1, 1, (2, 3))
            root(1, SQM[:, :, :], SQM[:, :, :], "latent_means", "latent_roots")
            shift_tiles(2, 0, (4, 5))
            shift_tiles(2, 1, (6, 7))
            for tt in range(TT):
                take_fill(("mla_q", tt), flat(QM[:, tt * MH:(tt + 1) * MH, :]), MH * QK)
            shift_tiles(3, 0, (8, 9))
            shift_tiles(3, 1, (10,))
            root(1, QKSS, QKSS, "qk_means", "qk_roots")
            act.wait_ge(sem("shift_by_dve"), 1)
            act.activation(LO[0:HD, 0, :], LO[0:HD, 0, :], ACT.Tanh)
            act.activation(LO[:, 1, :], LO[:, 1, :], ACT.Tanh, scale=0.5).then_inc(sem("lora_by_act"), 1)
            convs(8, 12)
            for n, dst in enumerate((QTm, KTm)):
                for b in range(2):
                    take_fill(("mla_T", 2 * n + b), flat(dst[0:QK, 2 * b:2 * b + 2, :]), 512, rows=QK)
            convs(12, 16)
            for u in range(NU, NU + MH + 1):
                if u < NU + MH:
                    exps(u)
                if u > NU:
                    take_probs_T(u - 1)
            conv_tap(16)
            conv_tanh(16)
            o = job_arrived(act, ("in2", 6, 0))
            act.activation(GGT[:, 0, :], o[:, S:2 * S], ACT.Tanh, scale=0.5).then_inc(sem("gg_tanh"), 1)
            o = job_arrived(act, ("in2", 6, 1))
            act.activation(flat(GGT[:, 1:3, :]), o[:, :], ACT.Tanh, scale=0.5).then_inc(sem("gg_tanh"), 1)
            take_fill(("yM_T",), flat(YT2[:, 3:5, :]), 512)
            act.wait_ge(sem("beta_in"), 1)
            act.activation(BETA, BETA, ACT.Tanh, scale=0.5).then_inc(sem("beta_tanh"), 1)
            softplus_parts(1, GSPT)
            act.wait_ge(sem("gdn_cumulated"), 1)
            act.activation(EGCUM, GCUM, ACT.Exp)
            act.activation(EKEND, GCUM[:, 0:P], ACT.Exp, bias=GCUM[:, P - 1:P], scale=-1.0)\
                .then_inc(sem("gdn_rows"), 1)

            for n, (dst, bias, tiles) in enumerate(((LW, "w0", (0, 1)), (LW, "w0", (2,)), (A3, "a0", (0, 1)), (A3, "a0", (2,)))):
                o = fill_arrived(act, ("lora", n))
                for j, t in enumerate(tiles):
                    ins = act.activation(dst[:, t, :], o[:, j * S:(j + 1) * S], ACT.Tanh, scale=0.5, bias=prm2(bias, t))
                fill_out(ins, ("lora", n))
            take_fill(("rw_g", 0), flat(GG[:, 0:2, :]), 512, 0.5)
            take_fill(("rw_g", 1), GG[:, 2, :], S, 0.5)
            act.wait_ge(sem("decay_sums"), 1)
            act.activation(EGC, G3[:, :, P + HD - 1], ACT.Exp)
            act.activation(E3[:, :, :], E3[:, :, :], ACT.Exp).then_inc(sem("decay_exp"), 1)
            root(1, T3[:, :, :], T3[:, :, :], "rw_means", "rw_roots")
            act.wait_ge(sem("alpha_ready"), 1)
            act.activation(E3[:, :, :], GM[:, :, :], ACT.Exp, scale=-1.0).then_inc(sem("decay_exp"), 1)
            act.wait_ge(sem("decay_exp"), 2)
            act.activation(GM[:, :, :], GM[:, :, :], ACT.Exp).then_inc(sem("decay_exp"), 1)
            take_fill(("b_T",), BTk, 384)
            take_fill(("k_T",), KTk, 384)
            for c in range(2):
                take_fill(("v_T", c), VT[:, c, :], 384)

            def take_t0(fam):
                for g in range(3):
                    take_fill((fam, "t0", g), flat(TM[:, 4 * g:4 * g + 4, :]), 512)

            take_t0("rw")
            take_fill(("sa", 0), SA[:, 0, :], 384)
            take_fill(("sa", 1), SA[:, 1, :], 384)
            take_fill(("y", 0), flat(E3[:, 0:2, :]), 512)
            take_fill(("y", 1), E3[:, 2, :], S)
            root(2, T3[:, :, :], T3[:, :, :], "rw_means", "rw_roots")
            root(1, GTMP[:, :, :], GTMP[:, :, :], "gdn_means", "gdn_roots")
            root(2, GTMP[:, :, :], GTMP[:, :, :], "gdn_means", "gdn_roots")
            for c in range(2):
                take_fill(("gv_T", c), GVT[:, c, :], 384)
            take_fill(("gk_T",), GKT, 384)
            for g in range(3):
                wait_fill_out(act, ("decay", g))
                m = GAT[:, 4 * g:4 * g + 4, :]
                act.activation(m, m, ACT.Exp).then_inc(sem("gdn_decay_exp"), 1)
            take_t0("gd")
            act.wait_ge(sem("y2_ready"), 1)
            out2 = PIECE_AT["out2", 0, 0]
            split_high(out2)
            split_high(out2 + 1)
            wait_fill_out(act, ("yM_T",))
            act.activation(OVER_HN[:, 0:5, :], YT2[:, 0:5, :], ACT.Copy).then_inc(sem("y2_high"), 1)
            take_fill(("du", 0), SA[:, 0, :], 384)
            take_fill(("du", 1), SA[:, 1, :], 384)
            take_fill(("o", 0), flat(GKB[:, 0:2, :]), 512)
            take_fill(("o", 1), GKB[:, 2, :], S)
            root(3, GTMP[:, :, :], GTMP[:, :, :], "gdn_means", "gdn_roots")

            act.wait_ge(sem("y2_ready"), 2)
            act.activation(OVER_HN[:, 5:8, :], YT2[:, 5:8, :], ACT.Copy).then_inc(sem("y2_high"), 1)
            for k in range(out2 + 2, out2 + 5):
                split_high(k)
            norm_stats(4)
            split_high(out2 + 5)
            norm_gains(3)

            def hidden2_high(q):
                act.wait_ge(sem("hidden_ready"), FF1_CHUNKS + q + 1)
                act.activation(flat(HID2_HIGH[:, 2 * q:2 * q + 2, :]), HF2[:, q % 2, :], ACT.Copy)\
                    .then_inc(sem("hidden_high"), 1)

            for q in range(2 * FF2_CHUNKS):
                c, j = divmod(q, 2)
                split_high(PIECE_AT["ffn2", c, j] + 2)
                o = job_arrived(act, ("ffn2", c, j))
                if q >= 2:
                    act.wait_ge(sem("hidden_split"), FF1_CHUNKS + q - 1)
                job_out(act.activation(HF2[:, q % 2, :], o[:, :], ACT.Relu), ("ffn2", c, j))
                if q:
                    hidden2_high(q - 1)
            hidden2_high(q)
            for k in range(PIECE_AT["down2", 0, 0] + 2, len(PIECES)):
                split_high(k)

        @block.vector
        def _(dve):
            steps = [0]

            def link(ins):
                steps[0] += 1
                ins.then_inc(sem("dve_steps"), 1)
                dve.wait_ge(sem("dve_steps"), steps[0])

            def bc(ap, shape):
                return ap.to_broadcast(shape)

            def flat(t):
                return t.rearrange("p a b -> p (a b)")

            def norm_scale(m):
                dve.wait_ge(sem("sums_ready"), 2 * (m + 1))
                dve.tensor_scalar(MEANSQ, SUMSQ, 1.0 / D, EPS, ALU.mult, ALU.add).then_inc(sem("means_ready"), 1)
                dve.wait_ge(sem("roots_ready"), m + 1)
                link(dve.reciprocal(RSTD, RMS))
                for tt in range(TT):
                    if m == 2:
                        dve.scalar_tensor_tensor(out=X[:, tt, :], in0=X[:, tt, :], scalar=RSTD[:, tt:tt + 1],
                                                 in1=NF[:, :], op0=ALU.mult, op1=ALU.mult).then_inc(sem("x2_ready"), 1)
                    else:
                        dve.tensor_scalar(HN[:, tt, :], X[:, tt, :], RSTD[:, tt:tt + 1], None, ALU.mult)\
                            .then_inc(sem("hn_ready"), 1)

            operand_parts = [0]

            def operand_high_arrived():
                operand_parts[0] += 1
                dve.wait_ge(sem("operand_high"), operand_parts[0])

            def split_low(k):
                if k >= len(PIECES):
                    return
                dve.wait_ge(sem("pieces_high"), k + 1)
                high, low = piece_parts(k)
                dve.tensor_tensor(low, piece_source(k), high.bitcast(F32), ALU.subtract)\
                    .then_inc(sem("pieces_split"), 1)

            def norm_gains(n):
                gain = [prm("norm_mix", 0, 8), prm("norm_ffn", 0, 8), prm("ln_mix", 0, 8), prm("ln_ffn", 0, 8)][n]
                if n in (1, 3):
                    fill_arrived(dve, ("norm", n, 3))
                for b in range(4) if n in (1, 3) else (1, 3):
                    o = fill_arrived(dve, ("norm", n, b))
                    if n in (1, 3):
                        operand_high_arrived()
                        for j in range(2):
                            k = 2 * b + j
                            ins = dve.scalar_tensor_tensor(out=OVER_HN[:, k, :], in0=o[:, j * S:(j + 1) * S],
                                                           scalar=gain[:, k:k + 1], in1=OVER_HT[:, k, :].bitcast(F32),
                                                           op0=ALU.mult, op1=ALU.subtract)
                        fill_out(ins, ("norm", n, b))
                        continue
                    for j in range(2):
                        k = 2 * b + j
                        ins = dve.tensor_scalar(HT[:, k, :], o[:, j * S:(j + 1) * S], gain[:, k:k + 1], None, ALU.mult)
                    fill_out(ins, ("norm", n, b))

            def take(job, dst, scale=1.0):
                o = job_arrived(dve, job)
                job_out(dve.tensor_scalar(dst, o[:, :], scale, None, ALU.mult), job)

            def softplus(k, src, t, dst):
                dve.scalar_tensor_tensor(out=t, in0=src, scalar=-1.0, in1=src, op0=ALU.mult, op1=ALU.min)\
                    .then_inc(sem("sp_minus_abs"), 1)
                dve.wait_ge(sem("sp_exp"), k + 1)
                dve.tensor_scalar(t, t, 1.0, None, ALU.add).then_inc(sem("sp_exp1"), 1)
                dve.wait_ge(sem("sp_ln"), k + 1)
                link(dve.scalar_tensor_tensor(out=dst, in0=src, scalar=0.0, in1=t, op0=ALU.max, op1=ALU.add))

            def conv_taps(n):
                job, half, _ = conv_tile(n)
                w, _ = conv_weights(n)
                dve.wait_ge(sem("conv_tap"), n + 1)
                o = STG[:, STAGED[job] % 2, half * S:(half + 1) * S]
                for tap in (2, 1, 0):
                    d = 3 - tap
                    a = ACC[:, n % 2, d:S]
                    ins = dve.scalar_tensor_tensor(out=a, in0=o[:, 0:S - d], scalar=w[tap], in1=a,
                                                   op0=ALU.mult, op1=ALU.add)
                    if tap:
                        link(ins)
                ins.then_inc(sem("conv_sum"), 1)

            def conv_out(n):
                dve.wait_ge(sem("conv_tanh"), n + 1)
                dve.scalar_tensor_tensor(out=conv_tile(n)[2], in0=TH[:, n % 2, :], scalar=1.0, in1=ACC[:, n % 2, :],
                                         op0=ALU.add, op1=ALU.mult).then_inc(sem("conv_done"), 1)

            def convs(first, last):
                for n in range(first, last):
                    conv_taps(n)
                    if n > first:
                        conv_out(n - 1)
                conv_out(last - 1)

            dve.wait_ge(sem("consts_in"), 16 * 6)
            dve.tensor_scalar(prm("conv_w", 0, 32), prm("conv_w", 0, 32), 0.5, None, ALU.mult)
            dve.tensor_scalar(prm("conv_b", 0, 8), prm("conv_b", 0, 8), 0.5, None, ALU.mult)
            dve.tensor_scalar(NSINK, prm("sinks", 0, 8), -1.0, None, ALU.mult)
            link(dve.tensor_scalar(negident[:, :], ident, -1.0, None, ALU.mult))
            o = fill_arrived(dve, ("table",))
            fill_out(dve.tensor_tensor(PT_[0:2 * NH, 0, :], o[0:2 * NH, 0:384], tbl("table_mask")[0:2 * NH, :],
                                       ALU.add), ("table",))
            norm_scale(0)
            norm_gains(0)
            o = job_arrived(dve, ("in1", 0, 0))
            dve.tensor_copy(DK1, o[:, 0:S])
            job_out(dve.tensor_scalar(SPX[:, 0:S], o[0:NH, S:2 * S], prm("dt_bias")[0:NH, :], None, ALU.add),
                    ("in1", 0, 0))
            o = job_arrived(dve, ("in1", 0, 1))
            dve.tensor_copy(DV1[:, :, :], o[:, S:2 * S].rearrange("p (t w) -> p t w", t=TT))
            job_out(dve.tensor_scalar(SPX[:, S:2 * S], o[0:NH, 0:S], prm("forget_bias")[0:NH, :], -1.0, ALU.add,
                                      ALU.mult), ("in1", 0, 1))
            wait_job_out(dve, ("in1", 0, 0))
            wait_job_out(dve, ("in1", 0, 1))
            dve.sem_inc(sem("params_halved"), 1)
            softplus(0, SPX, SPT, SPX)
            dve.wait_ge(sem("a_ready"), 1)
            dve.tensor_scalar(DECAY, SPX[:, 0:S], EALOG[0:NH, :], -1.0, ALU.mult, ALU.mult).then_inc(sem("dt_ready"), 1)
            dve.wait_ge(sem("dt_ready"), 1)
            dve.tensor_tensor_scan(ACUM, ones[0:NH, :], DECAY, 0.0, ALU.mult, ALU.add)
            dve.tensor_tensor_scan(FCUM, ones[0:NH, :], SPX[:, S:2 * S], 0.0, ALU.mult, ALU.subtract)\
                .then_inc(sem("rows_ready"), 1)
            convs(0, 8)
            o = fill_arrived(dve, ("dt_T",))
            fill_out(dve.tensor_copy(DTT, o[:, 0:TT * NH]), ("dt_T",))
            take(("in1", 3, 1), flat(CQ1[:, 2:4, :]), 0.125)
            wait_fill_out(dve, ("dt_T",))
            for tt in range(TT):
                o = fill_arrived(dve, ("xs_T", tt))
                src = o[:, :].rearrange("p (h w) -> p h w", h=NH)
                dst = [t[:, tt, :].rearrange("p (h w) -> p h w", h=NH) for t in (XDT, YB[0])]
                dve.tensor_tensor(dst[0], src, bc(DTT[:, tt * NH:(tt + 1) * NH].unsqueeze(2), [P, NH, HD]), ALU.mult)
                fill_out(dve.tensor_tensor(dst[1], src, bc(prm("d_skip", 0, NH).unsqueeze(2), [P, NH, HD]), ALU.mult),
                         ("xs_T", tt))
            take(("in1", 4, 1), flat(CK1[:, 2:4, :]))
            take(("in1", 5, 1), CV1[:, 1, :])
            take(("in1", 6, 1), flat(DQ1[:, 2:4, :]), 0.125)
            take(("in1", 7, 1), flat(BQ1[:, 2:4, :]), 0.125)
            take(("in1", 8, 1), flat(BK1[:, 2:4, :]))
            take(("in1", 9, 1), BV1[:, 1, :])
            for tt in range(TT):
                dve.wait_ge(sem("z_tanh"), tt + 1)
                o = job_bank(("in1", 10, tt))
                job_out(dve.scalar_tensor_tensor(out=SILZ[:, tt, :], in0=SILZ[:, tt, :], scalar=1.0, in1=o[:, :],
                                                 op0=ALU.add, op1=ALU.mult), ("in1", 10, tt))

            def bias_scores(u):
                br, h = ALL_UNITS[u]
                dve.wait_ge(sem("scores_written"), u + 1)
                if u >= 2:
                    dve.wait_ge(sem("probs_ready"), u - 1)
                o, s = BK[4 + u % 2], SB_[:, u % 2, :]
                if br == 0:
                    dve.tensor_tensor(s, o[:, 0:384], cst("ssd_mask"), ALU.add).then_inc(sem("scores_read"), 1)
                    return
                m = {1: BIAS[:, h, :], 2: cst("causal"), 3: BIAS[:, NH + h, :], 4: cst("mla_mask")}[br]
                init = NSINK[:, h:h + 1] if br == 3 else 3e38
                dve.tensor_tensor_reduce(s[:, 0:P], o[:, 0:P], m[:, P:S], -1.0, init, ALU.add, ALU.min,
                                         NEGM[:, u % 2, 0:1])
                dve.tensor_tensor_reduce(s[:, P:384], o[:, P:384], m, -1.0, init, ALU.add, ALU.min,
                                         NEGM[:, u % 2, 1:2]).then_inc(sem("scores_read"), 1)

            def finish_head(u):
                br, h = ALL_UNITS[u]
                dve.wait_ge(sem("heads_written"), u + 1)
                o = BK[7][:, (u % 2) * P:(u % 2 + 1) * P].rearrange("p (t w) -> p t w", t=TT)
                y = (YM if br == 4 else YB[br])[:, :, h * HD:(h + 1) * HD]
                if br == 0:
                    dve.tensor_tensor(y, o, y, ALU.add).then_inc(sem("heads_done"), 1)
                    return
                if br == 3:
                    link(dve.tensor_tensor(RSUM[:, u % 2, :], RSUM[:, u % 2, :], ESINK[:, u % 2, :], ALU.add))
                link(dve.reciprocal(RREC[:, u % 2, :], RSUM[:, u % 2, :]))
                dve.tensor_tensor(y, o, bc(RREC[:, u % 2, :].unsqueeze(2), [P, TT, HD]), ALU.mult)\
                    .then_inc(sem("heads_done"), 1)

            for u in range(NU + 1):
                if u == 16:
                    dve.wait_ge(sem("bias_in"), 16)
                if u < NU:
                    bias_scores(u)
                if u >= 1:
                    finish_head(u - 1)

            dve.tensor_scalar(SPT[:, 0:1], SPT[:, 0:1], 1.0, None, ALU.mult)
            dve.wait_ge(sem("heads_done"), NU)
            dve.scalar_tensor_tensor(out=flat(YB[0]), in0=flat(YB[0]), scalar=0.5, in1=flat(SILZ), op0=ALU.mult,
                                     op1=ALU.mult).then_inc(sem("ya_gated"), 1)
            split_low(0)
            dve.wait_ge(sem("ya_sums"), 2)
            dve.tensor_scalar(MEANSQ, SUMSQ, 1.0 / BW, EPS, ALU.mult, ALU.add).then_inc(sem("ya_means"), 1)
            dve.wait_ge(sem("ya_roots"), 1)
            link(dve.reciprocal(RSTD, RMS))
            for tt in range(TT):
                dve.tensor_scalar(YB[0][:, tt, :], YB[0][:, tt, :], RSTD[:, tt:tt + 1], None, ALU.mult)\
                    .then_inc(sem("ya_ready"), 1)

            def take_y_T(i):
                for b in range(2):
                    o = fill_arrived(dve, ("y_T", i, b))
                    dve.wait_ge(sem("y_high"), 2 * i + b + 1)
                    for j in range(2):
                        k = 2 * b + j
                        ins = dve.scalar_tensor_tensor(out=YT_LOW[i % 2][:, k, :], in0=o[:, j * S:(j + 1) * S],
                                                       scalar=prm("ssm_norm", k) if i == 0 else 1.0,
                                                       in1=YT_HIGH[i % 2][:, k, :].bitcast(F32),
                                                       op0=ALU.mult, op1=ALU.subtract)
                    fill_out(ins, ("y_T", i, b))

            take_y_T(0)
            split_low(1)
            take_y_T(1)
            for i in range(4):
                for j in range(4):
                    dc, tt = divmod(j, 2)
                    job = ("branch", i, j)
                    if tt:
                        split_low(2 * i + 2 + dc)
                    o = job_arrived(dve, job)
                    g = GT[:, tt, i * D + dc * 512:i * D + (dc + 1) * 512]
                    mix = HN[:, tt, dc * 512:(dc + 1) * 512]
                    job_out(dve.scalar_tensor_tensor(out=TMP if i else mix, in0=g, scalar=1.0, in1=o[:, :],
                                                     op0=ALU.add, op1=ALU.mult), job)
                    if i:
                        wait_job_out(dve, job)
                        ins = dve.tensor_tensor(mix, mix, TMP, ALU.add)
                        if (i, j) == (3, 3):
                            ins.then_inc(sem("mixed_ready"), 1)
                        else:
                            link(ins)
                if i < 2:
                    take_y_T(i + 2)
            fill_arrived(dve, ("mix_T", 3))
            for b in range(4):
                operand_high_arrived()
                fill_out(dve.tensor_tensor(flat(OVER_HN[:, 2 * b:2 * b + 2, :]), bank_of(("mix_T", b))[:, :],
                                           flat(OVER_HT[:, 2 * b:2 * b + 2, :]).bitcast(F32), ALU.subtract), ("mix_T", b))

            def add_to_x(o, tt, dc, scale):
                xs = X[:, tt, dc * 512:(dc + 1) * 512]
                return dve.scalar_tensor_tensor(out=xs, in0=o[:, :], scalar=scale, in1=xs, op0=ALU.mult, op1=ALU.add)

            def add_out(kind, scale):
                for dc in range(2):
                    split_low(PIECE_AT[kind, dc, 0] + 2)
                    if dc == 0:
                        split_low(PIECE_AT[kind, dc, 1] + 2)
                    for tt in range(TT):
                        o = job_arrived(dve, (kind, dc, tt))
                        job_out(add_to_x(o, tt, dc, scale), (kind, dc, tt))

            def add_down(kind, scale):
                for b in range(4):
                    o = fill_arrived(dve, (kind, b))
                    fill_out(add_to_x(o, b // 2, b % 2, scale), (kind, b))

            add_out("out1", 0.5)
            norm_scale(1)
            split_low(PIECE_AT["ffn1", 0, 1])
            norm_gains(1)

            def hidden_low(high, low, tiles, src, n):
                dve.wait_ge(sem("hidden_high"), n + 1)
                dve.tensor_tensor(flat(low[:, tiles, :]), src, flat(high[:, tiles, :]).bitcast(F32), ALU.subtract)\
                    .then_inc(sem("hidden_split"), 1)

            def hidden1_low(c):
                hidden_low(HID1_HIGH, HID1_LOW, slice(2 * c, 2 * c + 2), HF1[:, c % 2, :], c)

            for c in range(FF1_CHUNKS):
                split_low(PIECE_AT["ffn1", c, 0] + 2)
                dve.wait_ge(sem("ffn_tanh"), c + 1)
                sg = SG[:, c % 2, :]
                job_out(dve.scalar_tensor_tensor(out=sg, in0=sg, scalar=1.0, in1=job_bank(("ffn1", c, 0))[:, :],
                                                 op0=ALU.add, op1=ALU.mult), ("ffn1", c, 0))
                if c:
                    hidden1_low(c - 1)
                wait_job_out(dve, ("ffn1", c, 0))
                o = job_arrived(dve, ("ffn1", c, 1))
                dve.tensor_tensor(HF1[:, c % 2, :], sg, o[:, :], ALU.mult).then_inc(sem("hidden_ready"), 1)
                dve.wait_ge(sem("hidden_ready"), c + 1)
                dve.sem_inc(sem(f"job_out{JOB_AT['ffn1', c, 1] % 4}"), 1)
                split_low(PIECE_AT["ffn1", c, 0] + 3)
            hidden1_low(c)
            for k in range(PIECE_AT["down1", 0, 0] + 2, PIECE_AT["out2", 0, 0]):
                split_low(k)
            add_down("down1", 0.5)
            norm_scale(2)
            norm_scale(3)
            norm_gains(2)

            dve.wait_ge(sem("params2_in"), 16)
            for name, n, f in (("w0", 3, 0.5), ("a0", 3, 0.5), ("g_conv", 36, 0.5), ("o_norm", 1, 0.5),
                               ("q_qk", QK, QK ** -0.5)):
                link(dve.tensor_scalar(prm2(name, 0, n), prm2(name, 0, n), f, None, ALU.mult))
            dve.tensor_scalar(one_minus_mu[:, :], prm2("mu", 0, 11), -1.0, 1.0, ALU.mult, ALU.add)\
                .then_inc(sem("params2_ready"), 1)
            link(dve.tensor_copy(POSF, POS[:, :]))
            for tt in range(TT):
                link(dve.tensor_scalar(SIN[:, tt, :], prm2("inv_freq", 0, 16), POSF[:, tt:tt + 1], None, ALU.mult))
            turns, ang = flat(COS), flat(SIN)
            link(dve.tensor_scalar(turns, ang, 0.15915494309189535, ROUND, ALU.mult, ALU.add))
            link(dve.tensor_scalar(turns, turns, -ROUND, None, ALU.add))
            for part in (TWO_PI_A, TWO_PI_B, TWO_PI_C):
                link(dve.scalar_tensor_tensor(out=ang, in0=turns, scalar=-part, in1=ang, op0=ALU.mult, op1=ALU.add))
            link(dve.tensor_scalar(ang, ang, 3.1415925, -3.1415925, ALU.min, ALU.max))
            link(dve.scalar_tensor_tensor(out=turns, in0=ang, scalar=-1.0, in1=ang, op0=ALU.mult, op1=ALU.max))
            dve.tensor_scalar(turns, turns, -1.0, 1.5707963267948966, ALU.mult, ALU.add)\
                .then_inc(sem("angles_ready"), 1)

            def shift_tiles(i, j, tiles):
                wait_job_out(dve, ("in2", i, j))
                o = STG[:, STAGED["in2", i, j] % 2, :]
                for n, rt in enumerate(tiles):
                    z = RZ[:, rt, 1:S]
                    ins = dve.scalar_tensor_tensor(out=z, in0=o[:, n * S:(n + 1) * S - 1], scalar=prm2("mu", rt), in1=z,
                                                   op0=ALU.mult, op1=ALU.add)
                ins.then_inc(sem("shift_by_dve"), 1)

            shift_tiles(1, 0, (0, 1))
            shift_tiles(1, 1, (2, 3))
            o = fill_arrived(dve, ("mla_ss",))
            dve.tensor_scalar(SQM[:, 0, :], o[:, 0:S], 1.0 / 256, EPS, ALU.mult, ALU.add)
            link(dve.tensor_scalar(SQM[:, 2, :], o[:, S:2 * S], 1.0 / 128, EPS, ALU.mult, ALU.add))
            fill_out(dve.tensor_copy(SQM[:, 1, :], SQM[:, 0, :]), ("mla_ss",))
            wait_fill_out(dve, ("mla_ss",))
            dve.sem_inc(sem("latent_means"), 1)
            dve.wait_ge(sem("latent_roots"), 1)
            link(dve.reciprocal(SQM[:, :, :], SQM[:, :, :]))
            for t, gain in enumerate((prm2("q_norm", 0), prm2("q_norm", 1), prm2("kv_norm"))):
                ins = dve.scalar_tensor_tensor(out=CQF[:, t, :], in0=CQF[:, t, :], scalar=gain, in1=SQM[:, t, :],
                                               op0=ALU.mult, op1=ALU.mult)
            ins.then_inc(sem("latents_ready"), 1)
            shift_tiles(2, 0, (4, 5))
            shift_tiles(2, 1, (6, 7))
            for tt in range(TT):
                o = fill_arrived(dve, ("mla_kv", tt))
                kv = o[:, :].rearrange("p (h w) -> p h w", h=MH)
                dve.tensor_copy(KM[:, tt * MH:(tt + 1) * MH, 0:NOPE], kv[:, :, 0:NOPE])
                fill_out(dve.tensor_copy(VM[:, tt, :].rearrange("p (h w) -> p h w", h=MH), kv[:, :, NOPE:2 * NOPE]),
                         ("mla_kv", tt))
            wait_fill_out(dve, ("mla_kv", 0))
            wait_fill_out(dve, ("mla_kv", 1))
            shift_tiles(3, 0, (8, 9))
            shift_tiles(3, 1, (10,))
            o = job_arrived(dve, ("in2", 3, 2))
            dve.tensor_scalar(GAX, o[0:RH, S:2 * S], prm2("g_dtb")[0:RH, :], None, ALU.add)
            job_out(dve.tensor_copy(BETA, o[0:RH, 0:S]), ("in2", 3, 2))
            wait_job_out(dve, ("in2", 3, 2))
            dve.sem_inc(sem("beta_in"), 1)
            wait_fill_out(dve, ("mla_q", 0))
            wait_fill_out(dve, ("mla_q", 1))
            dve.wait_ge(sem("key_rope_by_pool"), 2)
            for n, m in enumerate((QM, KM)):
                link(dve.tensor_tensor(SQQ[:, :, :], m[:, :, :], m[:, :, :], ALU.mult))
                link(dve.tensor_reduce(QKSS[:, 8 * n:8 * n + 8], SQQ[:, :, :], AX_X, ALU.add))
            dve.tensor_scalar(QKSS, QKSS, 1.0 / QK, EPS, ALU.mult, ALU.add).then_inc(sem("qk_means"), 1)
            dve.wait_ge(sem("qk_roots"), 1)
            link(dve.reciprocal(QKSS, QKSS))
            dve.wait_ge(sem("sincos_ready"), 1)
            for n, (m, gain) in enumerate(((QM, "q_qk"), (KM, "k_qk"))):
                link(dve.tensor_tensor(m[:, :, :], m[:, :, :], bc(QKSS[:, 8 * n:8 * n + 8].unsqueeze(2), [P, 8, QK]),
                                       ALU.mult))
                link(dve.tensor_tensor(m[:, :, :], m[:, :, :], bc(prm2(gain, 0, QK).unsqueeze(1), [P, 8, QK]),
                                       ALU.mult))
                for tt in range(TT):
                    mt = m[:, tt * MH:(tt + 1) * MH, :]
                    c = bc(COS[:, tt, :].unsqueeze(1), [P, MH, 16])
                    s = bc(SIN[:, tt, :].unsqueeze(1), [P, MH, 16])
                    a, b = mt[:, :, NOPE:NOPE + 16], mt[:, :, NOPE + 16:QK]
                    r = [ROT[:, i, 0:64].rearrange("p (h w) -> p h w", h=MH) for i in range(4)]
                    dve.tensor_tensor(r[0], a, c, ALU.mult)
                    dve.tensor_tensor(r[1], b, s, ALU.mult)
                    dve.tensor_tensor(r[2], a, s, ALU.mult)
                    link(dve.tensor_tensor(r[3], b, c, ALU.mult))
                    dve.tensor_tensor(a, r[0], r[1], ALU.subtract)
                    link(dve.tensor_tensor(b, r[2], r[3], ALU.add))
            dve.sem_inc(sem("mla_qk_ready"), 1)
            dve.wait_ge(sem("lora_by_act"), 1)
            dve.tensor_scalar(LO[:, 1, :], LO[:, 1, :], 1.0, None, ALU.add).then_inc(sem("lora_by_dve"), 1)
            convs(8, 12)
            convs(12, 16)
            for u in range(NU, NU + MH + 1):
                if u < NU + MH:
                    bias_scores(u)
                if u > NU:
                    finish_head(u - 1)
            conv_taps(16)
            conv_out(16)
            dve.wait_ge(sem("gg_tanh"), 1)
            job_out(dve.scalar_tensor_tensor(out=GGT[:, 0, :], in0=GGT[:, 0, :], scalar=1.0,
                                             in1=job_bank(("in2", 6, 0))[:, S:2 * S], op0=ALU.add, op1=ALU.mult),
                    ("in2", 6, 0))
            dve.wait_ge(sem("gg_tanh"), 2)
            job_out(dve.scalar_tensor_tensor(out=flat(GGT[:, 1:3, :]), in0=flat(GGT[:, 1:3, :]), scalar=1.0,
                                             in1=job_bank(("in2", 6, 1))[:, :], op0=ALU.add, op1=ALU.mult),
                    ("in2", 6, 1))
            dve.wait_ge(sem("beta_tanh"), 1)
            link(dve.tensor_scalar(BETA, BETA, 0.5, 0.5, ALU.mult, ALU.add))
            softplus(1, GAX, GSPT, GAX)
            dve.wait_ge(sem("a_ready"), 2)
            link(dve.tensor_scalar(GLOG, GAX, EALOG[0:RH, :], -1.0, ALU.mult, ALU.mult))
            for c in range(2):
                ins = dve.tensor_tensor_scan(GCUM[:, c * P:(c + 1) * P], ones[0:RH, 0:P], GLOG[:, c * P:(c + 1) * P],
                                             0.0, ALU.mult, ALU.add)
            ins.then_inc(sem("gdn_cumulated"), 1)

            for n in range(4):
                wait_fill_out(dve, ("lora", n))
            link(dve.tensor_scalar(LW[:, :, :], LW[:, :, :], -0.5 * E_HALF, -0.5 * E_HALF, ALU.mult, ALU.add))
            link(dve.tensor_scalar(A3[:, :, :], A3[:, :, :], 0.5, 0.5, ALU.mult, ALU.add))
            for t in range(3):
                for c in range(2):
                    ins = dve.tensor_tensor_scan(G3[:, t, c * P:(c + 1) * P], ones[:, 0:P],
                                                 LW[:, t, c * P:(c + 1) * P], 0.0, ALU.mult, ALU.add)
            link(ins)
            g4 = flat(G3).rearrange("p (m w) -> p m w", m=6)
            link(dve.tensor_tensor(flat(GM).rearrange("p (m w) -> p m w", m=6), g4,
                                   bc(g4[:, :, HD - 1:HD], [P, 6, P]), ALU.subtract))
            dve.tensor_tensor(E3[:, :, :], GM[:, :, :], LW[:, :, :], ALU.subtract).then_inc(sem("decay_sums"), 1)

            def squares(m, dst, name):
                dve.tensor_tensor(dst[:, :, :], m[:, :, :], m[:, :, :], ALU.mult).then_inc(sem(name), 1)

            def means(names, dst, scale, eps, done):
                for name, a, b in zip(names, (0, 2), (2, 3)):
                    o = fill_arrived(dve, name)
                    ins = dve.tensor_scalar(flat(dst[:, a:b, :]), o[:, 0:(b - a) * S], scale, eps, ALU.mult, ALU.add)
                    fill_out(ins, name)
                    wait_fill_out(dve, name)
                dve.sem_inc(sem(done), 1)

            for t in range(3):
                ins = dve.tensor_scalar(KK[:, t, :], K3[:, t, :], prm2("k_k", t), None, ALU.mult)
            link(ins)
            squares(KK, T3, "rw_squares")
            means([("kk_ss", 0), ("kk_ss", 1)], T3, 1.0, 1e-6, "rw_means")
            dve.wait_ge(sem("rw_roots"), 1)
            link(dve.reciprocal(T3[:, :, :], T3[:, :, :]))
            link(dve.tensor_tensor(KK[:, :, :], KK[:, :, :], T3[:, :, :], ALU.mult))
            for t in range(3):
                ins = dve.tensor_scalar(T3[:, t, :], A3[:, t, :], -1.0, prm2("k_a", t), ALU.add, ALU.mult)
            link(ins)
            link(dve.scalar_tensor_tensor(out=flat(K3), in0=flat(T3), scalar=1.0, in1=flat(K3), op0=ALU.add,
                                          op1=ALU.mult))
            dve.tensor_tensor(A3[:, :, :], KK[:, :, :], A3[:, :, :], ALU.mult)
            for t in range(3):
                ins = dve.scalar_tensor_tensor(out=T3[:, t, :], in0=R3[:, t, :], scalar=prm2("r_k", t), in1=K3[:, t, :],
                                               op0=ALU.mult, op1=ALU.mult)
            ins.then_inc(sem("rw_squares"), 1)
            dve.wait_ge(sem("decay_exp"), 1)
            dve.tensor_tensor(KK[:, :, :], KK[:, :, :], E3[:, :, :], ALU.mult).then_inc(sem("alpha_ready"), 1)
            for name, a, b in ((("bonus", 0), 0, 2), (("bonus", 1), 2, 3)):
                o = fill_arrived(dve, name)
                fill_out(dve.tensor_tensor(flat(BON[:, a:b, :]), o[:, 0:(b - a) * S], flat(V3[:, a:b, :]), ALU.mult),
                         name)
            dve.wait_ge(sem("decay_exp"), 3)
            dve.tensor_tensor(A3[:, :, :], A3[:, :, :], E3[:, :, :], ALU.mult)
            dve.tensor_tensor(K3[:, :, :], K3[:, :, :], E3[:, :, :], ALU.mult)
            dve.tensor_tensor(R3[:, :, :], R3[:, :, :], GM[:, :, :], ALU.mult).then_inc(sem("rw_factors"), 1)

            dve.wait_ge(sem("mats_zeroed"), 4)

            def four(o):
                return o[:, :].rearrange("p (m w) -> p m w", m=4)

            def threes(t, g):
                return t[:, 3 * g:3 * g + 3, :]

            def three(o):
                return o[:, 0:384].rearrange("p (t w) -> p t w", t=3)

            for kind, dst, mask in (("aab", AT, "strict"), ("aak", PM, "strict"), ("mrb", MB, "incl"),
                                    ("mrk", MK, "incl")):
                mk = prm2(mask, 0, P)
                for g in range(4):
                    o = three(fill_arrived(dve, (kind, g)))
                    d = threes(dst, g)
                    dve.tensor_tensor(d[:, :, HD:P], o[:, :, HD:P], bc(mk[:, HD:P].unsqueeze(1), [P, 3, HD]), ALU.mult)
                    fill_out(dve.tensor_tensor(d[0:HD, :, 0:HD], o[0:HD, :, 0:HD],
                                               bc(mk[0:HD, 0:HD].unsqueeze(1), [HD, 3, HD]), ALU.mult), (kind, g))
            for c in range(2):
                o = fill_arrived(dve, ("av", c))
                fill_out(dve.tensor_scalar(RR[:, c, :], o[:, 0:384], -1.0, None, ALU.mult), ("av", c))

            def level_mask(lv):
                return prm2("levels", lv * P, P)

            def inverse(fam):
                link(dve.tensor_tensor(TTM[:, :, :], AT[:, :, :], bc(level_mask(0).unsqueeze(1), [P, NM, P]), ALU.mult))
                dve.scalar_tensor_tensor(out=TTM[:, :, :], in0=TTM[:, :, :], scalar=-1.0,
                                         in1=bc(ident.unsqueeze(1), [P, NM, P]), op0=ALU.mult, op1=ALU.add)\
                    .then_inc(sem("inverse_started"), 1)
                for lv in range(1, LEVELS):
                    for g in range(3):
                        o = fill_arrived(dve, (fam, "p", lv, g))
                        fill_out(dve.tensor_tensor(PM[:, 4 * g:4 * g + 4, :], four(o),
                                                   bc(level_mask(lv).unsqueeze(1), [P, 4, P]), ALU.mult),
                                 (fam, "p", lv, g))
                    for part, t in (("t", TM), ("tt", TTM)):
                        if part == "t" and lv == LEVELS - 1:
                            continue
                        for g in range(3):
                            o = fill_arrived(dve, (fam, part, lv, g))
                            m = flat(t[:, 4 * g:4 * g + 4, :])
                            fill_out(dve.tensor_tensor(m, m, o[:, :], ALU.subtract), (fam, part, lv, g))

            dve.wait_ge(sem("dve_steps"), steps[0])
            for g in range(4):
                wait_fill_out(dve, ("aab", g))
            inverse("rw")
            dve.wait_ge(sem("decay_exp"), 3)
            o = fill_arrived(dve, ("st",))
            for t in range(3):
                ins = dve.tensor_scalar(ST[:, t, :], o[:, t * HD:(t + 1) * HD], GM[:, t, P - 1:P], EGC[:, t:t + 1],
                                        ALU.mult, ALU.mult)
            fill_out(ins, ("st",))
            wait_fill_out(dve, ("av", 1))

            def subtract_state(name, rhs):
                for par in range(2):
                    o = fill_arrived(dve, (name, par))
                    r = rhs[:, 1, :].rearrange("p (t q w) -> p q t w", q=2, w=HD)[:, par]
                    src = o[:, 0:3 * HD].rearrange("p (t w) -> p t w", t=3)
                    fill_out(dve.tensor_tensor(r, r, src, ALU.subtract), (name, par))

            subtract_state("r1", RR)
            for name, a, b in ((("gn_mean", 0), 0, 2), (("gn_mean", 1), 2, 3)):
                o = fill_arrived(dve, name)
                e = flat(E3[:, a:b, :])
                fill_out(dve.scalar_tensor_tensor(out=e, in0=o[:, 0:(b - a) * S], scalar=-1.0 / HD, in1=e,
                                                  op0=ALU.mult, op1=ALU.add), name)
                wait_fill_out(dve, name)
            squares(E3, T3, "rw_squares")
            means([("gn_var", 0), ("gn_var", 1)], T3, 1.0 / HD, 64e-5, "rw_means")
            dve.wait_ge(sem("rw_roots"), 2)
            link(dve.reciprocal(T3[:, :, :], T3[:, :, :]))
            link(dve.tensor_tensor(E3[:, :, :], E3[:, :, :], T3[:, :, :], ALU.mult))
            for t in range(3):
                ins = dve.tensor_scalar(E3[:, t, :], E3[:, t, :], prm2("gn_g", t), prm2("gn_b", t), ALU.mult, ALU.add)
            link(ins)
            link(dve.tensor_tensor(E3[:, :, :], E3[:, :, :], BON[:, :, :], ALU.add))
            dve.tensor_tensor(YT2[:, 0:3, :], E3[:, :, :], GG[:, :, :], ALU.mult).then_inc(sem("y2_ready"), 1)

            for n, (m, scale, names) in enumerate(((GQ, HD ** -0.5, [("gq_ss", 0), ("gq_ss", 1)]),
                                                   (GK, 1.0, [("gk_ss", 0), ("gk_ss", 1)]))):
                squares(m, GKB, "gdn_squares")
                means(names, GTMP, 1.0, 1e-6, "gdn_means")
                dve.wait_ge(sem("gdn_roots"), n + 1)
                link(dve.reciprocal(GTMP[:, :, :], GTMP[:, :, :]))
                link(dve.scalar_tensor_tensor(out=flat(m), in0=flat(m), scalar=scale, in1=flat(GTMP), op0=ALU.mult,
                                              op1=ALU.mult))
            for name, a, b in ((("beta", 0), 0, 2), (("beta", 1), 2, 3)):
                o = fill_arrived(dve, name)
                src = o[:, 0:(b - a) * S]
                dve.tensor_tensor(flat(GKB[:, a:b, :]), src, flat(GK[:, a:b, :]), ALU.mult)
                fill_out(dve.tensor_tensor(flat(GV[:, a:b, :]), src, flat(GV[:, a:b, :]), ALU.mult), name)
                wait_fill_out(dve, name)

            o = three(fill_arrived(dve, ("g_e",)))
            dve.tensor_tensor(GKE[:, :, :], o, GKB[:, :, P:S], ALU.mult)
            fill_out(dve.tensor_tensor(GQD[:, :, :], o, GQ[:, :, P:S], ALU.mult), ("g_e",))
            o = three(fill_arrived(dve, ("g_k",)))
            fill_out(dve.tensor_tensor(GKD[:, :, :], o, GK[:, :, 0:P], ALU.mult), ("g_k",))
            for g in range(3):
                o = fill_arrived(dve, ("decay", g))
                fill_out(dve.tensor_tensor(GAT[:, 4 * g:4 * g + 4, :], four(o),
                                           bc(cst("ssd_mask")[:, 0:P].unsqueeze(1), [P, 4, P]), ALU.add), ("decay", g))
            dve.wait_ge(sem("gdn_decay_exp"), 3)
            for g in range(4):
                o = fill_arrived(dve, ("gkk", g))
                m = threes(AT, g)
                fill_out(dve.tensor_tensor(m, three(o), threes(GAT, g), ALU.mult), ("gkk", g))
                wait_fill_out(dve, ("gkk", g))
                link(dve.tensor_tensor(m, m, bc(prm2("strict", 0, P).unsqueeze(1), [P, 3, P]), ALU.mult))
            for g in range(4):
                o = fill_arrived(dve, ("gqk", g))
                m = threes(GAT, g)
                fill_out(dve.tensor_tensor(m, three(o), m, ALU.mult), ("gqk", g))
            inverse("gd")
            o = fill_arrived(dve, ("gst",))
            fill_out(dve.tensor_copy(flat(ST), o[:, 0:3 * HD]), ("gst",))
            wait_fill_out(dve, ("gv_T", 1))
            subtract_state("gr1", GVT)
            split_low(PIECE_AT["out2", 0, 0])
            split_low(PIECE_AT["out2", 0, 1])
            dve.wait_ge(sem("y2_high"), 1)
            dve.tensor_tensor(OVER_HT[:, 0:5, :], YT2[:, 0:5, :], OVER_HN[:, 0:5, :].bitcast(F32), ALU.subtract)
            wait_fill_out(dve, ("o", 0))
            wait_fill_out(dve, ("o", 1))
            squares(GKB, GQ, "gdn_squares")
            means([("o_ss", 0), ("o_ss", 1)], GTMP, 1.0 / HD, EPS, "gdn_means")
            dve.wait_ge(sem("gdn_roots"), 3)
            link(dve.reciprocal(GTMP[:, :, :], GTMP[:, :, :]))
            link(dve.scalar_tensor_tensor(out=flat(GKB), in0=flat(GKB), scalar=prm2("o_norm"), in1=flat(GTMP),
                                          op0=ALU.mult, op1=ALU.mult))
            dve.tensor_tensor(YT2[:, 5:8, :], GKB[:, :, :], GGT[:, :, :], ALU.mult).then_inc(sem("y2_ready"), 1)

            dve.wait_ge(sem("y2_high"), 2)
            dve.tensor_tensor(OVER_HT[:, 5:8, :], YT2[:, 5:8, :], OVER_HN[:, 5:8, :].bitcast(F32), ALU.subtract)\
                .then_inc(sem("y2_split"), 1)
            add_out("out2", 1.0)
            norm_scale(4)
            split_low(PIECE_AT["ffn2", 0, 1])
            norm_gains(3)

            def hidden2_low(q):
                hidden_low(HID2_HIGH, HID2_LOW, slice(2 * q, 2 * q + 2), HF2[:, q % 2, :], FF1_CHUNKS + q)

            for q in range(2 * FF2_CHUNKS):
                c, j = divmod(q, 2)
                split_low(PIECE_AT["ffn2", c, j] + 2)
                wait_job_out(dve, ("ffn2", c, j))
                m = HF2[:, q % 2, :]
                dve.tensor_tensor(m, m, m, ALU.mult).then_inc(sem("hidden_ready"), 1)
                if q:
                    hidden2_low(q - 1)
            hidden2_low(q)
            for k in range(PIECE_AT["down2", 0, 0] + 2, len(PIECES)):
                split_low(k)
            add_down("down2", 1.0)

        @block.gpsimd
        def _(pool):
            wait_fill_out(pool, ("table",))
            pool.dma_start(table_dram, PT_[0:2 * NH, 0, :].unsqueeze(1).to_broadcast([2 * NH, P, 384])).then_inc(sem("table_stored"), 16)
            pool.wait_ge(sem("table_stored"), 16)
            diagonal = bass.AP(tensor=table_dram.tensor, offset=table_dram.offset + P - 1,
                               ap=[[383, P], [P * 384, 2 * NH], [1, S]])
            pool.dma_start(BIAS[:, :, :], diagonal).then_inc(sem("bias_in"), 16)
            wait_fill_out(pool, ("cb", 0))
            wait_fill_out(pool, ("cb", 1))
            for u, (br, h) in enumerate(UNITS):
                if br == 0:
                    pool.wait_ge(sem("probs_ready"), u + 1)
                    pool.wait_ge(sem("heads_written"), u - 1)
                    pool.tensor_tensor(PT_[:, u % 2, :], PB_[:, u % 2, :], CB[:, h // 4, :], ALU.mult)\
                        .then_inc(sem("mix_by_pool"), 1)
            wait_job_out(pool, ("in2", 0, 1))
            for tt in range(TT):
                pool.tensor_copy(KM[:, tt * MH:(tt + 1) * MH, NOPE:QK],
                                 KR[:, tt, :].unsqueeze(1).to_broadcast([P, MH, ROPE]))\
                    .then_inc(sem("key_rope_by_pool"), 1)
            pool.wait_ge(sem("heads_done"), NU + MH)
            pool.wait_ge(sem("decay_exp"), 1)
            for m in (AT, PM, MB, MK):
                pool.memset(m[HD:P, :, 0:HD], 0.0).then_inc(sem("mats_zeroed"), 1)


def kernel(**inputs):
    import numpy as np
    import concourse.bacc as bacc
    from concourse.bass_utils import run_bass_kernel_spmd as run

    a = {k: np.asarray(v) for k, v in inputs.items()}
    f32 = np.float32

    def k_tiles(w):
        return w.reshape(-1, P, w.shape[1]).transpose(1, 0, 2).reshape(-1)

    w = a["w_in"][0]
    splits = dict(zip(("z", "xbc", "dt", "b", "c", "f", "dq", "dkv", "gate"),
                      np.split(w, np.cumsum([512, 1024, 8, 1536, 1536, 8, 512, 256])[0:8], axis=1)))
    dq = splits["dq"].reshape(D, 2, 4, HD).transpose(0, 2, 1, 3).reshape(D, 512)
    bq, bk, bv = np.split(splits["b"], 3, axis=1)
    cq, ck, cv = np.split(splits["c"], 3, axis=1)
    in1 = [np.concatenate([splits["dkv"], splits["dt"], splits["f"]], axis=1), splits["xbc"][:, 0:512],
           splits["xbc"][:, 512:1024], cq, ck, cv, dq, bq, bk, bv, splits["z"]]
    fg, fu = a["w_ffn_gate"][0], a["w_ffn_up"][0]
    w2 = a["w_in_2"][0]
    r, k, v, zw_za, zg, lat, gd = np.split(w2, np.cumsum([384, 384, 384, 128, 128, 416]), axis=1)
    rw = np.concatenate([zw_za, zg, k, v, r], axis=1)
    in2 = [lat, rw[:, 0:512], rw[:, 512:1024], np.concatenate([rw[:, 1024:], gd[:, 1536:]], axis=1),
           gd[:, 0:512], gd[:, 512:1024], gd[:, 1024:1536]]
    per_chunk = {
        "in1": lambda i: k_tiles(in1[i]),
        "gate": lambda i: k_tiles(splits["gate"][:, i * 512:(i + 1) * 512]),
        "branch": lambda i: k_tiles(a["w_branch"][0, i]),
        "out1": lambda i: k_tiles(a["w_out"][0][:, i * 512:(i + 1) * 512]),
        "ffn1": lambda i: k_tiles(np.concatenate([fg[:, i * 256:(i + 1) * 256], fu[:, i * 256:(i + 1) * 256]], axis=1)),
        "down1": lambda i: k_tiles(a["w_ffn_down"][0][i * 512:(i + 1) * 512]),
        "in2": lambda i: k_tiles(in2[i]),
        "out2": lambda i: k_tiles(a["w_out_2"][0][:, i * 512:(i + 1) * 512]),
        "ffn2": lambda i: k_tiles(a["w_ff1_2"][0][:, i * 512:(i + 1) * 512]),
        "down2": lambda i: k_tiles(a["w_ff2_2"][0][i * 512:(i + 1) * 512]),
    }
    weights = np.concatenate([per_chunk[n](i) for n, i, _ in CHUNKS])

    def cols(v):
        return np.ascontiguousarray(v).reshape(-1, P).T

    def spread(v):
        return np.broadcast_to(np.ascontiguousarray(v).reshape(1, -1), (P, v.size))

    def rows(v):
        out = np.zeros((P, v.shape[-1] if v.ndim > 1 else 1), v.dtype)
        out[0:v.shape[0]] = v.reshape(v.shape[0], -1)
        return out

    p1 = {"norm_mix": cols(a["norm_mix"][0]), "norm_ffn": cols(a["norm_ffn"][0]), "ln_mix": cols(a["ln_mix_g_2"][0]),
          "ln_ffn": cols(a["ln_ffn_g_2"][0]), "conv_w": cols(a["conv_w"][0]), "conv_b": cols(a["conv_b"][0]),
          "ssm_norm": cols(a["ssm_norm_w"][0]), "dt_bias": rows(a["dt_bias"][0]), "a_log": rows(a["a_log"][0]),
          "forget_bias": rows(a["forget_bias"][0]), "sinks": spread(a["sinks"][0]), "d_skip": spread(a["d_skip"][0])}
    mu = a["rwkv_mu_2"][0]
    mu = np.concatenate([mu[1152:1408], mu[384:1152], mu[0:384]])
    t, j = np.arange(P)[:, None], np.arange(P)[None, :]
    levels = []
    for lv in range(LEVELS):
        b = 1 << lv
        m = (t // (2 * b) == j // (2 * b)) & ((t // b) % 2 == 1) & ((j // b) % 2 == 0)
        levels.append(m.T if lv == 0 else m)
    pair_rows = np.zeros((P, 3 * P), f32)
    for h in range(RH):
        pair_rows[h, h * HD:(h + 1) * HD] = 1.0
    inv_freq = f32(10000.0) ** (-np.arange(0, ROPE, 2, dtype=f32) / f32(ROPE))
    p2 = {"mu": cols(mu), "w0": cols(a["rwkv_w0_2"][0]), "a0": cols(a["rwkv_a0_2"][0]), "k_k": cols(a["rwkv_k_k_2"][0]),
          "k_a": cols(a["rwkv_k_a_2"][0]), "r_k": cols(a["rwkv_r_k_2"][0].reshape(-1)), "gn_g": cols(a["rwkv_gn_g_2"][0]),
          "gn_b": cols(a["rwkv_gn_b_2"][0]), "q_norm": cols(a["mla_q_norm_g_2"][0]), "kv_norm": cols(a["mla_kv_norm_g_2"][0]),
          "g_conv": cols(a["gdn_conv_w_2"][0]), "g_alog": rows(a["gdn_a_log_2"][0]), "g_dtb": rows(a["gdn_dt_bias_2"][0]),
          "o_norm": cols(np.concatenate([a["gdn_o_norm_g_2"][0]] * 2)), "q_qk": spread(a["mla_q_qk_g_2"][0]),
          "k_qk": spread(a["mla_k_qk_g_2"][0]), "w2a2": np.concatenate([a["rwkv_w2_2"][0], a["rwkv_a2_2"][0]]),
          "g2": a["rwkv_g2_2"][0], "uq": a["mla_w_uq_2"][0].reshape(2, P, 384).transpose(1, 0, 2).reshape(P, 768),
          "ukv": a["mla_w_ukv_2"][0], "inv_freq": np.broadcast_to(inv_freq, (P, 16)), "strict": (j > t), "incl": (j >= t),
          "levels": np.concatenate(levels, axis=1), "blockones": (t // HD == j // HD), "pair_rows": pair_rows}
    params = np.concatenate([np.asarray(p1[n], f32) for n, _ in PARAMS], axis=1)
    params2 = np.concatenate([np.asarray(p2[n], f32) for n, _ in PARAMS2], axis=1)

    key = np.arange(S)[None, :]
    dist = 255 - np.arange(384)
    d = np.maximum(dist, 1).astype(f32)
    large = 16 + (np.log(d / f32(16)) / f32(np.log(64.0)) * f32(16)).astype(np.int32)
    bucket = np.where(dist < 16, np.maximum(dist, 0), np.minimum(large, 31))
    onehot = np.zeros((P, 384), f32)
    onehot[0:32] = (np.arange(32)[:, None] == bucket[None, :])
    table_mask = np.zeros((P, 384), f32)
    table_mask[0:NH] = np.where(dist >= 0, 0.0, NEG)
    table_mask[NH:2 * NH] = np.where((dist >= 0) & (dist < P), 0.0, NEG)
    after = np.where(key >= t, 0.0, NEG)
    c = {"ident": np.eye(P), "causal": np.where(P + t >= key, 0.0, NEG),
         "ssd_mask": np.concatenate([after, after[:, 0:P]], axis=1),
         "mla_mask": np.where(key // 64 <= (P + t) // 64, 0.0, NEG), "ones": np.ones((P, S)), "onehot": onehot,
         "table_mask": table_mask}
    consts = np.concatenate([np.asarray(c[n], f32) for n, _ in CONSTS], axis=1)
    tables = np.concatenate([onehot, table_mask], axis=1)

    arrays = {"x_dram": a["x"], "weights_dram": weights, "params_dram": params, "params2_dram": params2,
              "consts_dram": consts, "tables_dram": tables, "rel_bias_dram": a["rel_bias"], "norm_final_dram": spread(a["norm_final"]),
              "positions_dram": a["positions_2"].reshape(TT, P).T}
    nc = bacc.Bacc("TRN2", target_bir_lowering=False, num_devices=1)
    args = []
    for name in arrays:
        arrays[name] = np.ascontiguousarray(arrays[name])
        args.append(nc.dram_tensor(name, arrays[name].shape, mybir.dt.from_np(arrays[name].dtype),
                                   kind="ExternalInput").ap())
    args.append(nc.dram_tensor("bias_rows_dram", (2 * NH, P, 384), F32, kind="Internal").ap())
    args.append(nc.dram_tensor("out_dram", (1, S, D), F32, kind="ExternalOutput").ap())
    build(nc, *args)
    result = run(nc, [arrays], core_ids=[0])
    return result.results[0]["out_dram"]
```

```python
from contextlib import ExitStack

import concourse.bass as bass
from concourse import mybir

F32 = mybir.dt.float32
F32R = mybir.dt.float32r
I32 = mybir.dt.int32
ALU = mybir.AluOpType
ACT = mybir.ActivationFunctionType
AX_X = mybir.AxisListType.X

P = 128
S = 256
TT = S // P
D = 1024
KD = D // P
HD = 64
NH = 8
BW = 512
EPS = 1e-6
NEG = -1e30
NRING = 3
SLOT = 4096
FF1_CHUNKS, FF1_KT = 11, 22
FF2_CHUNKS, FF2_KT = 8, 32
RH = 6
MH, QK, NOPE, ROPE = 4, 96, 64, 32
NM = 2 * RH
LEVELS = 7

CHUNKS = [("in1", i, w) for i, w in enumerate([KD * 384] + [KD * 512] * 10)]
CHUNKS += [("gate", i, KD * 512) for i in range(8)]
CHUNKS += [("branch", i, 4 * D) for i in range(4)]
CHUNKS += [("out1", i, KD * 512) for i in range(2)]
CHUNKS += [("ffn1", i, KD * 512) for i in range(FF1_CHUNKS)]
CHUNKS += [("down1", i, min(4, FF1_KT - 4 * i) * D) for i in range((FF1_KT + 3) // 4)]
CHUNKS += [("in2", i, KD * {0: 416, 3: 396}.get(i, 512)) for i in range(7)]
CHUNKS += [("out2", i, KD * 512) for i in range(2)]
CHUNKS += [("ffn2", i, KD * 512) for i in range(FF2_CHUNKS)]
CHUNKS += [("down2", i, 4 * D) for i in range(FF2_KT // 4)]
CHUNK_AT = {(n, i): k for k, (n, i, _) in enumerate(CHUNKS)}
OFFSET = [0]
for _n, _i, _w in CHUNKS:
    OFFSET.append(OFFSET[-1] + P * _w)

JOBS = [("in1", i, j) for i in range(11) for j in range(2)]
JOBS += [("gate", i, j) for i in range(8) for j in range(2)]
JOBS += [("branch", i, j) for i in range(4) for j in range(4)]
JOBS += [("out1", i, j) for i in range(2) for j in range(2)]
JOBS += [("ffn1", i, j) for i in range(FF1_CHUNKS) for j in range(2)]
JOBS += [("in2", i, j) for i in range(7) for j in range(3 if i == 3 else 2)]
JOBS += [("out2", i, j) for i in range(2) for j in range(2)]
JOBS += [("ffn2", i, j) for i in range(FF2_CHUNKS) for j in range(2)]
JOB_AT = {j: k for k, j in enumerate(JOBS)}

SPLIT_IN2 = 3
SPLIT = ("in1", "branch", "out1", "ffn1", "down1", "out2", "ffn2", "down2")
PIECE = 2048
PIECES = [(n, i, j) for n, i, w in CHUNKS if n in SPLIT or (n == "in2" and i < SPLIT_IN2)
          for j in range(-(-w // PIECE))]
PIECE_AT = {p: k for k, p in enumerate(PIECES)}

PARAMS = [("norm_mix", 8), ("norm_ffn", 8), ("ln_mix", 8), ("ln_ffn", 8), ("conv_w", 32), ("conv_b", 8),
          ("ssm_norm", 4), ("dt_bias", 1), ("a_log", 1), ("forget_bias", 1), ("sinks", 8), ("d_skip", 8)]
PARAMS2 = [("mu", 11), ("w0", 3), ("a0", 3), ("k_k", 3), ("k_a", 3), ("r_k", 3), ("gn_g", 3), ("gn_b", 3),
           ("q_norm", 2), ("kv_norm", 1), ("g_conv", 36), ("g_alog", 1), ("g_dtb", 1), ("o_norm", 1),
           ("q_qk", 96), ("k_qk", 96), ("w2a2", 384), ("g2", 384), ("uq", 768), ("ukv", 512),
           ("inv_freq", 16), ("strict", 128), ("incl", 128), ("levels", LEVELS * 128), ("blockones", 128), ("pair_rows", 384)]
CONSTS = [("ident", 128), ("causal", 256), ("ssd_mask", 384), ("mla_mask", 256), ("ones", 256)]
TABLES = [("onehot", 384), ("table_mask", 384)]


def columns(table):
    at, out = 0, {}
    for name, n in table:
        out[name] = (at, at + n)
        at += n
    return out, at


PCOL, NP1 = columns(PARAMS)
P2COL, NP2 = columns(PARAMS2)
CCOL, NC = columns(CONSTS)
TCOL, NT = columns(TABLES)

UNITS = [(b, h) for b in (2, 0, 1, 3) for h in range(NH)]

TWO_PI_A, TWO_PI_B, TWO_PI_C = 6.28125, 0.0019340515136718750, 1.2556659146e-06
ROUND = 12582912.0
E_HALF = 0.6065306597126334


def weight_slots(kind, index):
    k = CHUNK_AT[kind, index]
    return k % NRING, k // NRING + 1


TOKEN_CHUNKS = [("in1", 5), ("in1", 9), ("in1", 10), ("out1", 0), ("out1", 1), ("out2", 0), ("out2", 1)]


def pieces_before(kind, index, j, counted):
    return sum(1 for p in PIECES[:PIECE_AT[kind, index, j] + 1] if p[0] in counted)


def norm_fills(n):
    return [(("norm", n, b), 4 + b) for b in range(4)]


def ring(names, banks, start=0):
    return [(name, banks[(start + k) % len(banks)]) for k, name in enumerate(names)]


HIGH = [4, 5, 6, 7]
ALL8 = [4, 5, 6, 7, 0, 1, 2, 3]
FILLS = norm_fills(0) + [(("table",), 4)]
FILLS += [(("dt_T",), 5), (("xs_T", 0), 6), (("xs_T", 1), 7), (("cb", 0), 4), (("cb", 1), 5)]
FILLS += [(("y_T", i, b), 4 + 2 * (i % 2) + b) for i in range(4) for b in range(2)]
FILLS += [(("mix_T", b), 4 + b) for b in range(4)]
FILLS += norm_fills(1) + [(("down1", b), 4 + b) for b in range(4)]
FILLS += norm_fills(2)
FILLS += ring([("mla_ss",), ("lora", 0), ("lora", 1), ("lora", 2), ("lora", 3), ("rw_g", 0), ("rw_g", 1),
               ("mla_q", 0), ("mla_q", 1), ("mla_kv", 0), ("mla_kv", 1)] + [("mla_T", b) for b in range(4)]
              + [("kk_ss", 0), ("kk_ss", 1), ("bonus", 0), ("bonus", 1)]
              + [("b_T",), ("k_T",), ("v_T", 0), ("v_T", 1), ("yM_T",)], HIGH)
MATS = [(kind, g) for kind in ("by_b", "by_k") for g in range(6)]


def matrix(c, h):
    return (h % 2) * RH + c * 3 + h // 2


GDN_PRE = {2: [("gq_ss", 0), ("gq_ss", 1)], 4: [("gk_ss", 0), ("gk_ss", 1)],
           6: [("beta", 0), ("beta", 1), ("g_e",), ("g_k",)]}
PLACES = sorted((matrix(c, h), c, h) for c in range(2) for h in range(RH))


def inverse_names(fam):
    out = [(fam, "t0", g) for g in range(3)]
    out += [("av", 0), ("av", 1)] if fam == "rw" else []
    for lv in range(1, LEVELS):
        out += GDN_PRE.get(lv, []) if fam == "rw" else []
        out += [(fam, "p", lv, g) for g in range(3)]
        if lv < LEVELS - 1:
            out += [(fam, "t", lv, g) for g in range(3)]
        out += [(fam, "tt", lv, g) for g in range(3)]
    return out


SOLVE_RW = [("sa", 0), ("st",), ("gv_T", 0), ("gv_T", 1), ("gk_T",), ("r1", 0), ("r1", 1), ("sa", 1), ("y", 0), ("y", 1)]
POST_RW = [("gn_mean", 0), ("gn_mean", 1), ("gn_var", 0), ("gn_var", 1)]
GDN_MATS = [("decay", g) for g in range(3)] + [("gkk", g) for g in range(4)] + [("gqk", g) for g in range(4)]
SOLVE_G = [("du", 0), ("gst",), ("gr1", 0), ("gr1", 1), ("du", 1), ("o", 0), ("o", 1), ("o_ss", 0), ("o_ss", 1)]
FILLS += ring(MATS + inverse_names("rw") + SOLVE_RW + POST_RW
              + GDN_MATS + inverse_names("gd") + SOLVE_G, ALL8)
FILLS += norm_fills(3) + [(("down2", b), 4 + b) for b in range(4)]
FILL_AT = {name: k for k, (name, _) in enumerate(FILLS)}
FILL_USES = []
_seen = [0] * 8
for _name, _b in FILLS:
    FILL_USES.append(_seen[_b])
    _seen[_b] += 1


def build(nc, x, weights, params, params2, consts, tables, rel_bias, norm_final, positions, table_dram, out):
    with ExitStack() as ctx:
        def sb(name, shape, dt=F32):
            return ctx.enter_context(nc.sbuf_tensor(name, shape, dt))

        sems = {}

        def sem(name):
            if name not in sems:
                sems[name] = ctx.enter_context(nc.semaphore(name))
            return sems[name]

        places = {}

        def placed(name, shape):
            places[name] = (nc.sbuf_base + 31) // 32 * 32
            return sb(name, shape)

        def over(name, place, at, shape):
            return nc.alloc_sbuf_tensor_at(name, [P] + shape, F32R, offset=places[place] + 4 * at)

        rings = [sb(f"weights{i}", [P, SLOT]) for i in range(NRING)]
        X = sb("X", [P, TT, D])
        HN = placed("HN", [P, TT, D])
        HT = placed("HT", [P, KD, S])
        PRM = sb("PRM", [P, NP1])
        CST = sb("CST", [P, NC])
        NF = sb("NF", [P, D])
        RELB = sb("RELB", [32, 2 * NH])
        POS = sb("POS", [P, TT], I32)
        BIAS = placed("BIAS", [P, 2 * NH, S])
        STAT = sb("STAT", [P, 64])
        SM8 = sb("SM8", [NH, 1792])
        negident = sb("negident", [P, P])
        one_minus_mu = sb("one_minus_mu", [P, 11])
        ARENA = placed("ARENA", [P, 26112])
        OVER_HT, OVER_HN = over("OVER_HT", "HT", 0, [KD, S]), over("OVER_HN", "HN", 0, [KD, S])
        FIRST_HIGH, FIRST_LOW = over("FIRST_HIGH", "BIAS", 0, [KD, S]), over("FIRST_LOW", "BIAS", KD * S, [KD, S])
        IN2_HIGH, IN2_LOW = over("IN2_HIGH", "ARENA", 11008, [KD, S]), over("IN2_LOW", "ARENA", 13056, [KD, S])
        W_HIGH = [[over(f"W_HIGH{b}{i}", "ARENA", at, [PIECE]) for i, at in enumerate(ats)]
                  for b, ats in enumerate(((10240, 14336), (0, 2048), (2816, 4864)))]
        W_LOW = [[over(f"W_LOW{b}{i}", "ARENA", at, [PIECE]) for i, at in enumerate(ats)]
                 for b, ats in enumerate(((12288, 24064), (4096, 6144), (6912, 8960)))]
        HID1_HIGH, HID1_LOW = over("HID1_HIGH", "ARENA", 0, [FF1_KT, S]), over("HID1_LOW", "ARENA", 16384, [FF1_KT, S])
        HID2_HIGH, HID2_LOW = over("HID2_HIGH", "ARENA", 8192, [FF2_KT, S]), over("HID2_LOW", "ARENA", 16384, [FF2_KT, S])

        def area(at, *shape):
            n = 1
            for v in shape:
                n *= v
            a = ARENA[:, at:at + n]
            if len(shape) == 2:
                a = a.rearrange("p (a b) -> p a b", a=shape[0])
            return a

        def prm(name, j=0, n=1):
            a = PCOL[name][0] + j
            return PRM[:, a:a + n]

        P2 = BIAS[:, :, :].rearrange("p a b -> p (a b)")

        def prm2(name, j=0, n=1):
            a = P2COL[name][0] + j
            return P2[:, a:a + n]

        def cst(name):
            a, b = CCOL[name]
            return CST[:, a:b]

        TBL = ARENA[:, 8192:8192 + NT]

        def tbl(name):
            a, b = TCOL[name]
            return TBL[:, a:b]

        ident = cst("ident")
        ones = cst("ones")

        GT = area(0, TT, 4 * D)
        SG = area(5632, 2, 512)
        HF1 = area(6656, 2, 512)
        XBC = area(8192, 8, S)
        CQ1, CK1 = area(10240, 4, S), area(11264, 4, S)
        BQ1, BK1 = area(12288, 4, S), area(13312, 4, S)
        DQ1, DK1 = area(14336, 4, S), area(15360, S)
        CV1, BV1, DV1 = area(15616, TT, BW), area(16640, TT, BW), area(17664, TT, P)
        YB = [HN[:, 0, :].rearrange("p (t w) -> p t w", t=TT)] + [area(17920 + 1024 * i, TT, BW) for i in range(3)]
        SILZ = HN[:, 1, :].rearrange("p (t w) -> p t w", t=TT)
        CB = area(20992, 2, 384)
        XDT = area(21760, TT, BW)
        SB_, PB_, PT_ = area(22784, 2, 384), area(23552, 2, 384), area(24320, 2, 384)
        YT_HIGH = [over(f"YT_HIGH{i}", "ARENA", at, [4, S]) for i, at in enumerate((8192, 9216))]
        YT_LOW = [over(f"YT_LOW{i}", "ARENA", at, [4, S]) for i, at in enumerate((16384, 22016))]
        TMP = area(20992, 2, 512)
        SQ1 = area(8192, 2, 512)
        SQA, SQB = area(0, 2, D), area(8192, 2, D)
        STG = area(22784, 2, 512)
        ACC, TH = area(25088, 2, S), area(25600, 2, S)

        RZ = area(0, 11, S)
        LO, K3, V3, R3 = RZ[:, 0:2, :], RZ[:, 2:5, :], RZ[:, 5:8, :], RZ[:, 8:11, :]
        A3, KK, GM, BON, GG, LW, G3, E3, T3 = [area(2816 + 768 * i, 3, S) for i in range(9)]
        GZ = area(9728, 12, S)
        GQ, GK, GV, GGT = [GZ[:, 3 * i:3 * i + 3, :] for i in range(4)]
        GKB = area(12800, 3, S)
        GKE, GQD, GKD = [area(13568 + 384 * i, 3, P) for i in range(3)]
        BTk, KTk, GKT = [HN[:, 0, 384 * i:384 * (i + 1)] if i < 2 else area(14720, 384) for i in range(3)]
        VT = HN[:, 1, 0:768].rearrange("p (c w) -> p c w", c=2)
        GVT = area(15104, 2, 384)
        AT, TM, TTM, PM = [area(15872 + 1536 * i, NM, P) for i in range(4)]
        MB = area(22016, NM, P)
        MK = area(2816 + 768 * 5, NM, P)
        GAT = MB
        RR = area(23552, 2, 384)
        SA = area(24320, 2, 384)
        ST = area(25088 + 0, 3, HD)
        CQF, SQM = area(15872, 3, S), area(16640, 3, S)
        KR = area(17408, TT, ROPE)
        QM, KM = area(17472, 8, QK), area(18240, 8, QK)
        VM = area(19008, TT, MH * HD)
        SQQ = area(19520, 8, QK)
        QTm, KTm = area(20288, MH, S), area(21312, MH, S)
        COS, SIN, ROT = area(22336, TT, 16), area(22368, TT, 16), area(19520, 4, 128)
        GTMP = area(13568, 3, S)
        YM = NF[:, 0:512].rearrange("p (t w) -> p t w", t=TT)
        YT2 = HT
        HF2 = area(24576, 2, 512)

        BK = [ctx.enter_context(nc.psum_tensor(f"bank{i}", [P, 512], F32)) for i in range(8)]

        def bank_of(name):
            return BK[FILLS[FILL_AT[name]][1]]

        def job_bank(job):
            return BK[JOB_AT[job] % 4]

        def fill_arrived(eng, name):
            eng.wait_ge(sem("fills_written"), FILL_AT[name] + 1)
            return bank_of(name)

        def fill_out(ins, name):
            ins.then_inc(sem(f"fill_out{FILLS[FILL_AT[name]][1]}"), 1)

        def wait_fill_out(eng, name):
            f = FILL_AT[name]
            eng.wait_ge(sem(f"fill_out{FILLS[f][1]}"), FILL_USES[f] + 1)

        def job_arrived(eng, job):
            eng.wait_ge(sem("jobs_written"), JOB_AT[job] + 1)
            return job_bank(job)

        def job_out(ins, job):
            ins.then_inc(sem(f"job_out{JOB_AT[job] % 4}"), 1)

        def wait_job_out(eng, job):
            j = JOB_AT[job]
            eng.wait_ge(sem(f"job_out{j % 4}"), j // 4 + 1)

        def piece_parts(k):
            kind = PIECES[k][0]
            rows = {"branch": 4, "down1": 2, "down2": 2}.get(kind, KD)
            b = 1 if kind in ("in1", "out2", "ffn2", "down2") else 2 if kind == "in2" else 0
            n = rows * piece_source(k).shape[-1]
            return [t[b][k % 2][:, 0:n].rearrange("p (k n) -> p k n", k=rows) for t in (W_HIGH, W_LOW)]

        def piece_source(k):
            kind, i, j = PIECES[k]
            width = CHUNKS[CHUNK_AT[kind, i]][2]
            rows = {"branch": 4, "down1": width // D, "down2": width // D}.get(kind, KD)
            w = rings[weight_slots(kind, i)[0]][:, 0:width].rearrange("p (k n) -> p k n", k=rows)
            if kind in ("down1", "down2"):
                return w[:, 2 * j:2 * j + 2, :]
            n = 512 if kind == "branch" else 256
            return w[:, :, j * n:min((j + 1) * n, width // rows)]

        def wait_piece_used(eng, k):
            kind, i, j = PIECES[k]
            if (kind, i) in TOKEN_CHUNKS and j == 0:
                eng.wait_ge(sem("first_halves"), TOKEN_CHUNKS.index((kind, i)) + 1)
            elif kind in ("ffn1", "ffn2", "in1", "in2"):
                eng.wait_ge(sem("jobs_written"), JOB_AT[kind, i, j] + 1)
            elif kind == "branch":
                eng.wait_ge(sem("jobs_written"), JOB_AT[kind, i, 2 * j + 1] + 1)
            elif kind in ("out1", "out2"):
                eng.wait_ge(sem("jobs_written"), JOB_AT[kind, i, 1] + 1)
            elif PIECES[k + 1:k + 2] and PIECES[k + 1][0] == kind:
                eng.wait_ge(sem(kind + "_pieces_read"), pieces_before(kind, i, j, (kind,)))
            else:
                eng.wait_ge(sem("fills_written"), FILL_AT[kind, 3] + 1)

        def attention_units(n):
            return sum(1 for b, _ in ALL_UNITS[:n] if b != 0)

        ALL_UNITS = UNITS + [(4, h) for h in range(MH)]
        NU = len(UNITS)

        block = ctx.enter_context(nc.Block())

        @block.sync
        def _(sp):
            for k, (kind, i, width) in enumerate(CHUNKS):
                if k >= NRING:
                    was, n = CHUNKS[k - NRING][0:2]
                    if (was, n, 0) in PIECE_AT:
                        sp.wait_ge(sem("pieces_split"), max(PIECE_AT[p] for p in PIECES if p[:2] == (was, n)) + 1)
                    else:
                        sp.wait_ge(sem("jobs_written"), max(JOB_AT[j] for j in JOBS if j[:2] == (was, n)) + 1)
                if k == 1:
                    sp.wait_ge(sem("consts_in"), 16 * 3)
                src = weights[OFFSET[k]:OFFSET[k + 1]].rearrange("(p n) -> p n", p=P)
                sp.dma_start(rings[k % NRING][:, 0:width], src).then_inc(sem(f"weights_in{k % NRING}"), 16)
            for b in range(4):
                wait_fill_out(sp, ("down2", b))
                tt, dc = divmod(b, 2)
                sp.dma_start(out[0, tt * P:(tt + 1) * P, dc * 512:(dc + 1) * 512],
                             X[:, tt, dc * 512:(dc + 1) * 512]).then_inc(sem("out_stored"), 16)
            sp.wait_ge(sem("out_stored"), 16 * 4)

        SUMSQ, MEANSQ, RMS, RSTD = [STAT[:, 2 * i:2 * i + 2] for i in range(4)]
        NEGM, RSUM, RREC, ESINK = [STAT[:, 8 + 4 * i:12 + 4 * i].rearrange("p (u t) -> p u t", u=2) for i in range(4)]
        DTT = STAT[:, 24:40]
        NSINK = STAT[:, 40:48]
        EGC = STAT[:, 48:51]
        EALOG = STAT[:, 51:52]
        QKSS = area(22500, 16)
        POSF = area(22516, 2)
        SPX, DECAY, ACUM, FCUM, SPT = [SM8[:, a:b] for a, b in ((0, 512), (512, 768), (768, 1024), (1024, 1280), (1280, 1792))]
        BETA, GCUM, EGCUM, EKEND, GAX, GSPT, GLOG = [SM8[0:RH, a:b] for a, b in (
            (0, 256), (256, 512), (512, 768), (768, 896), (1024, 1280), (1280, 1536), (1536, 1792))]

        @block.tensor
        def _(pe):
            state = {"fill": 0, "job": 0, "operand": None}

            def wait_operand(k):
                if state["operand"] is not None:
                    if k % 2 == 0:
                        wait_fill_out(pe, (*state["operand"], k // 2))
                    if k == KD - 1:
                        state["operand"] = None

            def open_fill(name):
                f = state["fill"]
                assert FILLS[f][0] == name, (FILLS[f], name)
                b = FILLS[f][1]
                if FILL_USES[f]:
                    pe.wait_ge(sem(f"fill_out{b}"), FILL_USES[f])
                return BK[b]

            def close_fill(ins):
                state["fill"] += 1
                ins.then_inc(sem("fills_written"), 1)

            def open_job(job):
                j = state["job"]
                assert JOBS[j] == job, (JOBS[j], job)
                if j >= 4:
                    pe.wait_ge(sem(f"job_out{j % 4}"), j // 4)
                return BK[j % 4]

            def close_job(ins):
                state["job"] += 1
                ins.then_inc(sem("jobs_written"), 1)

            def chunk(kind, i, k, n):
                slot, turn = weight_slots(kind, i)
                pe.wait_ge(sem(f"weights_in{slot}"), 16 * turn)
                return rings[slot][:, 0:k * n].rearrange("p (k n) -> p k n", k=k)

            def product_f(o, w, a, n=P):
                for k in range(KD):
                    wait_operand(k)
                    ins = pe.matmul(o, w[:, k, a:a + n], HT[:, k, :], start=(k == 0), stop=(k == KD - 1))
                return ins

            def product_t(o, w, tt, a, n, ks=range(KD)):
                for k in ks:
                    ins = pe.matmul(o, HT[:, k, tt * P:(tt + 1) * P], w[:, k, a:a + n],
                                    start=(k == 0), stop=(k == KD - 1))
                return ins

            def norm_transposes(n):
                banks = []
                for b in range(4):
                    banks.append(open_fill(("norm", n, b)))
                    state["fill"] += 1
                for tt in range(TT):
                    pe.wait_ge(sem(f"hn{tt}_ready"), n + 1)
                    for b in range(4):
                        for j in range(2):
                            k = 2 * b + j
                            ins = pe.transpose(banks[b][:, j * S + tt * P:j * S + (tt + 1) * P],
                                               HN[:, tt, k * P:(k + 1) * P], ident)
                        if tt == TT - 1:
                            ins.then_inc(sem("fills_written"), 1)
                state["operand"] = ("norm", n)

            def split_piece(kind, i, j):
                k = PIECE_AT[kind, i, j]
                pe.wait_ge(sem("pieces_split"), k + 1)
                return piece_parts(k)

            def product3(o, left, right, first=True, last=True):
                n = len(left[0])
                for k in range(n):
                    wait_operand(k)
                    for a, b in ((0, 0), (0, 1), (1, 0)):
                        ins = pe.matmul(o, left[a][k], right[b][k], start=(first and k == 0 and a + b == 0),
                                        stop=(last and k == n - 1 and a == 1))
                return ins

            def f_jobs_split(kind, i, high=OVER_HT, low=OVER_HN):
                for j in range(2):
                    w = split_piece(kind, i, j)
                    o = open_job((kind, i, j))
                    for t in range(2):
                        ins = product3(o[:, t * S:(t + 1) * S],
                                       [[part[:, k, t * P:(t + 1) * P] for k in range(KD)] for part in w],
                                       [[part[:, k, :] for k in range(KD)] for part in (high, low)])
                    close_job(ins)

            def two_f_jobs(kind, i, tiles=4):
                w = chunk(kind, i, KD, tiles * P)
                for j in range(2):
                    o = open_job((kind, i, j))
                    for t in range(2):
                        if 2 * j + t < tiles:
                            ins = product_f(o[:, t * S:(t + 1) * S], w, (2 * j + t) * P)
                    close_job(ins)

            def t_jobs_split(kind, i, high, low, late=False):
                for j in range(2):
                    w = split_piece(kind, i, j)
                    for tt in range(TT):
                        if j == 0:
                            o = open_job((kind, i, tt))
                            state["job"] += (1 if tt == 0 else 0)
                        if late and j == 0:
                            pe.wait_ge(sem("y2_split"), 1)
                            product3(o[:, 0:S], [[part[:, k, tt * P:(tt + 1) * P] for k in range(5)] for part in (high, low)],
                                     [[part[:, k, :] for k in range(5)] for part in w], last=False)
                    for tt in range(TT):
                        o = job_bank((kind, i, tt))
                        if late and j == 0:
                            for k in range(5, KD):
                                pe.wait_ge(sem("y2_split"), k - 3)
                                ins = product3(o[:, 0:S], [[part[:, k, tt * P:(tt + 1) * P]] for part in (high, low)],
                                               [[part[:, k, :]] for part in w], first=False, last=(k == KD - 1))
                        else:
                            ins = product3(o[:, j * S:(j + 1) * S],
                                           [[part[:, k, tt * P:(tt + 1) * P] for k in range(KD)] for part in (high, low)],
                                           [[part[:, k, :] for k in range(KD)] for part in w])
                        if j:
                            ins.then_inc(sem("jobs_written"), 1)
                        elif tt:
                            ins.then_inc(sem("first_halves"), 1)
                state["job"] += 1

            pe.wait_ge(sem("params_in"), 16 * 2)
            norm_transposes(0)

            pe.wait_ge(sem("consts_in"), 16 * 3)
            o = open_fill(("table",))
            close_fill(pe.matmul(o[0:2 * NH, 0:384], RELB[:, :], tbl("onehot")[0:32, :], start=True, stop=True))

            first = (FIRST_HIGH, FIRST_LOW)
            stream = [[part[:, k, :] for k in range(KD)] for part in first]
            w = split_piece("in1", 0, 0)
            o = open_job(("in1", 0, 0))
            product3(o[:, 0:S], [[part[:, k, 0:P] for k in range(KD)] for part in w], stream)
            for tt in range(TT):
                ins = product3(o[:, S + tt * P:S + (tt + 1) * P],
                               [[part[:, k, tt * P:(tt + 1) * P] for k in range(KD)] for part in first],
                               [[part[:, k, P:2 * P] for k in range(KD)] for part in w])
            close_job(ins)
            w = split_piece("in1", 0, 1)
            o = open_job(("in1", 0, 1))
            close_job(product3(o[:, 0:S], [[part[:, k, :] for k in range(KD)] for part in w], stream))
            for i in (1, 2, 3):
                f_jobs_split("in1", i, *first)
                if i == 2:
                    pe.wait_ge(sem("dt_ready"), 1)
                    o = open_fill(("dt_T",))
                    for tt in range(TT):
                        ins = pe.matmul(o[:, tt * NH:(tt + 1) * NH], SM8[:, tt * P:(tt + 1) * P],
                                        ident[0:NH, 0:NH], start=True, stop=True)
                    close_fill(ins)
            pe.wait_ge(sem("conv_done"), 8)
            for tt in range(TT):
                o = open_fill(("xs_T", tt))
                for k in range(4):
                    ins = pe.transpose(o[:, k * P:(k + 1) * P], XBC[:, k, tt * P:(tt + 1) * P], ident)
                close_fill(ins)
            for g in range(2):
                o = open_fill(("cb", g))
                pe.matmul(o[:, 0:S], XBC[:, 4 + g, 0:P], XBC[:, 6 + g, :], start=True, stop=True)
                close_fill(pe.matmul(o[:, S:384], XBC[:, 4 + g, P:S], XBC[:, 6 + g, P:S], start=True, stop=True))
            for i in range(4, 11):
                (t_jobs_split if ("in1", i) in TOKEN_CHUNKS else f_jobs_split)("in1", i, *first)

            def row_of(h, n, sign):
                a = ident if sign > 0 else negident[:, :]
                return a[0:NH, h:h + 1].to_broadcast([NH, n])

            def scores(u):
                br, h = ALL_UNITS[u]
                if u >= 2:
                    pe.wait_ge(sem("scores_read"), u - 1)
                o = BK[4 + u % 2]
                if br == 0:
                    a = SM8[:, 768:768 + S]
                    for (c0, c1, s0) in ((0, S, 0), (S, 384, P)):
                        pe.matmul(o[:, c0:c1], row_of(h, P, 1), a[:, s0:S], start=True, stop=False)
                        ins = pe.matmul(o[:, c0:c1], a[:, s0:s0 + P], row_of(h, c1 - c0, -1),
                                        start=False, stop=True)
                    ins.then_inc(sem("scores_written"), 1)
                    return
                pb, t = HD * (h % 2), h // 2
                if br == 4:
                    q, k = QTm[0:QK, h, :], KTm[0:QK, h, :]
                elif br == 3:
                    pb, t = HD * (h // 4), h % 4
                    q, k = DQ1[pb:pb + HD, t, :], DK1[pb:pb + HD, :]
                else:
                    Q, K = (CQ1, CK1) if br == 2 else (BQ1, BK1)
                    q, k = Q[pb:pb + HD, t, :], K[pb:pb + HD, t, :]
                for (c0, c1, q0) in ((0, P, 0), (P, 384, P)):
                    n = c1 - c0
                    ins = pe.matmul(o[:, c0:c1], q[:, q0:q0 + P], k[:, 0:n], start=True, stop=(br != 2))
                    if br == 2:
                        cum = SM8[:, 1024:1280]
                        pe.matmul(o[:, c0:c1], cum[:, q0:q0 + P], row_of(h, n, 1), start=False, stop=False)
                        ins = pe.matmul(o[:, c0:c1], row_of(h, P, -1), cum[:, 0:n], start=False, stop=True)
                ins.then_inc(sem("scores_written"), 1)

            def probs_T(u):
                if ALL_UNITS[u][0] == 0:
                    return
                pe.wait_ge(sem("probs_ready"), u + 1)
                n = attention_units(u)
                if n:
                    pe.wait_ge(sem("probsT_by_act"), n)
                for j in range(3):
                    ins = pe.transpose(BK[6][:, j * P:(j + 1) * P], PB_[:, u % 2, j * P:(j + 1) * P], ident)
                ins.then_inc(sem("probsT_written"), 1)

            def values(u):
                br, h = ALL_UNITS[u]
                if br == 0:
                    pe.wait_ge(sem("mix_by_pool"), u + 1 - attention_units(u + 1))
                else:
                    pe.wait_ge(sem("probsT_by_act"), attention_units(u + 1))
                if u >= 1:
                    pe.wait_ge(sem("heads_done"), u)
                V, a = {0: (XDT, h * HD), 1: (BV1, h * HD), 2: (CV1, h * HD), 3: (DV1, (h // 4) * HD),
                        4: (VM, h * HD)}[br]
                o = BK[7][:, (u % 2) * P:(u % 2 + 1) * P]
                pt = PT_[:, u % 2, :]
                pe.matmul(o[:, 0:HD], pt[:, 0:P], V[:, 0, a:a + HD], start=True, stop=True)
                pe.matmul(o[:, HD:2 * HD], pt[:, P:2 * P], V[:, 0, a:a + HD], start=True, stop=False)
                pe.matmul(o[:, HD:2 * HD], pt[:, 2 * P:3 * P], V[:, 1, a:a + HD], start=False, stop=True)\
                    .then_inc(sem("heads_written"), 1)

            for i in range(5, 11):
                wait_job_out(pe, ("in1", i, 0))
                wait_job_out(pe, ("in1", i, 1))
            for name in (("xs_T", 0), ("xs_T", 1), ("cb", 0), ("cb", 1)):
                wait_fill_out(pe, name)
            pe.wait_ge(sem("rows_ready"), 1)
            pe.wait_ge(sem("stream_by_pool"), 1)
            for u in range(NU + 1):
                if u < NU:
                    scores(u)
                if u >= 1:
                    probs_T(u - 1)
                if u < NU:
                    g, half = divmod(u, 2)
                    i, tt = divmod(g, 2)
                    w = chunk("gate", i, KD, 512)
                    o = open_job(("gate", i, tt)) if half == 0 else job_bank(("gate", i, tt))
                    ins = product_t(o[:, :], w, tt, 0, 512, range(4 * half, 4 * half + 4))
                    if half:
                        close_job(ins)
                if u >= 1:
                    values(u - 1)

            def branch_T(i):
                if i == 0:
                    pe.wait_ge(sem("ya_ready"), 2)
                    pe.wait_ge(sem("heads_done"), NU)
                for b in range(2):
                    o = open_fill(("y_T", i, b))
                    for j in range(2):
                        for tt in range(TT):
                            k = 2 * b + j
                            ins = pe.transpose(o[:, j * S + tt * P:j * S + (tt + 1) * P],
                                               YB[i][:, tt, k * P:(k + 1) * P], ident)
                    close_fill(ins)

            def branch_product(i):
                wait_fill_out(pe, ("y_T", i, 0))
                wait_fill_out(pe, ("y_T", i, 1))
                for dc in range(2):
                    w = split_piece("branch", i, dc)
                    for tt in range(TT):
                        o = open_job(("branch", i, 2 * dc + tt))
                        close_job(product3(o[:, :], [[part[:, k, tt * P:(tt + 1) * P] for k in range(4)]
                                                     for part in (YT_HIGH[i % 2], YT_LOW[i % 2])],
                                           [[part[:, k, :] for k in range(4)] for part in w]))

            branch_T(0)
            for i in range(4):
                if i < 3:
                    branch_T(i + 1)
                branch_product(i)


            def down(kind, high, low, nk, ready, fills):
                o = [bank_of((fills, b)) for b in range(4)]
                for b in range(4):
                    f = FILL_AT[fills, b]
                    pe.wait_ge(sem(f"fill_out{FILLS[f][1]}"), FILL_USES[f])
                for c in range(nk // 2):
                    w = split_piece(kind, c // 2, c % 2)
                    for k in range(2):
                        t = 2 * c + k
                        ready(t)
                        for tt in range(TT):
                            for dc in range(2):
                                ins = product3(o[2 * tt + dc][:, :],
                                               [[part[:, t, tt * P:(tt + 1) * P]] for part in (high, low)],
                                               [[part[:, k, dc * 512:(dc + 1) * 512]] for part in w],
                                               first=(t == 0), last=(t == nk - 1))
                                if t == nk - 1:
                                    close_fill(ins)
                    if t < nk - 1:
                        ins.then_inc(sem(kind + "_pieces_read"), 1)

            pe.wait_ge(sem("mixed_by_pool"), 12)
            for b in range(4):
                o = open_fill(("mix_T", b))
                for j in range(2):
                    for tt in range(TT):
                        k = 2 * b + j
                        ins = pe.transpose(o[:, j * S + tt * P:j * S + (tt + 1) * P],
                                           HN[:, tt, k * P:(k + 1) * P], ident)
                close_fill(ins)
            state["operand"] = ("mix_T",)
            for dc in range(2):
                t_jobs_split("out1", dc, OVER_HT, OVER_HN)

            norm_transposes(1)
            for i in range(FF1_CHUNKS):
                f_jobs_split("ffn1", i)
            down("down1", HID1_HIGH, HID1_LOW, FF1_KT, lambda t: pe.wait_ge(sem("hidden_split"), t // 2 + 1), "down1")

            norm_transposes(2)
            stream2 = (IN2_HIGH, IN2_LOW)
            w = split_piece("in2", 0, 0)
            o = open_job(("in2", 0, 0))
            for t in range(2):
                ins = product3(o[:, t * S:(t + 1) * S], [[part[:, k, t * P:(t + 1) * P] for k in range(KD)] for part in w],
                               [[part[:, k, :] for k in range(KD)] for part in stream2])
            close_job(ins)
            w = split_piece("in2", 0, 1)
            o = open_job(("in2", 0, 1))
            product3(o[:, 0:S], [[part[:, k, 0:P] for k in range(KD)] for part in w],
                     [[part[:, k, :] for k in range(KD)] for part in stream2])
            for tt in range(TT):
                ins = product3(o[:, S + tt * ROPE:S + (tt + 1) * ROPE],
                               [[part[:, k, tt * P:(tt + 1) * P] for k in range(KD)] for part in stream2],
                               [[part[:, k, P:P + ROPE] for k in range(KD)] for part in w])
            close_job(ins)
            f_jobs_split("in2", 1, *stream2)
            def tile_slots(names):
                for name, tiles in zip(names, ((0, 1), (2,))):
                    o = open_fill(name)
                    for n, t in enumerate(tiles):
                        yield o[:, n * S:(n + 1) * S], t, t == tiles[-1]

            def head_sums(names, src, ready, count):
                pe.wait_ge(sem(ready), count)
                for o, t, last in tile_slots(names):
                    ins = pe.matmul(o, prm2("blockones", 0, P), src[:, t, :], start=True, stop=True)
                    if last:
                        close_fill(ins)

            wait_job_out(pe, ("in2", 0, 0))
            wait_job_out(pe, ("in2", 0, 1))
            o = open_fill(("mla_ss",))
            for t in range(2):
                pe.matmul(o[:, 0:S], ones[:, 0:P], SQM[:, t, :], start=(t == 0), stop=(t == 1))
            close_fill(pe.matmul(o[:, S:2 * S], ones[:, 0:P], SQM[:, 2, :], start=True, stop=True))
            f_jobs_split("in2", 2, *stream2)
            pe.wait_ge(sem("stream_by_pool"), 2)
            pe.wait_ge(sem("lora_by_act"), 1)
            for n, (pb, tiles) in enumerate(((0, (0, 1)), (0, (2,)), (HD, (0, 1)), (HD, (2,)))):
                o = open_fill(("lora", n))
                for j, t in enumerate(tiles):
                    ins = pe.matmul(o[:, j * S:(j + 1) * S], prm2("w2a2", t * P, P)[pb:pb + HD, :],
                                    LO[pb:pb + HD, 0, :], start=True, stop=True)
                close_fill(ins)
            pe.wait_ge(sem("lora_by_dve"), 1)
            for o, t, last in tile_slots([("rw_g", 0), ("rw_g", 1)]):
                ins = pe.matmul(o, prm2("g2", t * P, P), LO[:, 1, :], start=True, stop=True)
                if last:
                    close_fill(ins)
            pe.wait_ge(sem("latents_ready"), 1)
            for tt in range(TT):
                o = open_fill(("mla_q", tt))
                for t in range(2):
                    ins = pe.matmul(o[:, 0:MH * QK], CQF[:, t, tt * P:(tt + 1) * P],
                                    prm2("uq", t * 384, 384), start=(t == 0), stop=(t == 1))
                close_fill(ins)
            for tt in range(TT):
                o = open_fill(("mla_kv", tt))
                close_fill(pe.matmul(o[:, :], CQF[:, 2, tt * P:(tt + 1) * P], prm2("ukv", 0, 512),
                                     start=True, stop=True))
            w = chunk("in2", 3, KD, 396)
            o = open_job(("in2", 3, 0))
            for t in range(2):
                ins = product_f(o[:, t * S:(t + 1) * S], w, t * P)
            close_job(ins)
            close_job(product_f(open_job(("in2", 3, 1))[:, 0:S], w, 2 * P))
            o = open_job(("in2", 3, 2))
            for t in range(2):
                ins = product_f(o[0:RH, t * S:(t + 1) * S], w, 384 + RH * t, RH)
            close_job(ins)
            pe.wait_ge(sem("mla_qk_ready"), 1)
            for n, src in enumerate((QM, KM)):
                for b in range(2):
                    o = open_fill(("mla_T", 2 * n + b))
                    for j in range(2):
                        for tt in range(TT):
                            ins = pe.transpose(o[0:QK, j * S + tt * P:j * S + (tt + 1) * P],
                                               src[:, tt * MH + 2 * b + j, :], ident)
                    close_fill(ins)
            for b in range(4):
                wait_fill_out(pe, ("mla_T", b))
            w = chunk("in2", 4, KD, 512)
            for u in range(NU, NU + MH + 1):
                if u < NU + MH:
                    scores(u)
                if u > NU:
                    probs_T(u - 1)
                if u < NU + MH:
                    j, t = divmod(u - NU, 2)
                    o = open_job(("in2", 4, j)) if t == 0 else job_bank(("in2", 4, j))
                    ins = product_f(o[:, t * S:(t + 1) * S], w, (u - NU) * P)
                    if t:
                        close_job(ins)
                if u > NU:
                    values(u - 1)
            pe.wait_ge(sem("heads_done"), NU + MH)
            head_sums([("kk_ss", 0), ("kk_ss", 1)], T3, "rw_squares", 1)
            two_f_jobs("in2", 5)
            two_f_jobs("in2", 6)
            head_sums([("bonus", 0), ("bonus", 1)], T3, "rw_squares", 2)
            pe.wait_ge(sem("rw_factors"), 1)
            pe.wait_ge(sem("factors_by_pool"), 1)
            for name, src in ((("b_T",), A3), (("k_T",), K3)):
                o = open_fill(name)
                for t in range(3):
                    ins = pe.transpose(o[:, t * P:(t + 1) * P], src[:, t, 0:P], ident)
                close_fill(ins)
            for c in range(2):
                o = open_fill(("v_T", c))
                for t in range(3):
                    ins = pe.transpose(o[:, t * P:(t + 1) * P], V3[:, t, c * P:(c + 1) * P], ident)
                close_fill(ins)
            o = open_fill(("yM_T",))
            for j in range(2):
                for tt in range(TT):
                    ins = pe.transpose(o[:, j * S + tt * P:j * S + (tt + 1) * P],
                                       YM[:, tt, j * P:(j + 1) * P], ident)
            close_fill(ins)
            for j in range(JOB_AT["out2", 0, 0] - 4, JOB_AT["out2", 0, 0]):
                wait_job_out(pe, JOBS[j])

            def pairs(name_of, size=4):
                for g in range(NM // size):
                    o = open_fill(name_of(g))
                    for n in range(size):
                        m, c, h = PLACES[size * g + n]
                        yield o[:, n * P:(n + 1) * P], m, c, h, n == size - 1

            both = ARENA[:, 2048:2048 + 2 * 1536].rearrange("p (q w) -> p q w", q=2)
            for kind, src in (("by_b", A3), ("by_k", K3)):
                for g in range(6):
                    o = open_fill((kind, g))
                    for n in range(2):
                        m, c, h = PLACES[2 * g + n]
                        pb, t, c0 = HD * (h % 2), h // 2, c * P
                        a, b = src[pb:pb + HD, t, :], both[pb:pb + HD, :, t * S:(t + 1) * S]
                        oo = o[:, n * S:(n + 1) * S].rearrange("p (q w) -> p q w", q=2)
                        pe.matmul(oo[:, :, HD:P], a[:, c0:c0 + P], b[:, :, c0 + HD:c0 + P], start=True, stop=True)
                        ins = pe.matmul(oo[0:HD, :, 0:HD], a[:, c0:c0 + HD], b[:, :, c0:c0 + HD], start=True, stop=True)
                    close_fill(ins)

            def removed_values():
                for g in range(6):
                    wait_fill_out(pe, ("by_k", g))
                for c in range(2):
                    wait_fill_out(pe, ("v_T", c))
                for c in range(2):
                    o = open_fill(("av", c))
                    for h in range(RH):
                        ins = pe.matmul(o[:, h * HD:(h + 1) * HD], PM[:, matrix(c, h), :],
                                        VT[:, c, h * HD:(h + 1) * HD], start=True, stop=True)
                    close_fill(ins)

            def product(name, left, right, needs):
                for g in range(3):
                    for need in needs(g):
                        wait_fill_out(pe, need)
                    o = open_fill(name(g))
                    for n in range(4):
                        m = 4 * g + n
                        ins = pe.matmul(o[:, n * P:(n + 1) * P], left[:, m, :], right[:, m, :],
                                        start=True, stop=True)
                    close_fill(ins)

            def pair_rows(t):
                return prm2("pair_rows", t * P, P)[0:RH, :]

            def delta_rule_part(lv):
                if lv == 2:
                    head_sums([("gq_ss", 0), ("gq_ss", 1)], GKB, "gdn_squares", 1)
                elif lv == 4:
                    head_sums([("gk_ss", 0), ("gk_ss", 1)], GKB, "gdn_squares", 2)
                elif lv == 6:
                    pe.wait_ge(sem("gdn_rows"), 1)
                    for o, t, last in tile_slots([("beta", 0), ("beta", 1)]):
                        ins = pe.matmul(o, pair_rows(t), SM8[0:RH, 0:S], start=True, stop=True)
                        if last:
                            close_fill(ins)
                    for name, a in ((("g_e",), 512 + P), (("g_k",), 768)):
                        o = open_fill(name)
                        for t in range(3):
                            ins = pe.matmul(o[:, t * P:(t + 1) * P], pair_rows(t), SM8[0:RH, a:a + P],
                                            start=True, stop=True)
                        close_fill(ins)

            def inverse(fam):
                for o, m, c, h, last in pairs(lambda g: (fam, "t0", g)):
                    n = PLACES.index((m, c, h))
                    if n % 4 == 0:
                        pe.wait_ge(sem("inverse_started"), n // 4 + (1 if fam == "rw" else 4))
                    ins = pe.transpose(o, TTM[:, m, :], ident)
                    if last:
                        close_fill(ins)
                if fam == "rw":
                    removed_values()
                for lv in range(1, LEVELS):
                    if fam == "rw":
                        delta_rule_part(lv)
                    product(lambda g: (fam, "p", lv, g), AT, TM,
                            lambda g: [(fam, "t0", g) if lv == 1 else (fam, "t", lv - 1, g)])
                    before = lambda g: [(fam, "p", lv, g)] + ([(fam, "tt", lv - 1, g)] if lv > 1 else [])
                    if lv < LEVELS - 1:
                        product(lambda g: (fam, "t", lv, g), TTM, PM, before)
                    product(lambda g: (fam, "tt", lv, g), PM, TTM, before)
                for g in range(3):
                    wait_fill_out(pe, (fam, "tt", LEVELS - 1, g))

            def solve(name, rhs, c):
                o = open_fill(name)
                for h in range(RH):
                    ins = pe.matmul(o[:, h * HD:(h + 1) * HD], TTM[:, matrix(c, h), :],
                                    rhs[:, c, h * HD:(h + 1) * HD], start=True, stop=True)
                close_fill(ins)

            def place(h):
                return HD * (h % 2), h // 2

            inverse("rw")
            wait_fill_out(pe, ("av", 0))
            solve(("sa", 0), RR, 0)
            wait_fill_out(pe, ("sa", 0))
            wait_fill_out(pe, ("b_T",))
            wait_fill_out(pe, ("k_T",))
            o = open_fill(("st",))
            for h in range(RH):
                pb, t = place(h)
                cols = slice(h * HD, (h + 1) * HD)
                so = o[pb:pb + HD, t * HD:(t + 1) * HD]
                pe.matmul(so, BTk[:, cols], SA[:, 0, cols], start=True, stop=False)
                ins = pe.matmul(so, KTk[:, cols], VT[:, 0, cols], start=False, stop=True)
            close_fill(ins)
            wait_fill_out(pe, ("beta", 1))
            wait_fill_out(pe, ("g_k",))
            for c in range(2):
                o = open_fill(("gv_T", c))
                for t in range(3):
                    ins = pe.transpose(o[:, t * P:(t + 1) * P], GV[:, t, c * P:(c + 1) * P], ident)
                close_fill(ins)
            o = open_fill(("gk_T",))
            for t in range(3):
                ins = pe.transpose(o[:, t * P:(t + 1) * P], GKD[:, t, :], ident)
            close_fill(ins)
            wait_fill_out(pe, ("st",))
            for par in range(2):
                o = open_fill(("r1", par))
                for h in range(par, RH, 2):
                    pb, t = place(h)
                    ins = pe.matmul(o[:, t * HD:(t + 1) * HD], KK[pb:pb + HD, t, P:S], ST[pb:pb + HD, t, :],
                                    start=True, stop=True)
                close_fill(ins)
            wait_fill_out(pe, ("r1", 0))
            wait_fill_out(pe, ("r1", 1))
            solve(("sa", 1), RR, 1)
            wait_fill_out(pe, ("sa", 1))

            def outputs(names, parts, state_q, state):
                for o, t, last in tile_slots(names):
                    for h in (2 * t, 2 * t + 1):
                        pb = HD * (h % 2)
                        for c in range(2):
                            mms = [(a[:, c, h * HD:(h + 1) * HD], b[:, matrix(c, h), :]) for a, b in parts]
                            if c:
                                mms.append((state[pb:pb + HD, t, :], state_q(t)[pb:pb + HD, :]))
                            for n, (a, b) in enumerate(mms):
                                ins = pe.matmul(o[pb:pb + HD, c * P:(c + 1) * P], a, b,
                                                start=(n == 0), stop=(n == len(mms) - 1))
                    if last:
                        close_fill(ins)

            outputs([("y", 0), ("y", 1)], [(SA, MB), (VT, MK)], lambda t: R3[:, t, P:S], ST)
            wait_fill_out(pe, ("y", 0))
            wait_fill_out(pe, ("y", 1))
            head_sums([("gn_mean", 0), ("gn_mean", 1)], E3, "rw_squares", 2)
            head_sums([("gn_var", 0), ("gn_var", 1)], T3, "rw_squares", 3)

            for o, m, c, h, last in pairs(lambda g: ("decay", g)):
                rows = SM8[0:RH, S + c * P:S + (c + 1) * P]
                pe.matmul(o, row_of(h, P, 1)[0:RH], rows, start=True, stop=False)
                ins = pe.matmul(o, rows, row_of(h, P, -1)[0:RH], start=False, stop=True)
                if last:
                    close_fill(ins)
            for kind, t_src in (("gkk", GKB), ("gqk", GQ)):
                for o, m, c, h, last in pairs(lambda g: (kind, g), 3):
                    pb, t = place(h)
                    ins = pe.matmul(o, GK[pb:pb + HD, t, c * P:(c + 1) * P], t_src[pb:pb + HD, t, c * P:(c + 1) * P],
                                    start=True, stop=True)
                    if last:
                        close_fill(ins)
            inverse("gd")
            for name in (("gv_T", 0), ("gv_T", 1), ("gk_T",)):
                wait_fill_out(pe, name)
            solve(("du", 0), GVT, 0)
            wait_fill_out(pe, ("du", 0))
            o = open_fill(("gst",))
            for h in range(RH):
                pb, t = place(h)
                cols = slice(h * HD, (h + 1) * HD)
                ins = pe.matmul(o[pb:pb + HD, t * HD:(t + 1) * HD], GKT[:, cols], SA[:, 0, cols],
                                start=True, stop=True)
            close_fill(ins)
            wait_fill_out(pe, ("gst",))
            for par in range(2):
                o = open_fill(("gr1", par))
                for h in range(par, RH, 2):
                    pb, t = place(h)
                    ins = pe.matmul(o[:, t * HD:(t + 1) * HD], GKE[pb:pb + HD, t, :], ST[pb:pb + HD, t, :],
                                    start=True, stop=True)
                close_fill(ins)
            wait_fill_out(pe, ("gr1", 0))
            wait_fill_out(pe, ("gr1", 1))
            solve(("du", 1), GVT, 1)
            wait_fill_out(pe, ("du", 1))
            for g in range(4):
                wait_fill_out(pe, ("gqk", g))
            outputs([("o", 0), ("o", 1)], [(SA, GAT)], lambda t: GQD[:, t, :], ST)
            head_sums([("o_ss", 0), ("o_ss", 1)], GQ, "gdn_squares", 3)

            wait_fill_out(pe, ("yM_T",))
            for b in range(4):
                pe.wait_ge(sem(f"fill_out{b}"), sum(bank == b for _, bank in FILLS))
            for dc in range(2):
                t_jobs_split("out2", dc, OVER_HN, OVER_HT, late=(dc == 0))
            norm_transposes(3)
            for i in range(FF2_CHUNKS):
                f_jobs_split("ffn2", i)
            down("down2", HID2_HIGH, HID2_LOW, FF2_KT,
                 lambda t: pe.wait_ge(sem("hidden_split"), FF1_CHUNKS + t // 2 + 1), "down2")

        def conv_weights(n):
            if n < 8:
                return [prm("conv_w", 8 * tap + n) for tap in range(4)], prm("conv_b", n)
            return [prm2("g_conv", 9 * tap + n - 8) for tap in range(4)], 0.0

        def conv_tile(n):
            if n < 8:
                return ("in1", 1 + n // 4, (n % 4) // 2), n % 2, XBC[:, n, :]
            m = n - 8
            return ("in2", 4 + m // 4, (m % 4) // 2), m % 2, GZ[:, m, :]

        STAGED = {job: n for n, job in enumerate(
            [("in1", i, j) for i in (1, 2) for j in range(2)]
            + [("in2", 1, 0), ("in2", 1, 1), ("in2", 2, 0), ("in2", 2, 1), ("in2", 3, 0), ("in2", 3, 1)]
            + [("in2", 4, 0), ("in2", 4, 1), ("in2", 5, 0), ("in2", 5, 1), ("in2", 6, 0)])}

        @block.scalar
        def _(act):
            act.dma_start(X[:, :, :], x.rearrange("b (t p) d -> p (b t) d", p=P)).then_inc(sem("x_in"), 16)
            act.dma_start(CST[:, 0:P], consts[:, 0:P]).then_inc(sem("params_in"), 16)
            act.dma_start(PRM[:, :], params).then_inc(sem("params_in"), 16)
            act.dma_start(TBL[0:32, :], tables).then_inc(sem("consts_in"), 16)
            act.dma_start(RELB[:, :], rel_bias).then_inc(sem("consts_in"), 16)
            act.dma_start(CST[:, P:NC], consts[:, P:NC]).then_inc(sem("consts_in"), 16)
            act.dma_start(NF[:, :], norm_final).then_inc(sem("late_in"), 16)
            act.dma_start(POS[:, :], positions).then_inc(sem("late_in"), 16)

            def root(n, src, dst, ready, done):
                act.wait_ge(sem(ready), n)
                act.activation(dst, src, ACT.Sqrt).then_inc(sem(done), 1)

            def norm_stats(m):
                for tt in range(TT):
                    if m == 0:
                        act.wait_ge(sem("x_in"), 16)
                    elif m in (1, 4):
                        for dc in range(2):
                            wait_job_out(act, ("out1" if m == 1 else "out2", dc, tt))
                    elif m == 2:
                        for dc in range(2):
                            wait_fill_out(act, ("down1", 2 * tt + dc))
                    else:
                        act.wait_ge(sem("x2_ready"), tt + 1)
                    junk = SQA[:, tt, :] if m == 1 else SQB[:, tt, :] if m == 4 else HN[:, tt, :]
                    act.activation(junk, X[:, tt, :], ACT.Square, accum_out=SUMSQ[:, tt:tt + 1])\
                        .then_inc(sem("sums_ready"), 1)
                root(m + 1, MEANSQ, RMS, "means_ready", "roots_ready")
                if m != 2:
                    act.wait_ge(sem("rstd_ready"), m + 1)
                    act.activation(HN[:, 1, :], X[:, 1, :], ACT.Copy, scale=RSTD[:, 1:2]).then_inc(sem("hn1_ready"), 1)

            def split_high(k):
                if k >= len(PIECES):
                    return
                kind, i, _ = PIECES[k]
                slot, turn = weight_slots(kind, i)
                act.wait_ge(sem(f"weights_in{slot}"), 16 * turn)
                if k >= 2:
                    wait_piece_used(act, k - 2)
                act.activation(piece_parts(k)[0], piece_source(k), ACT.Copy).then_inc(sem("pieces_high"), 1)

            def norm_gains(n):
                gain = [prm("norm_mix", 0, 8), prm("norm_ffn", 0, 8), prm("ln_mix", 0, 8), prm("ln_ffn", 0, 8)][n]
                high = (FIRST_HIGH, OVER_HT, IN2_HIGH, OVER_HT)[n]
                for b in range(4):
                    o = fill_arrived(act, ("norm", n, b))
                    for j in range(2):
                        k = 2 * b + j
                        ins = act.activation(high[:, k, :], o[:, j * S:(j + 1) * S], ACT.Copy, scale=gain[:, k:k + 1])
                    ins.then_inc(sem("operand_high"), 1)

            def stage(job, reader):
                o = job_arrived(act, job)
                n = len(stage_readers)
                if n >= 2:
                    act.wait_ge(sem(stage_readers[n - 2][0]), stage_readers[n - 2][1])
                stage_readers.append(reader)
                act.activation(STG[:, n % 2, :], o[:, :], ACT.Copy)
                return o

            stage_readers = []

            def conv_tap(n, release=True):
                job, half, _ = conv_tile(n)
                w, bias = conv_weights(n)
                if n < 8 and half == 0:
                    split_high(2 * job[1] + job[2] + 2)
                o = stage(job, ("conv_sum", min(n + 2, 17))) if half == 0 else job_bank(job)
                if n >= 2:
                    act.wait_ge(sem("conv_done"), n - 1)
                src = o[:, half * S:(half + 1) * S]
                if n < 8:
                    ins = act.activation(ACC[:, n % 2, :], src, ACT.Identity, bias=bias, scale=w[3])
                else:
                    ins = act.activation(ACC[:, n % 2, :], src, ACT.Copy, scale=w[3])
                ins.then_inc(sem("conv_tap"), 1)
                if half and release:
                    act.wait_ge(sem("conv_tap"), n + 1)
                    act.sem_inc(sem(f"job_out{JOB_AT[job] % 4}"), 1)

            def conv_tanh(n):
                act.wait_ge(sem("conv_sum"), n + 1)
                act.activation(TH[:, n % 2, :], ACC[:, n % 2, :], ACT.Tanh).then_inc(sem("conv_tanh"), 1)

            def convs(first, last):
                for n in range(first, last):
                    conv_tap(n)
                    if n > first:
                        conv_tanh(n - 1)
                conv_tanh(last - 1)

            def take(job, dst, scale=1.0):
                o = job_arrived(act, job)
                job_out(act.activation(dst, o[:, :], ACT.Copy, scale=scale), job)

            def take_fill(name, dst, n, scale=1.0, rows=P):
                o = fill_arrived(act, name)
                fill_out(act.activation(dst, o[0:rows, 0:n], ACT.Copy, scale=scale), name)

            def flat(t):
                return t.rearrange("p a b -> p (a b)")

            def softplus_parts(k, t):
                act.wait_ge(sem("sp_minus_abs"), k + 1)
                act.activation(t, t, ACT.Exp).then_inc(sem("sp_exp"), 1)
                act.wait_ge(sem("sp_exp1"), k + 1)
                act.activation(t, t, ACT.Ln).then_inc(sem("sp_ln"), 1)

            norm_stats(0)
            split_high(0)
            norm_gains(0)
            split_high(1)
            split_high(2)
            split_high(3)
            act.wait_ge(sem("params_halved"), 1)
            softplus_parts(0, SPT)
            act.activation(EALOG[0:NH, :], prm("a_log")[0:NH, :], ACT.Exp).then_inc(sem("a_ready"), 1)
            convs(0, 8)
            split_high(8)
            take(("in1", 3, 0), flat(CQ1[:, 0:2, :]), 0.125)
            for g in range(2):
                take_fill(("cb", g), CB[:, g, :], 384)
            for i, dst, scale in ((4, flat(CK1[:, 0:2, :]), 1.0), (5, CV1[:, 0, :], 1.0),
                                  (6, flat(DQ1[:, 0:2, :]), 0.125), (7, flat(BQ1[:, 0:2, :]), 0.125),
                                  (8, flat(BK1[:, 0:2, :]), 1.0), (9, BV1[:, 0, :], 1.0)):
                split_high(2 * i + 1)
                split_high(2 * i + 2)
                take(("in1", i, 0), dst, scale)
            split_high(21)
            for tt in range(TT):
                o = job_arrived(act, ("in1", 10, tt))
                act.activation(SILZ[:, tt, :], o[:, :], ACT.Tanh, scale=0.5).then_inc(sem("z_tanh"), 1)

            def exps(u):
                br, h = ALL_UNITS[u]
                act.wait_ge(sem("scores_read"), u + 1)
                if u >= 2:
                    if ALL_UNITS[u - 2][0] == 0:
                        act.wait_ge(sem("mix_by_pool"), u - 1 - attention_units(u - 1))
                    else:
                        act.wait_ge(sem("probsT_written"), attention_units(u - 1))
                    act.wait_ge(sem("heads_done"), u - 1)
                s, p = SB_[:, u % 2, :], PB_[:, u % 2, :]
                if br == 0:
                    act.activation(p, s, ACT.Exp).then_inc(sem("probs_ready"), 1)
                    return
                if br == 3:
                    act.activation(ESINK[:, u % 2, :], NEGM[:, u % 2, :], ACT.Exp, bias=prm("sinks", h))
                for tt, (c0, c1) in enumerate(((0, P), (P, 384))):
                    ins = act.activation(p[:, c0:c1], s[:, c0:c1], ACT.Exp, bias=NEGM[:, u % 2, tt:tt + 1],
                                         scale=-1.0, accum_out=RSUM[:, u % 2, tt:tt + 1])
                ins.then_inc(sem("probs_ready"), 1)

            def take_probs_T(u):
                if ALL_UNITS[u][0] == 0:
                    return
                act.wait_ge(sem("probsT_written"), attention_units(u + 1))
                if u >= 2:
                    act.wait_ge(sem("heads_written"), u - 1)
                act.activation(PT_[:, u % 2, :], BK[6][:, 0:384], ACT.Copy).then_inc(sem("probsT_by_act"), 1)

            act.wait_ge(sem("table_stored"), 16)
            for u in range(NU + 1):
                if u < NU:
                    exps(u)
                if u >= 1:
                    take_probs_T(u - 1)
                if u == 18:
                    act.wait_ge(sem("ya_gated"), 1)
                    for tt in range(TT):
                        act.activation(SQ1[:, tt, :], YB[0][:, tt, :], ACT.Square,
                                       accum_out=SUMSQ[:, tt:tt + 1]).then_inc(sem("ya_sums"), 1)
                if u == 20:
                    root(1, MEANSQ, RMS, "ya_means", "ya_roots")
                if u == 26:
                    act.wait_ge(sem("heads_done"), 24)
                    split_high(PIECE_AT["branch", 0, 0])
                if u < NU and u % 2:
                    i, tt = divmod(u // 2, 2)
                    o = job_arrived(act, ("gate", i, tt))
                    job_out(act.activation(GT[:, tt, i * 512:(i + 1) * 512], o[:, :], ACT.Tanh, scale=0.5),
                            ("gate", i, tt))
            act.dma_start(P2[:, 0:NP2], params2).then_inc(sem("params2_in"), 16)

            act.wait_ge(sem("heads_done"), NU)

            def take_y_T(i):
                for b in range(2):
                    o = fill_arrived(act, ("y_T", i, b))
                    if i >= 2:
                        job_arrived(act, ("branch", i - 2, 3))
                    for j in range(2):
                        ins = act.activation(YT_HIGH[i % 2][:, 2 * b + j, :], o[:, j * S:(j + 1) * S], ACT.Copy,
                                             scale=prm("ssm_norm", 2 * b + j) if i == 0 else 1.0)
                    ins.then_inc(sem("y_high"), 1)

            take_y_T(0)
            split_high(PIECE_AT["branch", 0, 1])
            take_y_T(1)
            for i in range(4):
                split_high(PIECE_AT["branch", i, 0] + 2)
                split_high(PIECE_AT["branch", i, 0] + 3)
                if i < 2:
                    take_y_T(i + 2)
            for b in range(4):
                o = fill_arrived(act, ("mix_T", b))
                act.activation(flat(OVER_HT[:, 2 * b:2 * b + 2, :]), o[:, :], ACT.Copy)\
                    .then_inc(sem("operand_high"), 1)
            out1 = PIECE_AT["out1", 0, 0]
            for k in range(out1 + 2, out1 + 5):
                split_high(k)
            norm_stats(1)
            norm_gains(1)
            split_high(out1 + 5)
            for c in range(FF1_CHUNKS):
                k = PIECE_AT["ffn1", c, 0]
                split_high(k + 2)
                o = job_arrived(act, ("ffn1", c, 0))
                if c >= 2:
                    wait_job_out(act, ("ffn1", c - 2, 1))
                act.activation(SG[:, c % 2, :], o[:, :], ACT.Tanh, scale=0.5).then_inc(sem("ffn_tanh"), 1)
                split_high(k + 3)
                act.wait_ge(sem("hidden_ready"), c + 1)
                act.activation(flat(HID1_HIGH[:, 2 * c:2 * c + 2, :]), HF1[:, c % 2, :], ACT.Copy)\
                    .then_inc(sem("hidden_high"), 1)
            in2 = PIECE_AT["in2", 0, 0]
            for k in range(PIECE_AT["down1", 0, 0] + 2, in2):
                split_high(k)
            norm_stats(2)
            split_high(in2)
            norm_stats(3)
            split_high(in2 + 1)
            norm_gains(2)
            split_high(in2 + 2)
            split_high(in2 + 3)

            o = job_arrived(act, ("in2", 0, 0))
            act.activation(flat(CQF[:, 0:2, :]), o[:, :], ACT.Copy)
            job_out(act.activation(flat(SQM[:, 0:2, :]), o[:, :], ACT.Square), ("in2", 0, 0))
            o = job_arrived(act, ("in2", 0, 1))
            act.activation(CQF[:, 2, :], o[:, 0:S], ACT.Copy)
            act.activation(SQM[:, 2, :], o[:, 0:S], ACT.Square)
            job_out(act.activation(flat(KR), o[:, S:S + TT * ROPE], ACT.Copy), ("in2", 0, 1))
            def shift_tiles(i, j, tiles):
                shifts[0] += 1
                if i == 1:
                    split_high(in2 + 2 * i + j + 2)
                o = job_arrived(act, ("in2", i, j))
                k = len(stage_readers)
                act.wait_ge(sem(stage_readers[k - 2][0]), stage_readers[k - 2][1])
                stage_readers.append(("shift_by_dve", shifts[0]))
                n = len(tiles) * S
                act.activation(STG[:, k % 2, 0:n], o[:, 0:n], ACT.Copy)
                for n, rt in enumerate(tiles):
                    ins = act.activation(RZ[:, rt, :], o[:, n * S:(n + 1) * S], ACT.Copy, scale=one_minus_mu[:, rt:rt + 1])
                job_out(ins, ("in2", i, j))

            shifts = [0]

            act.wait_ge(sem("params2_ready"), 1)
            act.wait_ge(sem("angles_ready"), 1)
            act.activation(SIN[:, :, :], SIN[:, :, :], ACT.Sin)
            act.activation(COS[:, :, :], COS[:, :, :], ACT.Sin).then_inc(sem("sincos_ready"), 1)
            act.activation(EALOG[0:RH, :], prm2("g_alog")[0:RH, :], ACT.Exp).then_inc(sem("a_ready"), 1)
            shift_tiles(1, 0, (0, 1))
            shift_tiles(1, 1, (2, 3))
            act.wait_ge(sem("shift_by_dve"), 1)
            act.activation(LO[0:HD, 0, :], LO[0:HD, 0, :], ACT.Tanh)
            act.activation(LO[:, 1, :], LO[:, 1, :], ACT.Tanh, scale=0.5).then_inc(sem("lora_by_act"), 1)
            root(1, SQM[:, :, :], SQM[:, :, :], "latent_means", "latent_roots")
            shift_tiles(2, 0, (4, 5))
            shift_tiles(2, 1, (6, 7))
            for n, (dst, bias, tiles) in enumerate(((LW, "w0", (0, 1)), (LW, "w0", (2,)), (A3, "a0", (0, 1)), (A3, "a0", (2,)))):
                o = fill_arrived(act, ("lora", n))
                for j, t in enumerate(tiles):
                    ins = act.activation(dst[:, t, :], o[:, j * S:(j + 1) * S], ACT.Tanh, scale=0.5, bias=prm2(bias, t))
                fill_out(ins, ("lora", n))
            take_fill(("rw_g", 0), flat(GG[:, 0:2, :]), 512, 0.5)
            take_fill(("rw_g", 1), GG[:, 2, :], S, 0.5)
            for tt in range(TT):
                take_fill(("mla_q", tt), flat(QM[:, tt * MH:(tt + 1) * MH, :]), MH * QK)
            act.wait_ge(sem("decay_sums"), 1)
            act.activation(EGC, G3[:, :, P + HD - 1], ACT.Exp)
            act.activation(E3[:, :, :], E3[:, :, :], ACT.Exp).then_inc(sem("decay_exp"), 1)
            root(1, QKSS, QKSS, "qk_means", "qk_roots")
            shift_tiles(3, 0, (8, 9))
            shift_tiles(3, 1, (10,))
            act.wait_ge(sem("beta_in"), 1)
            act.activation(BETA, BETA, ACT.Tanh, scale=0.5).then_inc(sem("beta_tanh"), 1)
            for n, dst in enumerate((QTm, KTm)):
                for b in range(2):
                    take_fill(("mla_T", 2 * n + b), flat(dst[0:QK, 2 * b:2 * b + 2, :]), 512, rows=QK)
            for u in range(NU, NU + MH + 1):
                if u < NU + MH:
                    exps(u)
                if u > NU:
                    take_probs_T(u - 1)
            root(1, T3[:, :, :], T3[:, :, :], "rw_means", "rw_roots")
            act.wait_ge(sem("alpha_ready"), 1)
            act.activation(E3[:, :, :], GM[:, :, :], ACT.Exp, scale=-1.0).then_inc(sem("decay_exp"), 1)
            act.wait_ge(sem("decay_exp"), 2)
            act.activation(GM[:, :, :], GM[:, :, :], ACT.Exp).then_inc(sem("decay_exp"), 1)
            convs(8, 12)
            convs(12, 16)
            conv_tap(16)
            conv_tanh(16)
            o = job_arrived(act, ("in2", 6, 0))
            act.activation(GGT[:, 0, :], o[:, S:2 * S], ACT.Tanh, scale=0.5).then_inc(sem("gg_tanh"), 1)
            o = job_arrived(act, ("in2", 6, 1))
            act.activation(flat(GGT[:, 1:3, :]), o[:, :], ACT.Tanh, scale=0.5).then_inc(sem("gg_tanh"), 1)
            take_fill(("b_T",), BTk, 384)
            take_fill(("k_T",), KTk, 384)
            for c in range(2):
                take_fill(("v_T", c), VT[:, c, :], 384)
            take_fill(("yM_T",), flat(YT2[:, 3:5, :]), 512)

            def take_t0(fam):
                for g in range(3):
                    take_fill((fam, "t0", g), flat(TM[:, 4 * g:4 * g + 4, :]), 512)

            take_t0("rw")
            act.wait_ge(sem("sp_minus_abs"), 2)
            act.activation(GSPT, GSPT, ACT.Exp).then_inc(sem("sp_exp"), 1)
            root(1, GTMP[:, :, :], GTMP[:, :, :], "gdn_means", "gdn_roots")
            act.wait_ge(sem("sp_exp1"), 2)
            act.activation(GSPT, GSPT, ACT.Ln).then_inc(sem("sp_ln"), 1)
            act.wait_ge(sem("gdn_cumulated"), 1)
            act.activation(EGCUM, GCUM, ACT.Exp)
            act.activation(EKEND, GCUM[:, 0:P], ACT.Exp, bias=GCUM[:, P - 1:P], scale=-1.0)\
                .then_inc(sem("gdn_rows"), 1)
            root(2, GTMP[:, :, :], GTMP[:, :, :], "gdn_means", "gdn_roots")
            take_fill(("sa", 0), SA[:, 0, :], 384)
            for c in range(2):
                take_fill(("gv_T", c), GVT[:, c, :], 384)
            take_fill(("gk_T",), GKT, 384)
            take_fill(("sa", 1), SA[:, 1, :], 384)
            take_fill(("y", 0), flat(E3[:, 0:2, :]), 512)
            take_fill(("y", 1), E3[:, 2, :], S)
            root(2, T3[:, :, :], T3[:, :, :], "rw_means", "rw_roots")
            for g in range(3):
                wait_fill_out(act, ("decay", g))
                m = GAT[:, 4 * g:4 * g + 4, :]
                act.activation(m, m, ACT.Exp).then_inc(sem("gdn_decay_exp"), 1)
            take_t0("gd")
            act.wait_ge(sem("y2_ready"), 1)
            out2 = PIECE_AT["out2", 0, 0]
            split_high(out2)
            split_high(out2 + 1)
            wait_fill_out(act, ("yM_T",))
            act.activation(OVER_HN[:, 0:5, :], YT2[:, 0:5, :], ACT.Copy).then_inc(sem("y2_high"), 1)
            take_fill(("du", 0), SA[:, 0, :], 384)
            take_fill(("du", 1), SA[:, 1, :], 384)
            take_fill(("o", 0), flat(GKB[:, 0:2, :]), 512)
            take_fill(("o", 1), GKB[:, 2, :], S)
            root(3, GTMP[:, :, :], GTMP[:, :, :], "gdn_means", "gdn_roots")

            for t in range(3):
                act.wait_ge(sem("y2_ready"), 2 + t)
                act.activation(OVER_HN[:, 5 + t, :], YT2[:, 5 + t, :], ACT.Copy).then_inc(sem("y2_high"), 1)
            for k in range(out2 + 2, out2 + 5):
                split_high(k)
            norm_stats(4)
            norm_gains(3)
            split_high(out2 + 5)

            def hidden2_high(q):
                act.wait_ge(sem("hidden_ready"), FF1_CHUNKS + q + 1)
                act.activation(flat(HID2_HIGH[:, 2 * q:2 * q + 2, :]), HF2[:, q % 2, :], ACT.Copy)\
                    .then_inc(sem("hidden_high"), 1)

            for q in range(2 * FF2_CHUNKS):
                c, j = divmod(q, 2)
                split_high(PIECE_AT["ffn2", c, j] + 2)
                o = job_arrived(act, ("ffn2", c, j))
                if q >= 2:
                    act.wait_ge(sem("hidden_split"), FF1_CHUNKS + q - 1)
                job_out(act.activation(HF2[:, q % 2, :], o[:, :], ACT.Relu), ("ffn2", c, j))
                if q:
                    hidden2_high(q - 1)
            hidden2_high(q)
            for k in range(PIECE_AT["down2", 0, 0] + 2, len(PIECES)):
                split_high(k)

        @block.vector
        def _(dve):
            steps = [0]

            def link(ins):
                steps[0] += 1
                ins.then_inc(sem("dve_steps"), 1)
                dve.wait_ge(sem("dve_steps"), steps[0])

            def bc(ap, shape):
                return ap.to_broadcast(shape)

            def flat(t):
                return t.rearrange("p a b -> p (a b)")

            def norm_scale(m):
                dve.wait_ge(sem("sums_ready"), 2 * (m + 1))
                dve.tensor_scalar(MEANSQ, SUMSQ, 1.0 / D, EPS, ALU.mult, ALU.add).then_inc(sem("means_ready"), 1)
                dve.wait_ge(sem("roots_ready"), m + 1)
                dve.reciprocal(RSTD, RMS).then_inc(sem("rstd_ready"), 1)
                dve.wait_ge(sem("rstd_ready"), m + 1)
                for tt in range(TT):
                    if m == 2:
                        dve.scalar_tensor_tensor(out=X[:, tt, :], in0=X[:, tt, :], scalar=RSTD[:, tt:tt + 1],
                                                 in1=NF[:, :], op0=ALU.mult, op1=ALU.mult).then_inc(sem("x2_ready"), 1)
                    elif tt == 0:
                        dve.tensor_scalar(HN[:, 0, :], X[:, 0, :], RSTD[:, 0:1], None, ALU.mult)\
                            .then_inc(sem("hn0_ready"), 1)

            operand_parts = [0]

            def operand_high_arrived():
                operand_parts[0] += 1
                dve.wait_ge(sem("operand_high"), operand_parts[0])

            def split_low(k):
                if k >= len(PIECES):
                    return
                dve.wait_ge(sem("pieces_high"), k + 1)
                high, low = piece_parts(k)
                dve.tensor_tensor(low, piece_source(k), high.bitcast(F32), ALU.subtract)\
                    .then_inc(sem("pieces_split"), 1)

            def norm_gains(n):
                gain = [prm("norm_mix", 0, 8), prm("norm_ffn", 0, 8), prm("ln_mix", 0, 8), prm("ln_ffn", 0, 8)][n]
                high, low = {0: (FIRST_HIGH, FIRST_LOW), 2: (IN2_HIGH, IN2_LOW)}.get(n, (OVER_HT, OVER_HN))
                fill_arrived(dve, ("norm", n, 3))
                for b in range(4):
                    operand_high_arrived()
                    o = bank_of(("norm", n, b))
                    for j in range(2):
                        k = 2 * b + j
                        ins = dve.scalar_tensor_tensor(out=low[:, k, :], in0=o[:, j * S:(j + 1) * S],
                                                       scalar=gain[:, k:k + 1], in1=high[:, k, :].bitcast(F32),
                                                       op0=ALU.mult, op1=ALU.subtract)
                    fill_out(ins, ("norm", n, b))

            def take(job, dst, scale=1.0):
                o = job_arrived(dve, job)
                job_out(dve.tensor_scalar(dst, o[:, :], scale, None, ALU.mult), job)

            def softplus(k, src, t, dst):
                dve.scalar_tensor_tensor(out=t, in0=src, scalar=-1.0, in1=src, op0=ALU.mult, op1=ALU.min)\
                    .then_inc(sem("sp_minus_abs"), 1)
                dve.wait_ge(sem("sp_exp"), k + 1)
                dve.tensor_scalar(t, t, 1.0, None, ALU.add).then_inc(sem("sp_exp1"), 1)
                dve.wait_ge(sem("sp_ln"), k + 1)
                link(dve.scalar_tensor_tensor(out=dst, in0=src, scalar=0.0, in1=t, op0=ALU.max, op1=ALU.add))

            def conv_taps(n):
                job, half, _ = conv_tile(n)
                w, _ = conv_weights(n)
                if n < 8 and half == 0:
                    split_low(2 * job[1] + job[2] + 2)
                dve.wait_ge(sem("conv_tap"), n + 1)
                o = STG[:, STAGED[job] % 2, half * S:(half + 1) * S]
                for tap in (2, 1, 0):
                    d = 3 - tap
                    a = ACC[:, n % 2, d:S]
                    ins = dve.scalar_tensor_tensor(out=a, in0=o[:, 0:S - d], scalar=w[tap], in1=a,
                                                   op0=ALU.mult, op1=ALU.add)
                    if tap:
                        link(ins)
                ins.then_inc(sem("conv_sum"), 1)

            def conv_out(n):
                dve.wait_ge(sem("conv_tanh"), n + 1)
                dve.scalar_tensor_tensor(out=conv_tile(n)[2], in0=TH[:, n % 2, :], scalar=1.0, in1=ACC[:, n % 2, :],
                                         op0=ALU.add, op1=ALU.mult).then_inc(sem("conv_done"), 1)

            def convs(first, last):
                for n in range(first, last):
                    conv_taps(n)
                    if n > first:
                        conv_out(n - 1)
                conv_out(last - 1)

            dve.wait_ge(sem("params_in"), 16 * 2)
            dve.tensor_scalar(prm("conv_w", 0, 32), prm("conv_w", 0, 32), 0.5, None, ALU.mult)
            dve.tensor_scalar(prm("conv_b", 0, 8), prm("conv_b", 0, 8), 0.5, None, ALU.mult)
            dve.tensor_scalar(NSINK, prm("sinks", 0, 8), -1.0, None, ALU.mult)
            link(dve.tensor_scalar(negident[:, :], ident, -1.0, None, ALU.mult))
            norm_scale(0)
            split_low(0)
            norm_gains(0)
            dve.wait_ge(sem("consts_in"), 16 * 3)
            o = fill_arrived(dve, ("table",))
            fill_out(dve.tensor_tensor(PT_[0:2 * NH, 0, :], o[0:2 * NH, 0:384], tbl("table_mask")[0:2 * NH, :],
                                       ALU.add), ("table",))
            split_low(1)
            split_low(2)
            o = job_arrived(dve, ("in1", 0, 0))
            dve.tensor_copy(DK1, o[:, 0:S])
            job_out(dve.tensor_copy(DV1[:, :, :], o[:, S:2 * S].rearrange("p (t w) -> p t w", t=TT)), ("in1", 0, 0))
            split_low(3)
            o = job_arrived(dve, ("in1", 0, 1))
            dve.tensor_scalar(SPX[:, 0:S], o[0:NH, 0:S], prm("dt_bias")[0:NH, :], None, ALU.add)
            job_out(dve.tensor_scalar(SPX[:, S:2 * S], o[32:32 + NH, 0:S], prm("forget_bias")[32:32 + NH, :], -1.0,
                                      ALU.add, ALU.mult), ("in1", 0, 1))
            wait_job_out(dve, ("in1", 0, 0))
            wait_job_out(dve, ("in1", 0, 1))
            dve.sem_inc(sem("params_halved"), 1)
            softplus(0, SPX, SPT, SPX)
            dve.wait_ge(sem("a_ready"), 1)
            dve.tensor_scalar(DECAY, SPX[:, 0:S], EALOG[0:NH, :], -1.0, ALU.mult, ALU.mult).then_inc(sem("dt_ready"), 1)
            dve.wait_ge(sem("dt_ready"), 1)
            dve.tensor_tensor_scan(ACUM, ones[0:NH, :], DECAY, 0.0, ALU.mult, ALU.add)
            dve.tensor_tensor_scan(FCUM, ones[0:NH, :], SPX[:, S:2 * S], 0.0, ALU.mult, ALU.subtract)\
                .then_inc(sem("rows_ready"), 1)
            convs(0, 8)
            o = fill_arrived(dve, ("dt_T",))
            fill_out(dve.tensor_copy(DTT, o[:, 0:TT * NH]), ("dt_T",))
            split_low(8)
            split_low(9)
            take(("in1", 3, 1), flat(CQ1[:, 2:4, :]), 0.125)
            wait_fill_out(dve, ("dt_T",))
            for tt in range(TT):
                o = fill_arrived(dve, ("xs_T", tt))
                src = o[:, :].rearrange("p (h w) -> p h w", h=NH)
                dst = [t[:, tt, :].rearrange("p (h w) -> p h w", h=NH) for t in (XDT, YB[0])]
                dve.tensor_tensor(dst[0], src, bc(DTT[:, tt * NH:(tt + 1) * NH].unsqueeze(2), [P, NH, HD]), ALU.mult)
                fill_out(dve.tensor_tensor(dst[1], src, bc(prm("d_skip", 0, NH).unsqueeze(2), [P, NH, HD]), ALU.mult),
                         ("xs_T", tt))
            for i, dst, scale in ((4, flat(CK1[:, 2:4, :]), 1.0), (5, CV1[:, 1, :], 1.0),
                                  (6, flat(DQ1[:, 2:4, :]), 0.125), (7, flat(BQ1[:, 2:4, :]), 0.125),
                                  (8, flat(BK1[:, 2:4, :]), 1.0), (9, BV1[:, 1, :], 1.0)):
                split_low(2 * i + 2)
                split_low(2 * i + 3)
                take(("in1", i, 1), dst, scale)
            for tt in range(TT):
                dve.wait_ge(sem("z_tanh"), tt + 1)
                o = job_bank(("in1", 10, tt))
                job_out(dve.scalar_tensor_tensor(out=SILZ[:, tt, :], in0=SILZ[:, tt, :], scalar=1.0, in1=o[:, :],
                                                 op0=ALU.add, op1=ALU.mult), ("in1", 10, tt))

            def bias_scores(u):
                br, h = ALL_UNITS[u]
                dve.wait_ge(sem("scores_written"), u + 1)
                if u >= 2:
                    dve.wait_ge(sem("probs_ready"), u - 1)
                o, s = BK[4 + u % 2], SB_[:, u % 2, :]
                if br == 0:
                    dve.tensor_tensor(s, o[:, 0:384], cst("ssd_mask"), ALU.add).then_inc(sem("scores_read"), 1)
                    return
                m = {1: BIAS[:, h, :], 2: cst("causal"), 3: BIAS[:, NH + h, :], 4: cst("mla_mask")}[br]
                init = NSINK[:, h:h + 1] if br == 3 else 3e38
                dve.tensor_tensor_reduce(s[:, 0:P], o[:, 0:P], m[:, P:S], -1.0, init, ALU.add, ALU.min,
                                         NEGM[:, u % 2, 0:1])
                dve.tensor_tensor_reduce(s[:, P:384], o[:, P:384], m, -1.0, init, ALU.add, ALU.min,
                                         NEGM[:, u % 2, 1:2]).then_inc(sem("scores_read"), 1)

            def finish_head(u):
                br, h = ALL_UNITS[u]
                dve.wait_ge(sem("heads_written"), u + 1)
                o = BK[7][:, (u % 2) * P:(u % 2 + 1) * P].rearrange("p (t w) -> p t w", t=TT)
                y = (YM if br == 4 else YB[br])[:, :, h * HD:(h + 1) * HD]
                if br == 0:
                    dve.tensor_tensor(y, o, y, ALU.add).then_inc(sem("heads_done"), 1)
                    return
                if br == 3:
                    link(dve.tensor_tensor(RSUM[:, u % 2, :], RSUM[:, u % 2, :], ESINK[:, u % 2, :], ALU.add))
                link(dve.reciprocal(RREC[:, u % 2, :], RSUM[:, u % 2, :]))
                dve.tensor_tensor(y, o, bc(RREC[:, u % 2, :].unsqueeze(2), [P, TT, HD]), ALU.mult)\
                    .then_inc(sem("heads_done"), 1)

            def normalise_ssd(u):
                if u == 17:
                    dve.wait_ge(sem("heads_done"), 16)
                    dve.scalar_tensor_tensor(out=flat(YB[0]), in0=flat(YB[0]), scalar=0.5, in1=flat(SILZ), op0=ALU.mult,
                                             op1=ALU.mult).then_inc(sem("ya_gated"), 1)
                elif u == 19:
                    dve.wait_ge(sem("ya_sums"), 2)
                    dve.tensor_scalar(MEANSQ, SUMSQ, 1.0 / BW, EPS, ALU.mult, ALU.add).then_inc(sem("ya_means"), 1)
                elif u == 21:
                    dve.wait_ge(sem("ya_roots"), 1)
                    link(dve.reciprocal(RSTD, RMS))
                    for tt in range(TT):
                        dve.tensor_scalar(YB[0][:, tt, :], YB[0][:, tt, :], RSTD[:, tt:tt + 1], None, ALU.mult)\
                            .then_inc(sem("ya_ready"), 1)

            for u in range(NU + 1):
                if u == 16:
                    dve.wait_ge(sem("bias_in"), 16)
                if u < NU:
                    bias_scores(u)
                if u >= 1:
                    finish_head(u - 1)
                if u >= 17:
                    normalise_ssd(u)
                if u == 27:
                    split_low(PIECE_AT["branch", 0, 0])

            def take_y_T(i):
                for b in range(2):
                    o = fill_arrived(dve, ("y_T", i, b))
                    dve.wait_ge(sem("y_high"), 2 * i + b + 1)
                    for j in range(2):
                        k = 2 * b + j
                        ins = dve.scalar_tensor_tensor(out=YT_LOW[i % 2][:, k, :], in0=o[:, j * S:(j + 1) * S],
                                                       scalar=prm("ssm_norm", k) if i == 0 else 1.0,
                                                       in1=YT_HIGH[i % 2][:, k, :].bitcast(F32),
                                                       op0=ALU.mult, op1=ALU.subtract)
                    fill_out(ins, ("y_T", i, b))

            take_y_T(0)
            split_low(PIECE_AT["branch", 0, 1])
            take_y_T(1)
            for i in range(4):
                for j in range(4):
                    dc, tt = divmod(j, 2)
                    job = ("branch", i, j)
                    if tt and (i, dc) != (3, 1):
                        split_low(PIECE_AT["branch", i, dc] + 2)
                    o = job_arrived(dve, job)
                    g = GT[:, tt, i * D + dc * 512:i * D + (dc + 1) * 512]
                    mix = HN[:, tt, dc * 512:(dc + 1) * 512]
                    n = 4 * i + j - 4
                    if n >= 2:
                        dve.wait_ge(sem("mixed_by_pool"), n - 1)
                    job_out(dve.scalar_tensor_tensor(out=TMP[:, n % 2, :] if i else mix, in0=g, scalar=1.0,
                                                     in1=o[:, :], op0=ALU.add, op1=ALU.mult), job)
                if i < 2:
                    take_y_T(i + 2)
            split_low(PIECE_AT["out1", 0, 1])
            fill_arrived(dve, ("mix_T", 3))
            for b in range(4):
                operand_high_arrived()
                fill_out(dve.tensor_tensor(flat(OVER_HN[:, 2 * b:2 * b + 2, :]), bank_of(("mix_T", b))[:, :],
                                           flat(OVER_HT[:, 2 * b:2 * b + 2, :]).bitcast(F32), ALU.subtract), ("mix_T", b))

            def add_to_x(o, tt, dc, scale):
                xs = X[:, tt, dc * 512:(dc + 1) * 512]
                return dve.scalar_tensor_tensor(out=xs, in0=o[:, :], scalar=scale, in1=xs, op0=ALU.mult, op1=ALU.add)

            def add_out(kind, scale):
                for dc in range(2):
                    split_low(PIECE_AT[kind, dc, 0] + 2)
                    if dc == 0:
                        split_low(PIECE_AT[kind, dc, 1] + 2)
                    for tt in range(TT):
                        o = job_arrived(dve, (kind, dc, tt))
                        job_out(add_to_x(o, tt, dc, scale), (kind, dc, tt))

            def add_down(kind, scale):
                for b in range(4):
                    o = fill_arrived(dve, (kind, b))
                    fill_out(add_to_x(o, b // 2, b % 2, scale), (kind, b))

            add_out("out1", 0.5)
            norm_scale(1)
            norm_gains(1)
            split_low(PIECE_AT["ffn1", 0, 1])

            def hidden_low(high, low, tiles, src, n):
                dve.wait_ge(sem("hidden_high"), n + 1)
                dve.tensor_tensor(flat(low[:, tiles, :]), src, flat(high[:, tiles, :]).bitcast(F32), ALU.subtract)\
                    .then_inc(sem("hidden_split"), 1)

            def hidden1_low(c):
                hidden_low(HID1_HIGH, HID1_LOW, slice(2 * c, 2 * c + 2), HF1[:, c % 2, :], c)

            for c in range(FF1_CHUNKS):
                split_low(PIECE_AT["ffn1", c, 0] + 2)
                dve.wait_ge(sem("ffn_tanh"), c + 1)
                sg = SG[:, c % 2, :]
                job_out(dve.scalar_tensor_tensor(out=sg, in0=sg, scalar=1.0, in1=job_bank(("ffn1", c, 0))[:, :],
                                                 op0=ALU.add, op1=ALU.mult), ("ffn1", c, 0))
                if c:
                    hidden1_low(c - 1)
                wait_job_out(dve, ("ffn1", c, 0))
                o = job_arrived(dve, ("ffn1", c, 1))
                dve.tensor_tensor(HF1[:, c % 2, :], sg, o[:, :], ALU.mult).then_inc(sem("hidden_ready"), 1)
                dve.wait_ge(sem("hidden_ready"), c + 1)
                dve.sem_inc(sem(f"job_out{JOB_AT['ffn1', c, 1] % 4}"), 1)
                split_low(PIECE_AT["ffn1", c, 0] + 3)
            hidden1_low(c)
            in2 = PIECE_AT["in2", 0, 0]
            for k in range(PIECE_AT["down1", 0, 0] + 2, in2):
                split_low(k)
            add_down("down1", 0.5)
            dve.wait_ge(sem("late_in"), 32)
            norm_scale(2)
            norm_scale(3)
            split_low(in2)
            norm_gains(2)
            split_low(in2 + 1)

            dve.wait_ge(sem("params2_in"), 16)
            for name, n, f in (("w0", 3, 0.5), ("a0", 3, 0.5), ("g_conv", 36, 0.5), ("o_norm", 1, 0.5),
                               ("q_qk", QK, QK ** -0.5)):
                link(dve.tensor_scalar(prm2(name, 0, n), prm2(name, 0, n), f, None, ALU.mult))
            dve.tensor_scalar(one_minus_mu[:, :], prm2("mu", 0, 11), -1.0, 1.0, ALU.mult, ALU.add)\
                .then_inc(sem("params2_ready"), 1)
            link(dve.tensor_copy(POSF, POS[:, :]))
            for tt in range(TT):
                link(dve.tensor_scalar(SIN[:, tt, :], prm2("inv_freq", 0, 16), POSF[:, tt:tt + 1], None, ALU.mult))
            turns, ang = flat(COS), flat(SIN)
            link(dve.tensor_scalar(turns, ang, 0.15915494309189535, ROUND, ALU.mult, ALU.add))
            link(dve.tensor_scalar(turns, turns, -ROUND, None, ALU.add))
            for part in (TWO_PI_A, TWO_PI_B, TWO_PI_C):
                link(dve.scalar_tensor_tensor(out=ang, in0=turns, scalar=-part, in1=ang, op0=ALU.mult, op1=ALU.add))
            link(dve.tensor_scalar(ang, ang, 3.1415925, -3.1415925, ALU.min, ALU.max))
            link(dve.scalar_tensor_tensor(out=turns, in0=ang, scalar=-1.0, in1=ang, op0=ALU.mult, op1=ALU.max))
            dve.tensor_scalar(turns, turns, -1.0, 1.5707963267948966, ALU.mult, ALU.add)\
                .then_inc(sem("angles_ready"), 1)

            def shift_tiles(i, j, tiles):
                if i == 1:
                    split_low(in2 + 2 * i + j + 2)
                wait_job_out(dve, ("in2", i, j))
                o = STG[:, STAGED["in2", i, j] % 2, :]
                for n, rt in enumerate(tiles):
                    z = RZ[:, rt, 1:S]
                    ins = dve.scalar_tensor_tensor(out=z, in0=o[:, n * S:(n + 1) * S - 1], scalar=prm2("mu", rt), in1=z,
                                                   op0=ALU.mult, op1=ALU.add)
                ins.then_inc(sem("shift_by_dve"), 1)

            def squares(m, dst, name):
                dve.tensor_tensor(dst[:, :, :], m[:, :, :], m[:, :, :], ALU.mult).then_inc(sem(name), 1)

            def means(names, dst, scale, eps, done):
                for name, a, b in zip(names, (0, 2), (2, 3)):
                    o = fill_arrived(dve, name)
                    ins = dve.tensor_scalar(flat(dst[:, a:b, :]), o[:, 0:(b - a) * S], scale, eps, ALU.mult, ALU.add)
                    fill_out(ins, name)
                    wait_fill_out(dve, name)
                dve.sem_inc(sem(done), 1)

            split_low(in2 + 2)
            split_low(in2 + 3)
            shift_tiles(1, 0, (0, 1))
            shift_tiles(1, 1, (2, 3))
            dve.wait_ge(sem("lora_by_act"), 1)
            dve.tensor_scalar(LO[:, 1, :], LO[:, 1, :], 1.0, None, ALU.add).then_inc(sem("lora_by_dve"), 1)
            o = fill_arrived(dve, ("mla_ss",))
            dve.tensor_scalar(SQM[:, 0, :], o[:, 0:S], 1.0 / 256, EPS, ALU.mult, ALU.add)
            link(dve.tensor_scalar(SQM[:, 2, :], o[:, S:2 * S], 1.0 / 128, EPS, ALU.mult, ALU.add))
            fill_out(dve.tensor_copy(SQM[:, 1, :], SQM[:, 0, :]), ("mla_ss",))
            wait_fill_out(dve, ("mla_ss",))
            dve.sem_inc(sem("latent_means"), 1)
            dve.wait_ge(sem("latent_roots"), 1)
            link(dve.reciprocal(SQM[:, :, :], SQM[:, :, :]))
            for t, gain in enumerate((prm2("q_norm", 0), prm2("q_norm", 1), prm2("kv_norm"))):
                ins = dve.scalar_tensor_tensor(out=CQF[:, t, :], in0=CQF[:, t, :], scalar=gain, in1=SQM[:, t, :],
                                               op0=ALU.mult, op1=ALU.mult)
            ins.then_inc(sem("latents_ready"), 1)
            shift_tiles(2, 0, (4, 5))
            shift_tiles(2, 1, (6, 7))
            for n in range(4):
                wait_fill_out(dve, ("lora", n))
            link(dve.tensor_scalar(LW[:, :, :], LW[:, :, :], -0.5 * E_HALF, -0.5 * E_HALF, ALU.mult, ALU.add))
            link(dve.tensor_scalar(A3[:, :, :], A3[:, :, :], 0.5, 0.5, ALU.mult, ALU.add))
            for t in range(3):
                for c in range(2):
                    ins = dve.tensor_tensor_scan(G3[:, t, c * P:(c + 1) * P], ones[:, 0:P],
                                                 LW[:, t, c * P:(c + 1) * P], 0.0, ALU.mult, ALU.add)
            link(ins)
            g4 = flat(G3).rearrange("p (m w) -> p m w", m=6)
            link(dve.tensor_tensor(flat(GM).rearrange("p (m w) -> p m w", m=6), g4,
                                   bc(g4[:, :, HD - 1:HD], [P, 6, P]), ALU.subtract))
            dve.tensor_tensor(E3[:, :, :], GM[:, :, :], LW[:, :, :], ALU.subtract).then_inc(sem("decay_sums"), 1)

            for t in range(3):
                ins = dve.tensor_scalar(KK[:, t, :], K3[:, t, :], prm2("k_k", t), None, ALU.mult)
            link(ins)
            squares(KK, T3, "rw_squares")
            for tt in range(TT):
                o = fill_arrived(dve, ("mla_kv", tt))
                kv = o[:, :].rearrange("p (h w) -> p h w", h=MH)
                dve.tensor_copy(KM[:, tt * MH:(tt + 1) * MH, 0:NOPE], kv[:, :, 0:NOPE])
                fill_out(dve.tensor_copy(VM[:, tt, :].rearrange("p (h w) -> p h w", h=MH), kv[:, :, NOPE:2 * NOPE]),
                         ("mla_kv", tt))
            wait_fill_out(dve, ("mla_kv", 0))
            wait_fill_out(dve, ("mla_kv", 1))
            wait_fill_out(dve, ("mla_q", 0))
            wait_fill_out(dve, ("mla_q", 1))
            dve.wait_ge(sem("key_rope_by_pool"), 2)
            for n, m in enumerate((QM, KM)):
                link(dve.tensor_tensor(SQQ[:, :, :], m[:, :, :], m[:, :, :], ALU.mult))
                link(dve.tensor_reduce(QKSS[:, 8 * n:8 * n + 8], SQQ[:, :, :], AX_X, ALU.add))
            dve.tensor_scalar(QKSS, QKSS, 1.0 / QK, EPS, ALU.mult, ALU.add).then_inc(sem("qk_means"), 1)
            dve.wait_ge(sem("qk_roots"), 1)
            link(dve.reciprocal(QKSS, QKSS))
            dve.wait_ge(sem("sincos_ready"), 1)
            for n, (m, gain) in enumerate(((QM, "q_qk"), (KM, "k_qk"))):
                link(dve.tensor_tensor(m[:, :, :], m[:, :, :], bc(QKSS[:, 8 * n:8 * n + 8].unsqueeze(2), [P, 8, QK]),
                                       ALU.mult))
                link(dve.tensor_tensor(m[:, :, :], m[:, :, :], bc(prm2(gain, 0, QK).unsqueeze(1), [P, 8, QK]),
                                       ALU.mult))
                for tt in range(TT):
                    mt = m[:, tt * MH:(tt + 1) * MH, :]
                    c = bc(COS[:, tt, :].unsqueeze(1), [P, MH, 16])
                    s = bc(SIN[:, tt, :].unsqueeze(1), [P, MH, 16])
                    a, b = mt[:, :, NOPE:NOPE + 16], mt[:, :, NOPE + 16:QK]
                    r = [ROT[:, i, 0:64].rearrange("p (h w) -> p h w", h=MH) for i in range(4)]
                    dve.tensor_tensor(r[0], a, c, ALU.mult)
                    dve.tensor_tensor(r[1], b, s, ALU.mult)
                    dve.tensor_tensor(r[2], a, s, ALU.mult)
                    link(dve.tensor_tensor(r[3], b, c, ALU.mult))
                    dve.tensor_tensor(a, r[0], r[1], ALU.subtract)
                    link(dve.tensor_tensor(b, r[2], r[3], ALU.add))
            dve.sem_inc(sem("mla_qk_ready"), 1)
            shift_tiles(3, 0, (8, 9))
            shift_tiles(3, 1, (10,))
            o = job_arrived(dve, ("in2", 3, 2))
            dve.tensor_scalar(GAX, o[0:RH, S:2 * S], prm2("g_dtb")[0:RH, :], None, ALU.add)
            job_out(dve.tensor_copy(BETA, o[0:RH, 0:S]), ("in2", 3, 2))
            wait_job_out(dve, ("in2", 3, 2))
            dve.sem_inc(sem("beta_in"), 1)
            for u in range(NU, NU + MH + 1):
                if u < NU + MH:
                    bias_scores(u)
                if u > NU:
                    finish_head(u - 1)
            means([("kk_ss", 0), ("kk_ss", 1)], T3, 1.0, 1e-6, "rw_means")
            dve.wait_ge(sem("rw_roots"), 1)
            link(dve.reciprocal(T3[:, :, :], T3[:, :, :]))
            link(dve.tensor_tensor(KK[:, :, :], KK[:, :, :], T3[:, :, :], ALU.mult))
            for t in range(3):
                ins = dve.tensor_scalar(T3[:, t, :], A3[:, t, :], -1.0, prm2("k_a", t), ALU.add, ALU.mult)
            link(ins)
            link(dve.scalar_tensor_tensor(out=flat(K3), in0=flat(T3), scalar=1.0, in1=flat(K3), op0=ALU.add,
                                          op1=ALU.mult))
            dve.tensor_tensor(A3[:, :, :], KK[:, :, :], A3[:, :, :], ALU.mult)
            for t in range(3):
                ins = dve.scalar_tensor_tensor(out=T3[:, t, :], in0=R3[:, t, :], scalar=prm2("r_k", t), in1=K3[:, t, :],
                                               op0=ALU.mult, op1=ALU.mult)
            ins.then_inc(sem("rw_squares"), 1)
            dve.wait_ge(sem("decay_exp"), 1)
            dve.tensor_tensor(KK[:, :, :], KK[:, :, :], E3[:, :, :], ALU.mult).then_inc(sem("alpha_ready"), 1)
            convs(8, 12)
            convs(12, 16)
            for name, a, b in ((("bonus", 0), 0, 2), (("bonus", 1), 2, 3)):
                o = fill_arrived(dve, name)
                fill_out(dve.tensor_tensor(flat(BON[:, a:b, :]), o[:, 0:(b - a) * S], flat(V3[:, a:b, :]), ALU.mult),
                         name)
            dve.wait_ge(sem("decay_exp"), 3)
            dve.tensor_tensor(A3[:, :, :], A3[:, :, :], E3[:, :, :], ALU.mult).then_inc(sem("rw_factors"), 1)
            conv_taps(16)
            conv_out(16)
            dve.wait_ge(sem("gg_tanh"), 1)
            job_out(dve.scalar_tensor_tensor(out=GGT[:, 0, :], in0=GGT[:, 0, :], scalar=1.0,
                                             in1=job_bank(("in2", 6, 0))[:, S:2 * S], op0=ALU.add, op1=ALU.mult),
                    ("in2", 6, 0))
            dve.wait_ge(sem("gg_tanh"), 2)
            job_out(dve.scalar_tensor_tensor(out=flat(GGT[:, 1:3, :]), in0=flat(GGT[:, 1:3, :]), scalar=1.0,
                                             in1=job_bank(("in2", 6, 1))[:, :], op0=ALU.add, op1=ALU.mult),
                    ("in2", 6, 1))

            dve.wait_ge(sem("mats_zeroed"), 4)

            def four(o):
                return o[:, :].rearrange("p (m w) -> p m w", m=4)

            def threes(t, g):
                return t[:, 3 * g:3 * g + 3, :]

            def three(o):
                return o[:, 0:384].rearrange("p (t w) -> p t w", t=3)

            def masked(kind, strict_dst, incl_dst, fills=range(6)):
                for g in fills:
                    o = fill_arrived(dve, (kind, g))[:, :].rearrange("p (n q w) -> p n q w", n=2, q=2)
                    for q, dst, mask in ((0, incl_dst, "incl"), (1, strict_dst, "strict")):
                        d, mk = dst[:, 2 * g:2 * g + 2, :], prm2(mask, 0, P)
                        dve.tensor_tensor(d[:, :, HD:P], o[:, :, q, HD:P], bc(mk[:, HD:P].unsqueeze(1), [P, 2, HD]),
                                          ALU.mult)
                        ins = dve.tensor_tensor(d[0:HD, :, 0:HD], o[0:HD, :, q, 0:HD],
                                                bc(mk[0:HD, 0:HD].unsqueeze(1), [HD, 2, HD]), ALU.mult)
                    fill_out(ins, (kind, g))

            masked("by_b", AT, MB)

            def level_mask(lv):
                return prm2("levels", lv * P, P)

            def delta_rule_squares(n):
                squares((GQ, GK)[n], GKB, "gdn_squares")

            def delta_rule_unit(n):
                m = flat((GQ, GK)[n])
                dve.wait_ge(sem("gdn_roots"), n + 1)
                link(dve.reciprocal(GTMP[:, :, :], GTMP[:, :, :]))
                link(dve.scalar_tensor_tensor(out=m, in0=m, scalar=HD ** -0.5 if n == 0 else 1.0, in1=flat(GTMP),
                                              op0=ALU.mult, op1=ALU.mult))

            def delta_rule_part(lv):
                if lv == 1:
                    delta_rule_squares(0)
                    dve.wait_ge(sem("beta_tanh"), 1)
                    dve.tensor_scalar(BETA, BETA, 0.5, 0.5, ALU.mult, ALU.add)
                    dve.scalar_tensor_tensor(out=GSPT, in0=GAX, scalar=-1.0, in1=GAX, op0=ALU.mult, op1=ALU.min)\
                        .then_inc(sem("sp_minus_abs"), 1)
                elif lv == 2:
                    means([("gq_ss", 0), ("gq_ss", 1)], GTMP, 1.0, 1e-6, "gdn_means")
                    dve.wait_ge(sem("sp_exp"), 2)
                    dve.tensor_scalar(GSPT, GSPT, 1.0, None, ALU.add).then_inc(sem("sp_exp1"), 1)
                elif lv == 3:
                    delta_rule_unit(0)
                    delta_rule_squares(1)
                elif lv == 4:
                    means([("gk_ss", 0), ("gk_ss", 1)], GTMP, 1.0, 1e-6, "gdn_means")
                    dve.wait_ge(sem("sp_ln"), 2)
                    link(dve.scalar_tensor_tensor(out=GAX, in0=GAX, scalar=0.0, in1=GSPT, op0=ALU.max, op1=ALU.add))
                    dve.wait_ge(sem("a_ready"), 2)
                    link(dve.tensor_scalar(GLOG, GAX, EALOG[0:RH, :], -1.0, ALU.mult, ALU.mult))
                    for c in range(2):
                        ins = dve.tensor_tensor_scan(GCUM[:, c * P:(c + 1) * P], ones[0:RH, 0:P],
                                                     GLOG[:, c * P:(c + 1) * P], 0.0, ALU.mult, ALU.add)
                    ins.then_inc(sem("gdn_cumulated"), 1)
                elif lv == 5:
                    delta_rule_unit(1)
                else:
                    for name, a, b in ((("beta", 0), 0, 2), (("beta", 1), 2, 3)):
                        o = fill_arrived(dve, name)
                        src = o[:, 0:(b - a) * S]
                        dve.tensor_tensor(flat(GKB[:, a:b, :]), src, flat(GK[:, a:b, :]), ALU.mult)
                        fill_out(dve.tensor_tensor(flat(GV[:, a:b, :]), src, flat(GV[:, a:b, :]), ALU.mult), name)
                        wait_fill_out(dve, name)
                    o = three(fill_arrived(dve, ("g_e",)))
                    dve.tensor_tensor(GKE[:, :, :], o, GKB[:, :, P:S], ALU.mult)
                    fill_out(dve.tensor_tensor(GQD[:, :, :], o, GQ[:, :, P:S], ALU.mult), ("g_e",))
                    o = three(fill_arrived(dve, ("g_k",)))
                    fill_out(dve.tensor_tensor(GKD[:, :, :], o, GK[:, :, 0:P], ALU.mult), ("g_k",))

            def start_inverse(groups=range(3)):
                for g in groups:
                    tt, at = TTM[:, 4 * g:4 * g + 4, :], AT[:, 4 * g:4 * g + 4, :]
                    link(dve.tensor_tensor(tt, at, bc(level_mask(0).unsqueeze(1), [P, 4, P]), ALU.mult))
                    dve.scalar_tensor_tensor(out=tt, in0=tt, scalar=-1.0, in1=bc(ident.unsqueeze(1), [P, 4, P]),
                                             op0=ALU.mult, op1=ALU.add).then_inc(sem("inverse_started"), 1)

            def finish_rwkv(lv):
                if lv == 1:
                    dve.wait_ge(sem("rw_roots"), 2)
                    link(dve.reciprocal(T3[:, 0:2, :], T3[:, 0:2, :]))
                elif lv == 2:
                    link(dve.reciprocal(T3[:, 2, :], T3[:, 2, :]))
                    link(dve.tensor_tensor(E3[:, :, :], E3[:, :, :], T3[:, :, :], ALU.mult))
                elif lv == 3:
                    for t in range(3):
                        ins = dve.tensor_scalar(E3[:, t, :], E3[:, t, :], prm2("gn_g", t), prm2("gn_b", t), ALU.mult,
                                                ALU.add)
                    link(ins)
                elif lv == 4:
                    link(dve.tensor_tensor(E3[:, :, :], E3[:, :, :], BON[:, :, :], ALU.add))
                    dve.tensor_tensor(YT2[:, 0:3, :], E3[:, :, :], GG[:, :, :], ALU.mult).then_inc(sem("y2_ready"), 1)

            def inverse(fam):
                for lv in range(1, LEVELS):
                    for g in range(3):
                        o = fill_arrived(dve, (fam, "p", lv, g))
                        fill_out(dve.tensor_tensor(PM[:, 4 * g:4 * g + 4, :], four(o),
                                                   bc(level_mask(lv).unsqueeze(1), [P, 4, P]), ALU.mult),
                                 (fam, "p", lv, g))
                    if fam == "rw":
                        delta_rule_part(lv)
                    else:
                        finish_rwkv(lv)
                    for part, t in (("t", TM), ("tt", TTM)):
                        if part == "t" and lv == LEVELS - 1:
                            continue
                        for g in range(3):
                            o = fill_arrived(dve, (fam, part, lv, g))
                            m = flat(t[:, 4 * g:4 * g + 4, :])
                            fill_out(dve.tensor_tensor(m, m, o[:, :], ALU.subtract), (fam, part, lv, g))

            for g in range(6):
                wait_fill_out(dve, ("by_b", g))
            for g in range(3):
                start_inverse((g,))
                masked("by_k", PM, MK, (2 * g, 2 * g + 1))
            for c in range(2):
                o = fill_arrived(dve, ("av", c))
                fill_out(dve.tensor_scalar(RR[:, c, :], o[:, 0:384], -1.0, None, ALU.mult), ("av", c))
            inverse("rw")
            dve.wait_ge(sem("decay_exp"), 3)
            o = fill_arrived(dve, ("st",))
            for t in range(3):
                ins = dve.tensor_scalar(ST[:, t, :], o[:, t * HD:(t + 1) * HD], GM[:, t, P - 1:P], EGC[:, t:t + 1],
                                        ALU.mult, ALU.mult)
            fill_out(ins, ("st",))
            wait_fill_out(dve, ("av", 1))

            def subtract_state(name, rhs):
                for par in range(2):
                    o = fill_arrived(dve, (name, par))
                    r = rhs[:, 1, :].rearrange("p (t q w) -> p q t w", q=2, w=HD)[:, par]
                    src = o[:, 0:3 * HD].rearrange("p (t w) -> p t w", t=3)
                    fill_out(dve.tensor_tensor(r, r, src, ALU.subtract), (name, par))

            subtract_state("r1", RR)
            for name, a, b in ((("gn_mean", 0), 0, 2), (("gn_mean", 1), 2, 3)):
                o = fill_arrived(dve, name)
                e = flat(E3[:, a:b, :])
                fill_out(dve.scalar_tensor_tensor(out=e, in0=o[:, 0:(b - a) * S], scalar=-1.0 / HD, in1=e,
                                                  op0=ALU.mult, op1=ALU.add), name)
                wait_fill_out(dve, name)
            squares(E3, T3, "rw_squares")
            means([("gn_var", 0), ("gn_var", 1)], T3, 1.0 / HD, 64e-5, "rw_means")
            for g in range(3):
                o = fill_arrived(dve, ("decay", g))
                fill_out(dve.tensor_tensor(GAT[:, 4 * g:4 * g + 4, :], four(o),
                                           bc(cst("ssd_mask")[:, 0:P].unsqueeze(1), [P, 4, P]), ALU.add), ("decay", g))
            dve.wait_ge(sem("gdn_decay_exp"), 3)
            for g in range(4):
                o = fill_arrived(dve, ("gkk", g))
                m = threes(AT, g)
                fill_out(dve.tensor_tensor(m, three(o), threes(GAT, g), ALU.mult), ("gkk", g))
                wait_fill_out(dve, ("gkk", g))
                link(dve.tensor_tensor(m, m, bc(prm2("strict", 0, P).unsqueeze(1), [P, 3, P]), ALU.mult))
            start_inverse()
            for g in range(4):
                o = fill_arrived(dve, ("gqk", g))
                m = threes(GAT, g)
                fill_out(dve.tensor_tensor(m, three(o), m, ALU.mult), ("gqk", g))
            inverse("gd")
            o = fill_arrived(dve, ("gst",))
            fill_out(dve.tensor_copy(flat(ST), o[:, 0:3 * HD]), ("gst",))
            wait_fill_out(dve, ("gv_T", 1))
            subtract_state("gr1", GVT)
            split_low(PIECE_AT["out2", 0, 0])
            split_low(PIECE_AT["out2", 0, 1])
            dve.wait_ge(sem("y2_high"), 1)
            dve.tensor_tensor(OVER_HT[:, 0:5, :], YT2[:, 0:5, :], OVER_HN[:, 0:5, :].bitcast(F32), ALU.subtract)\
                .then_inc(sem("y2_split"), 1)
            wait_fill_out(dve, ("o", 0))
            wait_fill_out(dve, ("o", 1))
            squares(GKB, GQ, "gdn_squares")
            means([("o_ss", 0), ("o_ss", 1)], GTMP, 1.0 / HD, EPS, "gdn_means")
            dve.wait_ge(sem("gdn_roots"), 3)
            def last_low(t):
                dve.wait_ge(sem("y2_high"), 2 + t)
                dve.tensor_tensor(OVER_HT[:, 5 + t, :], YT2[:, 5 + t, :], OVER_HN[:, 5 + t, :].bitcast(F32), ALU.subtract)\
                    .then_inc(sem("y2_split"), 1)

            for t in range(3):
                link(dve.reciprocal(GTMP[:, t, :], GTMP[:, t, :]))
                link(dve.scalar_tensor_tensor(out=GKB[:, t, :], in0=GKB[:, t, :], scalar=prm2("o_norm"),
                                              in1=GTMP[:, t, :], op0=ALU.mult, op1=ALU.mult))
                dve.tensor_tensor(YT2[:, 5 + t, :], GKB[:, t, :], GGT[:, t, :], ALU.mult).then_inc(sem("y2_ready"), 1)
                if t:
                    last_low(t - 1)
            last_low(2)

            add_out("out2", 1.0)
            norm_scale(4)
            norm_gains(3)
            split_low(PIECE_AT["ffn2", 0, 1])

            def hidden2_low(q):
                hidden_low(HID2_HIGH, HID2_LOW, slice(2 * q, 2 * q + 2), HF2[:, q % 2, :], FF1_CHUNKS + q)

            for q in range(2 * FF2_CHUNKS):
                c, j = divmod(q, 2)
                split_low(PIECE_AT["ffn2", c, j] + 2)
                wait_job_out(dve, ("ffn2", c, j))
                m = HF2[:, q % 2, :]
                dve.tensor_tensor(m, m, m, ALU.mult).then_inc(sem("hidden_ready"), 1)
                if q:
                    hidden2_low(q - 1)
            hidden2_low(q)
            for k in range(PIECE_AT["down2", 0, 0] + 2, len(PIECES)):
                split_low(k)
            add_down("down2", 1.0)

        @block.gpsimd
        def _(pool):
            wait_fill_out(pool, ("table",))
            pool.dma_start(table_dram, PT_[0:2 * NH, 0, :].unsqueeze(1).to_broadcast([2 * NH, P, 384])).then_inc(sem("table_stored"), 16)
            pool.wait_ge(sem("table_stored"), 16)
            for b in range(4):
                wait_fill_out(pool, ("norm", 0, b))
            pool.tensor_tensor(HT[:, :, :], FIRST_HIGH[:, :, :].bitcast(F32), FIRST_LOW[:, :, :].bitcast(F32), ALU.add)\
                .then_inc(sem("stream_by_pool"), 1)
            pool.wait_ge(sem("stream_by_pool"), 1)
            job_arrived(pool, ("in1", 10, 1))
            diagonal = bass.AP(tensor=table_dram.tensor, offset=table_dram.offset + P - 1,
                               ap=[[383, P], [P * 384, 2 * NH], [1, S]])
            pool.dma_start(BIAS[:, :, :], diagonal).then_inc(sem("bias_in"), 16)
            wait_fill_out(pool, ("cb", 0))
            wait_fill_out(pool, ("cb", 1))
            for u, (br, h) in enumerate(UNITS):
                if br == 0:
                    pool.wait_ge(sem("probs_ready"), u + 1)
                    pool.wait_ge(sem("heads_written"), u - 1)
                    pool.tensor_tensor(PT_[:, u % 2, :], PB_[:, u % 2, :], CB[:, h // 4, :], ALU.mult)\
                        .then_inc(sem("mix_by_pool"), 1)
            for i in range(1, 4):
                for j in range(4):
                    dc, tt = divmod(j, 2)
                    n = 4 * i + j - 4
                    wait_job_out(pool, ("branch", i, j))
                    mix = HN[:, tt, dc * 512:(dc + 1) * 512]
                    if i > 1:
                        pool.wait_ge(sem("mixed_by_pool"), n - 3)
                    pool.tensor_tensor(mix, mix, TMP[:, n % 2, :], ALU.add).then_inc(sem("mixed_by_pool"), 1)
            for b in range(4):
                wait_fill_out(pool, ("norm", 2, b))
            pool.tensor_tensor(HT[:, :, :], IN2_HIGH[:, :, :].bitcast(F32), IN2_LOW[:, :, :].bitcast(F32), ALU.add)\
                .then_inc(sem("stream_by_pool"), 1)
            wait_job_out(pool, ("in2", 0, 1))
            for tt in range(TT):
                pool.tensor_copy(KM[:, tt * MH:(tt + 1) * MH, NOPE:QK],
                                 KR[:, tt, :].unsqueeze(1).to_broadcast([P, MH, ROPE]))\
                    .then_inc(sem("key_rope_by_pool"), 1)
            pool.wait_ge(sem("rw_squares"), 2)
            pool.wait_ge(sem("decay_exp"), 3)
            pool.tensor_tensor(K3[:, :, :], K3[:, :, :], E3[:, :, :], ALU.mult)
            pool.tensor_tensor(R3[:, :, :], R3[:, :, :], GM[:, :, :], ALU.mult).then_inc(sem("factors_by_pool"), 1)
            pool.wait_ge(sem("factors_by_pool"), 1)
            pool.wait_ge(sem("heads_done"), NU + MH)
            pool.wait_ge(sem("decay_exp"), 1)
            pool.wait_ge(sem("conv_done"), 17)
            for m in (AT, PM, MB, MK):
                pool.memset(m[HD:P, :, 0:HD], 0.0).then_inc(sem("mats_zeroed"), 1)


def kernel(**inputs):
    import numpy as np
    import concourse.bacc as bacc
    from concourse.bass_utils import run_bass_kernel_spmd as run

    a = {k: np.asarray(v) for k, v in inputs.items()}
    f32 = np.float32

    def k_tiles(w):
        return w.reshape(-1, P, w.shape[1]).transpose(1, 0, 2).reshape(-1)

    w = a["w_in"][0]
    splits = dict(zip(("z", "xbc", "dt", "b", "c", "f", "dq", "dkv", "gate"),
                      np.split(w, np.cumsum([512, 1024, 8, 1536, 1536, 8, 512, 256])[0:8], axis=1)))
    dq = splits["dq"].reshape(D, 2, 4, HD).transpose(0, 2, 1, 3).reshape(D, 512)
    bq, bk, bv = np.split(splits["b"], 3, axis=1)
    cq, ck, cv = np.split(splits["c"], 3, axis=1)
    pad = np.zeros((D, 88), w.dtype)
    in1 = [np.concatenate([splits["dkv"], splits["dt"], pad[:, 0:24], splits["f"], pad], axis=1), splits["xbc"][:, 0:512],
           splits["xbc"][:, 512:1024], cq, ck, cv, dq, bq, bk, bv, splits["z"]]
    fg, fu = a["w_ffn_gate"][0], a["w_ffn_up"][0]
    w2 = a["w_in_2"][0]
    r, k, v, zw_za, zg, lat, gd = np.split(w2, np.cumsum([384, 384, 384, 128, 128, 416]), axis=1)
    rw = np.concatenate([zw_za, zg, k, v, r], axis=1)
    in2 = [lat, rw[:, 0:512], rw[:, 512:1024], np.concatenate([rw[:, 1024:], gd[:, 1536:]], axis=1),
           gd[:, 0:512], gd[:, 512:1024], gd[:, 1024:1536]]
    per_chunk = {
        "in1": lambda i: k_tiles(in1[i]),
        "gate": lambda i: k_tiles(splits["gate"][:, i * 512:(i + 1) * 512]),
        "branch": lambda i: k_tiles(a["w_branch"][0, i]),
        "out1": lambda i: k_tiles(a["w_out"][0][:, i * 512:(i + 1) * 512]),
        "ffn1": lambda i: k_tiles(np.concatenate([fg[:, i * 256:(i + 1) * 256], fu[:, i * 256:(i + 1) * 256]], axis=1)),
        "down1": lambda i: k_tiles(a["w_ffn_down"][0][i * 512:(i + 1) * 512]),
        "in2": lambda i: k_tiles(in2[i]),
        "out2": lambda i: k_tiles(a["w_out_2"][0][:, i * 512:(i + 1) * 512]),
        "ffn2": lambda i: k_tiles(a["w_ff1_2"][0][:, i * 512:(i + 1) * 512]),
        "down2": lambda i: k_tiles(a["w_ff2_2"][0][i * 512:(i + 1) * 512]),
    }
    weights = np.concatenate([per_chunk[n](i) for n, i, _ in CHUNKS])

    def cols(v):
        return np.ascontiguousarray(v).reshape(-1, P).T

    def spread(v):
        return np.broadcast_to(np.ascontiguousarray(v).reshape(1, -1), (P, v.size))

    def rows(v, at=0):
        out = np.zeros((P, v.shape[-1] if v.ndim > 1 else 1), v.dtype)
        out[at:at + v.shape[0]] = v.reshape(v.shape[0], -1)
        return out

    p1 = {"norm_mix": cols(a["norm_mix"][0]), "norm_ffn": cols(a["norm_ffn"][0]), "ln_mix": cols(a["ln_mix_g_2"][0]),
          "ln_ffn": cols(a["ln_ffn_g_2"][0]), "conv_w": cols(a["conv_w"][0]), "conv_b": cols(a["conv_b"][0]),
          "ssm_norm": cols(a["ssm_norm_w"][0]), "dt_bias": rows(a["dt_bias"][0]), "a_log": rows(a["a_log"][0]),
          "forget_bias": rows(a["forget_bias"][0], 32), "sinks": spread(a["sinks"][0]), "d_skip": spread(a["d_skip"][0])}
    mu = a["rwkv_mu_2"][0]
    mu = np.concatenate([mu[1152:1408], mu[384:1152], mu[0:384]])
    t, j = np.arange(P)[:, None], np.arange(P)[None, :]
    levels = []
    for lv in range(LEVELS):
        b = 1 << lv
        m = (t // (2 * b) == j // (2 * b)) & ((t // b) % 2 == 1) & ((j // b) % 2 == 0)
        levels.append(m.T if lv == 0 else m)
    pair_rows = np.zeros((P, 3 * P), f32)
    for h in range(RH):
        pair_rows[h, h * HD:(h + 1) * HD] = 1.0
    inv_freq = f32(10000.0) ** (-np.arange(0, ROPE, 2, dtype=f32) / f32(ROPE))
    p2 = {"mu": cols(mu), "w0": cols(a["rwkv_w0_2"][0]), "a0": cols(a["rwkv_a0_2"][0]), "k_k": cols(a["rwkv_k_k_2"][0]),
          "k_a": cols(a["rwkv_k_a_2"][0]), "r_k": cols(a["rwkv_r_k_2"][0].reshape(-1)), "gn_g": cols(a["rwkv_gn_g_2"][0]),
          "gn_b": cols(a["rwkv_gn_b_2"][0]), "q_norm": cols(a["mla_q_norm_g_2"][0]), "kv_norm": cols(a["mla_kv_norm_g_2"][0]),
          "g_conv": cols(a["gdn_conv_w_2"][0]), "g_alog": rows(a["gdn_a_log_2"][0]), "g_dtb": rows(a["gdn_dt_bias_2"][0]),
          "o_norm": cols(np.concatenate([a["gdn_o_norm_g_2"][0]] * 2)), "q_qk": spread(a["mla_q_qk_g_2"][0]),
          "k_qk": spread(a["mla_k_qk_g_2"][0]), "w2a2": np.concatenate([a["rwkv_w2_2"][0], a["rwkv_a2_2"][0]]),
          "g2": a["rwkv_g2_2"][0], "uq": a["mla_w_uq_2"][0].reshape(2, P, 384).transpose(1, 0, 2).reshape(P, 768),
          "ukv": a["mla_w_ukv_2"][0], "inv_freq": np.broadcast_to(inv_freq, (P, 16)), "strict": (j > t), "incl": (j >= t),
          "levels": np.concatenate(levels, axis=1), "blockones": (t // HD == j // HD), "pair_rows": pair_rows}
    params = np.concatenate([np.asarray(p1[n], f32) for n, _ in PARAMS], axis=1)
    params2 = np.concatenate([np.asarray(p2[n], f32) for n, _ in PARAMS2], axis=1)

    key = np.arange(S)[None, :]
    dist = 255 - np.arange(384)
    d = np.maximum(dist, 1).astype(f32)
    large = 16 + (np.log(d / f32(16)) / f32(np.log(64.0)) * f32(16)).astype(np.int32)
    bucket = np.where(dist < 16, np.maximum(dist, 0), np.minimum(large, 31))
    onehot = np.zeros((P, 384), f32)
    onehot[0:32] = (np.arange(32)[:, None] == bucket[None, :])
    table_mask = np.zeros((P, 384), f32)
    table_mask[0:NH] = np.where(dist >= 0, 0.0, NEG)
    table_mask[NH:2 * NH] = np.where((dist >= 0) & (dist < P), 0.0, NEG)
    after = np.where(key >= t, 0.0, NEG)
    c = {"ident": np.eye(P), "causal": np.where(P + t >= key, 0.0, NEG),
         "ssd_mask": np.concatenate([after, after[:, 0:P]], axis=1),
         "mla_mask": np.where(key // 64 <= (P + t) // 64, 0.0, NEG), "ones": np.ones((P, S)), "onehot": onehot,
         "table_mask": table_mask}
    consts = np.concatenate([np.asarray(c[n], f32) for n, _ in CONSTS], axis=1)
    tables = np.concatenate([onehot, table_mask], axis=1)[0:32]

    arrays = {"x_dram": a["x"], "weights_dram": weights, "params_dram": params, "params2_dram": params2,
              "consts_dram": consts, "tables_dram": tables, "rel_bias_dram": a["rel_bias"], "norm_final_dram": spread(a["norm_final"]),
              "positions_dram": a["positions_2"].reshape(TT, P).T}
    nc = bacc.Bacc("TRN2", target_bir_lowering=False, num_devices=1)
    args = []
    for name in arrays:
        arrays[name] = np.ascontiguousarray(arrays[name])
        args.append(nc.dram_tensor(name, arrays[name].shape, mybir.dt.from_np(arrays[name].dtype),
                                   kind="ExternalInput").ap())
    args.append(nc.dram_tensor("bias_rows_dram", (2 * NH, P, 384), F32, kind="Internal").ap())
    args.append(nc.dram_tensor("out_dram", (1, S, D), F32, kind="ExternalOutput").ap())
    build(nc, *args)
    result = run(nc, [arrays], core_ids=[0])
    return result.results[0]["out_dram"]
```
